# Optimizing a Trainium2 kernel written in Bass

```python
import jax
import jax.numpy as jnp
from jax import lax
import numpy as np

D_MODEL = 1024
BATCH = 1
SEQ = 256
DEPTH = 2

GRID_W = 64
CTX_LEN = 256
EPS = 1e-6
N_MOD = 6

MLA_HEADS = 8
MLA_Q_RANK = 384
MLA_KV_RANK = 256
MLA_NOPE = 64
MLA_ROPE = 32
MLA_QK = MLA_NOPE + MLA_ROPE
MLA_V = 64
MLA_WIDTH = MLA_HEADS * MLA_V
ROPE_THETA = 10000.0
Q_BLOCK = 128

HY_WIDTH = 256
HY_SHORT = 3
HY_BANDS = 16
HY_EMB = 1 + 2 * HY_BANDS
HY_HIDDEN = 64
HY_DIRS = 2

GM_WIDTH = 256
GM_CHUNK = 128
GM_GROUPS = 4
GM_GROUP_W = GM_WIDTH // GM_GROUPS

N_BRANCH = 3
OFF_Q = 0
OFF_KV = OFF_Q + MLA_Q_RANK
OFF_KR = OFF_KV + MLA_KV_RANK
OFF_HY = OFF_KR + MLA_ROPE
OFF_GM = OFF_HY + 3 * HY_WIDTH
OFF_GT = OFF_GM + 2 * GM_WIDTH
IN_W = OFF_GT + N_BRANCH * D_MODEL

N_EXPERTS = 16
N_GROUPS = 4
EXP_PER_GROUP = N_EXPERTS // N_GROUPS
TOP_K = 2
D_EXPERT = 512

kernel_name = "hybrid_mla_hyena_gmlp_moe_dit"

def rms_norm(x, g):
    xf = x.astype(jnp.float32)
    y = xf * lax.rsqrt(jnp.mean(xf * xf, axis=-1, keepdims=True) + EPS)
    return (y * g.astype(jnp.float32)).astype(x.dtype)

def modulate(x, g, shift, scale):
    return rms_norm(x, g) * (1 + scale) + shift

def axial_rope_tables(rows):
    row = jnp.repeat(jnp.arange(rows, dtype=jnp.float32), GRID_W)
    col = jnp.tile(jnp.arange(GRID_W, dtype=jnp.float32), rows)
    n_freq = MLA_ROPE // 4
    inv = ROPE_THETA ** (-jnp.arange(n_freq, dtype=jnp.float32) / n_freq)
    ang = jnp.concatenate([row[:, None] * inv, col[:, None] * inv], axis=-1)
    return jnp.cos(ang), jnp.sin(ang)

def apply_rope(x, cos, sin):
    xr = x.astype(jnp.float32).reshape(*x.shape[:-1], MLA_ROPE // 2, 2)
    x1, x2 = xr[..., 0], xr[..., 1]
    c = cos[None, :, None, :]
    s = sin[None, :, None, :]
    out = jnp.stack([x1 * c - x2 * s, x1 * s + x2 * c], axis=-1)
    return out.reshape(x.shape).astype(x.dtype)

def mla_q(pq, g_qa, w_uq, g_qn, rope):
    B, L, _ = pq.shape
    q = (rms_norm(pq, g_qa) @ w_uq).reshape(B, L, MLA_HEADS, MLA_QK)
    q = rms_norm(q, g_qn)
    if rope is not None:
        q = jnp.concatenate([q[..., :MLA_NOPE], apply_rope(q[..., MLA_NOPE:], *rope)], axis=-1)
    return q

def mla_kv(pkv, pkr, g_kva, w_ukv, g_kn, rope):
    B, L, _ = pkv.shape
    kv = (rms_norm(pkv, g_kva) @ w_ukv).reshape(B, L, MLA_HEADS, MLA_NOPE + MLA_V)
    k_rope = jnp.broadcast_to(pkr[:, :, None, :], (B, L, MLA_HEADS, MLA_ROPE))
    k = rms_norm(jnp.concatenate([kv[..., :MLA_NOPE], k_rope.astype(kv.dtype)], axis=-1), g_kn)
    if rope is not None:
        k = jnp.concatenate([k[..., :MLA_NOPE], apply_rope(k[..., MLA_NOPE:], *rope)], axis=-1)
    return k, kv[..., MLA_NOPE:]

def block_attention(q, k, v):
    B, L, H, Dq = q.shape
    nb = L // Q_BLOCK
    qb = jnp.moveaxis(q.reshape(B, nb, Q_BLOCK, H, Dq), 1, 0)
    scale = Dq ** -0.5

    def attend_block(qblk):
        s = jnp.einsum('bqhd,bkhd->bhqk', qblk, k, preferred_element_type=jnp.float32) * scale
        p = jax.nn.softmax(s, axis=-1).astype(v.dtype)
        return jnp.einsum('bhqk,bkhd->bqhd', p, v)

    o = lax.map(attend_block, qb)
    return jnp.moveaxis(o, 0, 1).reshape(B, L, H * v.shape[-1])

def hyena_filters(L, w1, b1, w2, b2, w3, b3, freq, decay):
    f32 = lambda a: a.astype(jnp.float32)
    t = jnp.arange(L, dtype=jnp.float32)
    t_unit = t / max(L - 1, 1)
    bands = jnp.linspace(1e-4, HY_BANDS - 1, HY_BANDS, dtype=jnp.float32)
    ang = (2 * jnp.pi / L) * t[:, None] * bands[None, :]
    z = jnp.concatenate([t_unit[:, None], jnp.cos(ang), -jnp.sin(ang)], axis=-1)
    hdn = jnp.sin(f32(freq) * (z @ f32(w1) + f32(b1)))
    hdn = jnp.sin(f32(freq) * (hdn @ f32(w2) + f32(b2)))
    k = (hdn @ f32(w3) + f32(b3)).reshape(L, HY_DIRS, HY_WIDTH)
    k = k * jnp.exp(-t_unit[:, None, None] * jnp.abs(f32(decay))[None])
    return k * lax.rsqrt(jnp.sum(k * k, axis=(0, 1), keepdims=True) + EPS)

def bidir_long_conv(u, k):
    B, L, C = u.shape
    filt = jnp.concatenate([k[:, 0], jnp.zeros((1, C), k.dtype), k[:0:-1, 1]], axis=0)
    n = 2 * L
    uf = jnp.fft.rfft(u.astype(jnp.float32), n=n, axis=1)
    kf = jnp.fft.rfft(filt.astype(jnp.float32), n=n, axis=0)
    y = jnp.fft.irfft(uf * kf[None], n=n, axis=1)[:, :L]
    return y.astype(u.dtype)

def hyena_branch(p, conv_w, conv_b, filt, bias):
    L = p.shape[1]
    half = HY_SHORT // 2
    pp = jnp.pad(p, ((0, 0), (half, half), (0, 0)))
    z = conv_b + pp[:, 0:L] * conv_w[0]
    for j in range(1, HY_SHORT):
        z = z + pp[:, j:j + L] * conv_w[j]
    x0, x1, v = jnp.split(z, 3, axis=-1)
    u = v * x1
    return x0 * (bidir_long_conv(u, filt) + u * bias)

def gmlp_branch(p, g_v, w_s, b_s):
    B, L, _ = p.shape
    u, v = jnp.split(jax.nn.gelu(p), 2, axis=-1)
    v = rms_norm(v, g_v).reshape(B, L // GM_CHUNK, GM_CHUNK, GM_GROUPS, GM_GROUP_W)
    s = jnp.einsum('gij,bnjgc->bnigc', w_s, v) + jnp.swapaxes(b_s, 0, 1)[:, :, None]
    return u * s.reshape(B, L, GM_WIDTH)

def merge_branches(a, b, m, p_gate, w_pa, w_pb, w_pc, w_out):
    ga, gb, gm = jnp.split(jax.nn.sigmoid(p_gate), N_BRANCH, axis=-1)
    y = ga * (a @ w_pa) + gb * (b @ w_pb) + gm * (m @ w_pc)
    return y @ w_out

def token_mixer(h, lp, rope, ctx_kv):
    L = h.shape[1]
    p = h @ lp['w_in']
    pq, pkv, pkr = p[..., OFF_Q:OFF_KV], p[..., OFF_KV:OFF_KR], p[..., OFF_KR:OFF_HY]
    phy, pgm, pgt = p[..., OFF_HY:OFF_GM], p[..., OFF_GM:OFF_GT], p[..., OFF_GT:]
    q = mla_q(pq, lp['g_qa'], lp['w_uq'], lp['g_qn'], rope)
    k, v = mla_kv(pkv, pkr, lp['g_kva'], lp['w_ukv'], lp['g_kn'], rope)
    if ctx_kv is None:
        a = block_attention(q, k, v)
    else:
        a = block_attention(q, jnp.concatenate([k, ctx_kv[0].astype(k.dtype)], axis=1),
                            jnp.concatenate([v, ctx_kv[1].astype(v.dtype)], axis=1))
    filt = hyena_filters(L, lp['hy_w1'], lp['hy_b1'], lp['hy_w2'], lp['hy_b2'], lp['hy_w3'], lp['hy_b3'],
                         lp['hy_freq'], lp['hy_decay'])
    b = hyena_branch(phy, lp['hy_conv_w'], lp['hy_conv_b'], filt, lp['hy_bias'])
    m = gmlp_branch(pgm, lp['gm_norm_g'], lp['gm_ws'], lp['gm_bs'])
    y = merge_branches(a, b, m, pgt, lp['w_pa'], lp['w_pb'], lp['w_pc'], lp['w_out'])
    return y, k, v

def context_kv(hc, lp):
    pc = hc @ lp['w_in'][:, OFF_KV:OFF_HY]
    return mla_kv(pc[..., :MLA_KV_RANK], pc[..., MLA_KV_RANK:], lp['g_kva'], lp['w_ukv'], lp['g_kn'], None)

def moe_ffn(h, router_w, router_b, w_gate, w_up, w_down):
    aff = jax.nn.sigmoid(jnp.einsum('bld,de->ble', h, router_w, preferred_element_type=jnp.float32))
    sel = aff + router_b.astype(jnp.float32)
    grp = sel.reshape(*sel.shape[:-1], N_GROUPS, EXP_PER_GROUP)
    grp_score = jnp.sum(lax.top_k(grp, TOP_K)[0], axis=-1)
    in_grp = jnp.argmax(grp_score, axis=-1)[..., None] == jnp.arange(N_GROUPS)
    in_grp = jnp.repeat(in_grp, EXP_PER_GROUP, axis=-1)
    _, idx = lax.top_k(jnp.where(in_grp, sel, -jnp.inf), TOP_K)
    wts = jnp.take_along_axis(aff, idx, axis=-1)
    wts = wts / jnp.sum(wts, axis=-1, keepdims=True)
    comb = jnp.einsum('blk,blke->ble', wts, jax.nn.one_hot(idx, N_EXPERTS, dtype=jnp.float32)).astype(h.dtype)
    out = jnp.zeros_like(h)
    for e in range(N_EXPERTS):
        hid = jax.nn.silu(h @ w_gate[e]) * (h @ w_up[e])
        out = out + comb[..., e:e + 1] * (hid @ w_down[e])
    return out

def setup_inputs(seed: int = 0) -> dict:
    key = jax.random.key(seed)
    ks = iter(jax.random.split(key, 40))

    def nrm(shape, scale):
        return scale * jax.random.normal(next(ks), shape, jnp.float32)

    D = D_MODEL
    decay_base = jnp.linspace(3.07, 15.35, HY_WIDTH, dtype=jnp.float32)
    return {
        'x': nrm((BATCH, SEQ, D), 1.0),
        'c': nrm((BATCH, D), 1.0),
        'ctx': nrm((BATCH, CTX_LEN, D), 1.0),
        'c_ctx': nrm((D,), 1.0),
        'w_mod': nrm((DEPTH, D, N_MOD * D), 0.5 * D ** -0.5),
        'b_mod': nrm((DEPTH, N_MOD * D), 0.02),
        'norm1_g': 1.0 + nrm((DEPTH, D), 0.02),
        'norm2_g': 1.0 + nrm((DEPTH, D), 0.02),
        'w_in': nrm((DEPTH, D, IN_W), D ** -0.5),
        'g_qa': 1.0 + nrm((DEPTH, MLA_Q_RANK), 0.02),
        'w_uq': nrm((DEPTH, MLA_Q_RANK, MLA_HEADS * MLA_QK), MLA_Q_RANK ** -0.5),
        'g_kva': 1.0 + nrm((DEPTH, MLA_KV_RANK), 0.02),
        'w_ukv': nrm((DEPTH, MLA_KV_RANK, MLA_HEADS * (MLA_NOPE + MLA_V)), MLA_KV_RANK ** -0.5),
        'g_qn': 1.0 + nrm((DEPTH, MLA_QK), 0.02),
        'g_kn': 1.0 + nrm((DEPTH, MLA_QK), 0.02),
        'hy_conv_w': nrm((DEPTH, HY_SHORT, 3 * HY_WIDTH), HY_SHORT ** -0.5),
        'hy_conv_b': nrm((DEPTH, 3 * HY_WIDTH), 0.02),
        'hy_w1': nrm((DEPTH, HY_EMB, HY_HIDDEN), HY_EMB ** -0.5),
        'hy_b1': nrm((DEPTH, HY_HIDDEN), 0.1),
        'hy_w2': nrm((DEPTH, HY_HIDDEN, HY_HIDDEN), HY_HIDDEN ** -0.5),
        'hy_b2': nrm((DEPTH, HY_HIDDEN), 0.1),
        'hy_w3': nrm((DEPTH, HY_HIDDEN, HY_DIRS * HY_WIDTH), HY_HIDDEN ** -0.5),
        'hy_b3': nrm((DEPTH, HY_DIRS * HY_WIDTH), 0.02),
        'hy_freq': 1.0 + nrm((DEPTH, HY_HIDDEN), 0.1),
        'hy_decay': decay_base[None, None, :] + nrm((DEPTH, HY_DIRS, HY_WIDTH), 0.1),
        'hy_bias': nrm((DEPTH, HY_WIDTH), 0.5),
        'gm_norm_g': 1.0 + nrm((DEPTH, GM_WIDTH), 0.02),
        'gm_ws': nrm((DEPTH, GM_GROUPS, GM_CHUNK, GM_CHUNK), GM_CHUNK ** -0.5),
        'gm_bs': 1.0 + nrm((DEPTH, GM_GROUPS, GM_CHUNK), 0.02),
        'w_pa': nrm((DEPTH, MLA_WIDTH, D), MLA_WIDTH ** -0.5),
        'w_pb': nrm((DEPTH, HY_WIDTH, D), HY_WIDTH ** -0.5),
        'w_pc': nrm((DEPTH, GM_WIDTH, D), GM_WIDTH ** -0.5),
        'w_out': nrm((DEPTH, D, D), D ** -0.5),
        'router_w': nrm((D, N_EXPERTS), D ** -0.5),
        'router_b': nrm((N_EXPERTS,), 0.01),
        'moe_w_gate': nrm((DEPTH, N_EXPERTS, D, D_EXPERT), D ** -0.5),
        'moe_w_up': nrm((DEPTH, N_EXPERTS, D, D_EXPERT), D ** -0.5),
        'moe_w_down': nrm((DEPTH, N_EXPERTS, D_EXPERT, D), D_EXPERT ** -0.5),
    }

def reference(x, c, ctx, c_ctx, w_mod, b_mod, norm1_g, norm2_g, w_in, g_qa, w_uq, g_kva, w_ukv, g_qn, g_kn,
              hy_conv_w, hy_conv_b, hy_w1, hy_b1, hy_w2, hy_b2, hy_w3, hy_b3, hy_freq, hy_decay, hy_bias,
              gm_norm_g, gm_ws, gm_bs, w_pa, w_pb, w_pc, w_out, router_w, router_b,
              moe_w_gate, moe_w_up, moe_w_down):
    ROWS = x.shape[1] // GRID_W
    rope = axial_rope_tables(ROWS)
    silu_c = jax.nn.silu(c)
    silu_cc = jax.nn.silu(c_ctx)[None]
    xc = ctx
    for l in range(DEPTH):
        last = l == DEPTH - 1
        lp = dict(w_in=w_in[l], g_qa=g_qa[l], w_uq=w_uq[l], g_kva=g_kva[l], w_ukv=w_ukv[l],
                  g_qn=g_qn[l], g_kn=g_kn[l], hy_conv_w=hy_conv_w[l], hy_conv_b=hy_conv_b[l],
                  hy_w1=hy_w1[l], hy_b1=hy_b1[l], hy_w2=hy_w2[l], hy_b2=hy_b2[l], hy_w3=hy_w3[l],
                  hy_b3=hy_b3[l], hy_freq=hy_freq[l], hy_decay=hy_decay[l], hy_bias=hy_bias[l],
                  gm_norm_g=gm_norm_g[l], gm_ws=gm_ws[l], gm_bs=gm_bs[l],
                  w_pa=w_pa[l], w_pb=w_pb[l], w_pc=w_pc[l], w_out=w_out[l])
        mod = jnp.split((silu_c @ w_mod[l] + b_mod[l])[:, None, :], N_MOD, axis=-1)
        n_ctx_mod = 2 if last else N_MOD
        mod_c = jnp.split((silu_cc @ w_mod[l][:, :n_ctx_mod * D_MODEL]
                           + b_mod[l][:n_ctx_mod * D_MODEL])[:, None, :], n_ctx_mod, axis=-1)

        hc = modulate(xc, norm1_g[l], mod_c[0], mod_c[1])
        if last:
            k_c, v_c = context_kv(hc, lp)
        else:
            y_c, k_c, v_c = token_mixer(hc, lp, None, None)
            xc = xc + mod_c[2] * y_c
            xc = xc + mod_c[5] * moe_ffn(modulate(xc, norm2_g[l], mod_c[3], mod_c[4]),
                                         router_w, router_b, moe_w_gate[l], moe_w_up[l], moe_w_down[l])

        h = modulate(x, norm1_g[l], mod[0], mod[1])
        y, _, _ = token_mixer(h, lp, rope, (k_c, v_c))
        x = x + mod[2] * y
        x = x + mod[5] * moe_ffn(modulate(x, norm2_g[l], mod[3], mod[4]),
                                 router_w, router_b, moe_w_gate[l], moe_w_up[l], moe_w_down[l])
    return x


_drawn_inputs = setup_inputs


def setup_inputs(seed=0):
    import zlib

    import numpy as np

    out = dict(_drawn_inputs(seed))
    spreads = {}
    factors = {'g_qa': 5.0, 'g_kva': 4.848, 'g_qn': 8.0, 'g_kn': 8.0, 'gm_norm_g': 4.83, 'gm_bs': 4.021}
    for name, (base, spread) in spreads.items():
        noise = np.random.default_rng([zlib.crc32(name.encode()), seed]).standard_normal(out[name].shape)
        drawn = base * np.exp(spread * noise) if base else spread * noise
        out[name] = jnp.asarray(drawn.astype(out[name].dtype))
    for name, factor in factors.items():
        out[name] = (out[name] * factor).astype(out[name].dtype)
    return out
```

```python
from contextlib import ExitStack

import numpy as np

import concourse.bass as bass
from concourse import mybir

F32 = mybir.dt.float32
BF16 = mybir.dt.bfloat16
ALU = mybir.AluOpType
ACT = mybir.ActivationFunctionType
AX = mybir.AxisListType

P = 128
D = 1024
KD = D // P
DEPTH = 2
LX = 256
LC = 256
T = LX + LC
GRID_W = 64
EPS = 1e-6
HEADS, NOPE, ROPE, VD = 8, 64, 32, 64
QK = NOPE + ROPE
QR, KVR = 384, 256
HY = 256
BANDS = 16
EMB = 1 + 2 * BANDS
HID = 64
GM = 256
GROUPS = 4
OFF_KV = QR
OFF_HY = QR + KVR + ROPE
OFF_GM = OFF_HY + 3 * HY
OFF_GT = OFF_GM + 2 * GM
NE, FE = 16, 512
KF = FE // P
SCALE = float(QK) ** -0.5
UNIT = 4096
RING = 3
BIG = 1e30
ROUND = 12582912.0
TWO_PI_HI = 6.28125
TWO_PI_LO = float(np.float32(2 * np.pi - 6.28125))

COLS = {}
_at = 0
for _name, _n in (("g1", 16), ("g2", 16), ("bmod", 96), ("gqa", 3), ("gkva", 2), ("gqn", 1), ("gkn", 1),
                  ("convw", 18), ("convb", 6), ("hybias", 2), ("gmg", 2), ("b1", 1), ("b2", 1), ("freq", 1)):
    COLS[_name] = (_at, _at + _n)
    _at += _n
NCOLS = _at
FW = 2 * HID + 2 * HY

MIX_UNITS = ["q", "kv", "uq", "ukv", "hy0", "hy1", "hy2", "gm", "p0", "gt00", "gt01", "gt02",
             "p1", "gt10", "gt11", "gt12", "out0", "out1"]
NMOD = 12
NMIX = len(MIX_UNITS)
NEXP = 3 * NE


def build(nc, ins, out, known, dump=None):
    counts, found = {}, {}
    ctx = ExitStack()
    with ctx:
        def sb(name, shape, dt=F32):
            return ctx.enter_context(nc.sbuf_tensor(name, shape, dt))

        stage = sb("stage", [P, RING, UNIT])
        whi = sb("whi", [P, RING, UNIT], BF16)
        wlo = sb("wlo", [P, RING, UNIT], BF16)
        xT = sb("xT", [P, KD, T])
        h = sb("h", [P, KD, 2, T], BF16)
        cos_s = sb("cos_s", [P, 2, 256])
        sin_s = sb("sin_s", [P, 2, 256])
        ident = sb("ident", [P, P])
        ones = sb("ones", [P, P])
        rope = sb("rope", [QK, 2, LX])
        rot = sb("rot", [QK, QK])
        rw = sb("rw", [P, KD, NE])
        rb = sb("rb", [P, NE])
        order = sb("order", [P, 4 + NE])
        esel = sb("esel", [NE, NE * P], BF16)
        cols = sb("cols", [P, DEPTH, NCOLS])
        cT = sb("cT", [P, KD, 2])
        modc = sb("modc", [P, 48, 2])
        gs = sb("gs", [P, 2, KD, 2])
        ws = sb("ws", [P, GROUPS, P])
        bs = sb("bs", [1, GROUPS * P])
        kfilt = sb("kfilt", [P, DEPTH, 2, 2, HY])
        small = sb("small", [P, 64])
        arena = sb("arena", [P, 52 * 256])
        ps = [ctx.enter_context(nc.psum_tensor(f"bank{i}", [P, 512], F32)) for i in range(8)]

        def kb(a, b):
            return arena[:, a * 256:b * 256]

        def pair(a, n):
            return kb(a, a + 2 * n).bitcast(BF16).rearrange("p (c s t) -> p c s t", c=n, s=2)

        def f32v(a, b, **dims):
            n = list(dims.values())
            if len(n) == 1:
                return kb(a, b).rearrange("p (a t) -> p a t", a=n[0])
            return kb(a, b).rearrange("p (a b t) -> p a b t", a=n[0], b=n[1])

        aT, bT, mT = pair(0, 4), pair(8, 2), pair(12, 2)
        sq, rstd, hf = f32v(16, 20, n=2), kb(20, 22), f32v(22, 26, n=2)
        pT, tmp = f32v(8, 12, n=4), f32v(12, 16, n=2)
        qn, kvn = pair(16, 3), pair(22, 2)
        kr, V = kb(26, 28), f32v(28, 36, n=4)
        qh, kh = f32v(36, 40, n=2), f32v(40, 44, n=2)
        prob = f32v(44, 48, n=2)
        rq = f32v(48, 52, n=2)
        pq, pkv = f32v(36, 42, n=3), f32v(44, 48, n=2)
        z = f32v(16, 28, n=6)
        pad = arena[:, 28 * 256:28 * 256 + 2 * 2 * 258].rearrange("p (b s t) -> p b s t", b=2, s=2)
        uR, U, Y = f32v(33, 35, n=2), f32v(35, 39, n=2, m=2), f32v(39, 43, n=2, m=2)
        hyt = f32v(43, 47, n=2, m=2)
        hyb = f32v(47, 49, n=2)
        gl, gsq, grs = f32v(16, 24, n=4), f32v(24, 28, n=2), kb(28, 30)
        vn, vR = f32v(30, 34, n=2), f32v(34, 38, n=4)
        gmt = f32v(38, 42, n=2)
        br, sig = f32v(16, 40, n=3, m=4), f32v(40, 44, n=2)
        ylo4, yhi4 = pair(44, 4), pair(0, 4)
        sg, cb, th = f32v(16, 24, n=4), f32v(24, 28, n=2), f32v(28, 36, n=4)
        hid = pair(36, 4)
        lgT, rt = kb(44, 46), kb(46, 48)
        combT = kb(48, 51).bitcast(BF16).rearrange("p (s t) -> p s t", s=3)
        fw = kb(16, 19)[:, 0:FW]
        zT, tneg = kb(19, 20), kb(20, 21)
        cosk, sink = f32v(21, 23, n=2), f32v(23, 25, n=2)
        fa, fk, fr_, fh = kb(25, 26), kb(26, 27), kb(27, 28), f32v(28, 30, n=2)
        dec, decay, kf = kb(30, 32), f32v(32, 36, n=2), f32v(36, 40, n=2)
        ksq, krs, kab = f32v(40, 44, n=2), kb(44, 45), f32v(45, 49, n=2, m=2)

        sems = {}

        def sem_of(kind):
            if kind not in sems:
                sems[kind] = ctx.enter_context(nc.semaphore(kind))
            return sems[kind]

        def now(kind, *which, by=1):
            counts[kind] = counts.get(kind, 0) + by
            assert (kind, *which) not in found, (kind, which)
            found[(kind, *which)] = counts[kind]
            return sem_of(kind), by

        def after(kind, *which):
            if known is None:
                return sem_of(kind), 1
            return sem_of(kind), known[(kind, *which)]

        s_stage = [sem_of(f"stage_loaded{i}") for i in range(RING)]
        s_hi, s_lo, s_used = sem_of("hi_split"), sem_of("lo_split"), sem_of("unit_used")
        s_mod = sem_of("mod_unit_used")

        def dma_unit(l, i):
            return l * (NMOD + NMIX + NEXP) + i

        def mix_unit(l, i):
            return l * (NMIX + NEXP) + i, dma_unit(l, NMOD + i)

        def expert_unit(l, e, i):
            return l * (NMIX + NEXP) + NMIX + 3 * e + i, dma_unit(l, NMOD + NMIX + 3 * e + i)

        def col(l, name):
            a, b = COLS[name]
            return cols[:, l, a:b]

        def unit_source(l, name):
            w = ins["w_in"][l]
            if name == "q":
                return [(0, 8 * QR, w[:, 0:QR], 8)]
            if name == "kv":
                return [(0, 8 * (KVR + ROPE), w[:, OFF_KV:OFF_HY], 8)]
            if name == "uq":
                return [(0, 3 * HEADS * QK, ins["w_uq"][l], 3)]
            if name == "ukv":
                return [(0, 2 * HEADS * (NOPE + VD), ins["w_ukv"][l], 2)]
            if name[:2] == "hy":
                a = OFF_HY + 256 * int(name[2])
                return [(0, 8 * 256, w[:, a:a + 256], 8)]
            if name == "gm":
                return [(0, UNIT, w[:, OFF_GM:OFF_GT], 8)]
            if name[0] == "p":
                c = slice(512 * int(name[1]), 512 * int(name[1]) + 512)
                return [(0, 2048, ins["w_pa"][l][:, c], 4), (2048, 3072, ins["w_pb"][l][:, c], 2),
                        (3072, 4096, ins["w_pc"][l][:, c], 2)]
            if name[:2] == "gt":
                a = OFF_GT + D * int(name[3]) + 512 * int(name[2])
                return [(0, UNIT, w[:, a:a + 512], 8)]
            return [(0, UNIT, ins["w_out"][l][:, 512 * int(name[3]):512 * int(name[3]) + 512], 8)]

        def unit_width(l, name):
            return max(b for _, b, _, _ in unit_source(l, name))

        block = ctx.enter_context(nc.Block())

        @block.sync
        def _(sp):
            for l in range(DEPTH):
                def mod_source(g):
                    return ins["w_mod"][l].rearrange("(k p) (g n) -> g p k n", p=P, n=512)[g]

                for g in range(NMOD):
                    n = dma_unit(l, g)
                    if g >= RING:
                        sp.wait_ge(s_mod, l * NMOD + g - RING + 1)
                    elif l > 0:
                        sp.wait_ge(s_lo, l * (NMIX + NEXP) - RING + g + 1)
                    sp.dma_start(stage[:, n % RING, :].rearrange("p (k n) -> p k n", k=8),
                                 mod_source(g)).then_inc(s_stage[n % RING], 16)
                for i, name in enumerate(MIX_UNITS):
                    su, n = mix_unit(l, i)
                    if i < RING:
                        sp.wait_ge(s_mod, (l + 1) * NMOD - RING + i + 1)
                    else:
                        sp.wait_ge(s_lo, su - RING + 1)
                    parts = unit_source(l, name)
                    for j, (a, b, src, k) in enumerate(parts):
                        ins_ = sp.dma_start(stage[:, n % RING, a:b].rearrange("p (k n) -> p k n", k=k),
                                            src.rearrange("(k p) n -> p k n", p=P))
                        ins_.then_inc(s_stage[n % RING], 16)
                gate, up, down = (ins[w][l].rearrange("e (k p) n -> e p k n", p=P)
                                  for w in ("moe_w_gate", "moe_w_up", "moe_w_down"))
                su0, _ = expert_unit(l, 0, 0)
                with sp.Fori(0, NE) as e:
                    for i, (w, k) in enumerate(((gate, 8), (up, 8), (down, 4))):
                        sp.wait_ge(s_lo, e * 3 + (su0 + i - RING + 1))
                        sp.dma_start(stage[:, i, :].rearrange("p (k n) -> p k n", k=k),
                                     w[bass.ds(e, 1)].rearrange("a p k n -> (a p) k n")).then_inc(s_stage[i], 16)
            for k in range(KD):
                if k % 4 == 0:
                    sp.wait_ge(*after("moe_added", DEPTH - 1, NE - 1, k + 3, 0))
                    sp.dma_start(out[:, k:k + 4, :], xT[:, k:k + 4, 0:LX]).then_inc(*now("stored", k, by=16))
            sp.wait_ge(*after("stored", 4))

        def landed(l, i):
            n = dma_unit(l, i)
            total = 0
            for m in range(n % RING, n + 1, RING):
                ll, ii = divmod(m, NMOD + NMIX + NEXP)
                j = ii - NMOD
                parts = 3 if 0 <= j < NMIX and MIX_UNITS[j][0] == "p" else 1
                total += 16 * parts
            return s_stage[n % RING], total

        @block.gpsimd
        def _(pool):
            for k, (dst, src) in enumerate(((cT[:], ins["cT"]), (cols[:], ins["cols"]),
                                            (ident[:], ins["ident"]), (ones[:], ins["ones"]))):
                pool.dma_start(dst, src).then_inc(*now("small_loaded", k, by=16))
            pool.wait_ge(*after("small_loaded", 3))
            for k, (dst, src) in enumerate((
                    (zT[0:EMB, :], ins["zT"]), (tneg[0:1, :], ins["tneg"]), (cosk, ins["cosk"]),
                    (sink, ins["sink"]), (fw, ins["fw"][0]), (dec[0:1, :], ins["decay"][0:1]))):
                pool.dma_start(dst, src).then_inc(*now("filter_loaded", 0, k, by=16))
            pool.dma_start(xT[:, :, 0:LX], ins["xT"]).then_inc(*now("x_loaded", 0, by=16))
            pool.dma_start(xT[:, :, LX:T], ins["ctxT"]).then_inc(*now("x_loaded", 1, by=16))
            for k, (dst, src) in enumerate((
                    (cos_s[:], ins["cos_s"]), (sin_s[:], ins["sin_s"]), (rope[:], ins["rope"]),
                    (rot[:], ins["rot"]), (rw[:], ins["rw"]), (rb[:], ins["rb"]), (order[:], ins["order"]),
                    (esel[:], ins["esel"]), (ws[:], ins["ws"][0]), (bs[:], ins["bs"][0:1]))):
                pool.dma_start(dst, src).then_inc(*now("const_loaded", k, by=16))
            pool.wait_ge(*after("filt_spec", 0, 1))
            pool.dma_start(fw, ins["fw"][1]).then_inc(*now("filter_loaded", 1, 4, by=16))
            pool.dma_start(dec[0:1, :], ins["decay"][1:2]).then_inc(*now("filter_loaded", 1, 5, by=16))
            for l in range(DEPTH):
                if l > 0:
                    pool.wait_ge(*after("gm_spatial", l - 1, 3))
                    pool.dma_start(ws[:], ins["ws"][l]).then_inc(*now("spatial_loaded", l, 0, by=16))
                    pool.dma_start(bs[:], ins["bs"][l:l + 1]).then_inc(*now("spatial_loaded", l, 1, by=16))
                n = T if l == 0 else LX

                def gated(e, first):
                    for i in range(KF):
                        if i == 0:
                            pool.wait_ge(sem_of(f"comb_spread{l}"), e + 1)
                        pool.wait_ge(sem_of(f"silu_gate{l}"), e * KF + i + 1)
                        nc.gpsimd.tensor_tensor(sg[:, i, 0:n], sg[:, i, 0:n], cb[:, 0, 0:n],
                                                ALU.mult).then_inc(sem_of(f"gate_weighted{l}"), 1)

                with pool.Fori(0, NE) as e:
                    gated(e, False)

        @block.tensor
        def _(pe):
            def mm(o, a, b, start, stop):
                return nc.tensor.matmul(o, a, b, start=start, stop=stop)

            def mm3(o, w, act, first, last):
                mm(o, w[0], act[0], first, False)
                mm(o, w[0], act[1], False, False)
                return mm(o, w[1], act[0], False, last)

            def weights(slot, k, kn, a, b, base=0):
                w = kn
                return (whi[:, slot, base + k * w + a:base + k * w + b], wlo[:, slot, base + k * w + a:base + k * w + b])

            def project(o, slot, width, a, b, n, hn=None, nk=8, base=0, act=None):
                act = h if act is None else act
                for k in range(nk):
                    last = mm3(o, weights(slot, k, width, a, b, base), (act[:, k, 0, 0:n], act[:, k, 1, 0:n]),
                               k == 0, k == nk - 1)
                return last

            pe.wait_ge(*after("small_loaded", 3))
            pe.wait_ge(*after("filter_loaded", 0, 5))
            for l in range(DEPTH):
                if l > 0:
                    pe.wait_ge(*after("filter_loaded", l, 5))
                mm(ps[0][0:HID, 0:256], fw[0:EMB, 0:HID], zT[0:EMB, 0:256], True, True).then_inc(*now("filt_mm", l, 0))
                pe.wait_ge(*after("filt_sin", l, 0))
                mm(ps[1][0:HID, 0:256], fw[0:HID, HID:2 * HID], fh[0:HID, 0, :], True, True).then_inc(*now("filt_mm", l, 1))
                pe.wait_ge(*after("filt_sin", l, 1))
                pe.wait_ge(*after("decay_abs", l))
                for c in range(2):
                    mm(ps[2 + c][:, :], fh[0:HID + 1, 1, c * P:c * P + P], fw[0:HID + 1, 2 * HID:FW], True, True)
                    mm(ps[4 + c][:, :], tneg[0:1, c * P:c * P + P], dec[0:1, :], True, True).then_inc(*now("filt_mm", l, 2 + c))
                for c in range(2):
                    pe.wait_ge(*after("filt_sq", l, c))
                    for d in range(2):
                        last = mm(ps[0][:, 0:256], ones[:], ksq[:, c, d * HY:d * HY + HY], c == 0 and d == 0, c == 1 and d == 1)
                last.then_inc(*now("filt_ssq", l))
                pe.wait_ge(*after("filt_ab", l))
                for f in range(2):
                    for part, table in ((0, cosk), (1, sink)):
                        if part == 0 and f == 0 and False:
                            pass
                        for c in range(2):
                            last = mm(ps[6 + f][:, part * 256:part * 256 + 256], table[:, c, f * P:f * P + P],
                                      kab[:, part, c, :], c == 0, c == 1)
                    last.then_inc(*now("filt_spec", l, f))

            for l in range(DEPTH):
                n = T if l == 0 else LX
                pe.wait_ge(*after("silu_c"))
                if l > 0:
                    pe.wait_ge(*after("moe_added", l - 1, NE - 1, 7, 1))
                with pe.Fori(0, NMOD // RING) as g:
                    for i in range(RING):
                        pe.wait_ge(s_stage[i], g * 16 + landed(l, i)[1])
                        for m in range(4):
                            o = ps[0][:, bass.ds(g * (RING * 8) + (i * 8 + m * 2), 2)]
                            for k in range(KD):
                                last = mm(o, stage[:, i, k * 512 + m * P:k * 512 + m * P + P], cT[:, k, :],
                                          k == 0, k == KD - 1)
                        last.then_inc(s_mod, 1)

                def norm_sum(which):
                    m = T if which == 0 else n
                    for k in range(KD):
                        if which == 1 and k == 0:
                            pe.wait_ge(*after("x_mixed", l, 7))
                        pe.wait_ge(*after("x_squared", l, which, k))
                        mm(ps[1][:, 0:m], ones[:], sq[:, k % 2, 0:m], k == 0, k == KD - 1).then_inc(*now("x_summed", l, which, k))

                norm_sum(0)
                for k in range(KD):
                    pe.wait_ge(*after("h_ready", l, 0, k))

                def unit(i):
                    su, _ = mix_unit(l, i)
                    pe.wait_ge(s_lo, su + 1)
                    return su % RING

                s = unit(0)
                for m in range(3):
                    last = project(ps[2 + m][:, 0:n], s, QR, m * P, m * P + P, n)
                    last.then_inc(*now("q_low", l, m)) if m < 2 else None
                last.then_inc(s_used, 1)
                mm(ps[0][0:1, 0:1], ones[:, 0:1], ones[:, 0:1], True, True).then_inc(*now("q_low", l, 2))
                s = unit(1)
                for m in range(2):
                    project(ps[5 + m][:, 0:T], s, KVR + ROPE, m * P, m * P + P, T).then_inc(*now("kv_low", l, m))
                o = ps[7][NOPE:QK, 0:T]
                for k in range(8):
                    last = mm3(o, weights(s, k, KVR + ROPE, KVR, KVR + ROPE), (h[:, k, 0, 0:T], h[:, k, 1, 0:T]), k == 0, k == 7)
                last.then_inc(s_used, 1)
                mm(ps[0][0:1, 1:2], ones[:, 0:1], ones[:, 0:1], True, True).then_inc(*now("kv_low", l, 2))
                for m in range(3):
                    pe.wait_ge(*after("q_low_sq", l, m))
                    mm(ps[0][:, 0:n], ones[:], tmp[:, m % 2, 0:n], m == 0, m == 2).then_inc(*now("q_low_sum", l, m))
                for m in range(2):
                    pe.wait_ge(*after("kv_low_sq", l, m))
                    mm(ps[1][:, 0:T], ones[:], tmp[:, (m + 1) % 2, 0:T], m == 0, m == 1).then_inc(*now("kv_low_sum", l, m))

                sq_, skv = unit(2), unit(3)
                pe.wait_ge(*after("kvn_ready", l))
                for tc in range(4):
                    b = 2 + tc
                    for k in range(2):
                        v = [w[:, skv, k * 1024:k * 1024 + 1024].rearrange("p (h c) -> p h c", h=HEADS)[:, :, NOPE:NOPE + VD]
                             for w in (whi, wlo)]
                        c = slice(tc * P, tc * P + P)
                        mm(ps[b][:, :], kvn[:, k, 0, c], v[0], k == 0, False)
                        mm(ps[b][:, :], kvn[:, k, 1, c], v[0], False, False)
                        last = mm(ps[b][:, :], kvn[:, k, 0, c], v[1], False, k == 1)
                    last.then_inc(*now("v_mm", l, tc))

                def heads_project(i):
                    if i == 0:
                        pe.wait_ge(*after("kvn_ready", l))
                        pe.wait_ge(*after("qn_ready", l))
                    else:
                        pe.wait_ge(*after("q_roped", l, i - 1))
                        pe.wait_ge(*after("k_roped", l, i - 1))
                    for k in range(3):
                        last = mm3(ps[0][0:QK, 0:n], weights(sq_, k, HEADS * QK, i * QK, i * QK + QK),
                                   (qn[:, k, 0, 0:n], qn[:, k, 1, 0:n]), k == 0, k == 2)
                    last.then_inc(*now("q_mm", l, i))
                    for k in range(2):
                        last = mm3(ps[1][0:NOPE, 0:T], weights(skv, k, 1024, i * P, i * P + NOPE),
                                   (kvn[:, k, 0, 0:T], kvn[:, k, 1, 0:T]), k == 0, k == 1)
                    last.then_inc(*now("k_mm", l, i))

                def heads_sum(i):
                    if i == 0:
                        pe.wait_ge(*after("v_copied", l, 1))
                    else:
                        pe.wait_ge(*after("k_root", l, i - 1))
                    pe.wait_ge(*after("q_squared", l, i))
                    mm(ps[2][0:QK, 0:n], ones[0:QK, 0:QK], tmp[0:QK, 0, 0:n], True, True).then_inc(*now("q_sum", l, i))
                    pe.wait_ge(*after("k_squared", l, i))
                    mm(ps[3][0:QK, 0:T], ones[0:QK, 0:QK], tmp[0:QK, 1, 0:T], True, True).then_inc(*now("k_sum", l, i))

                def heads_rotate(i):
                    b = i % 2
                    pe.wait_ge(*after("q_normed", l, i))
                    mm(ps[0][0:QK, 0:LX], rot[:], qh[0:QK, b, 0:LX], True, True).then_inc(*now("q_rot", l, i))
                    pe.wait_ge(*after("k_normed", l, i))
                    mm(ps[1][0:QK, 0:LX], rot[:], kh[0:QK, b, 0:LX], True, True).then_inc(*now("k_rot", l, i))

                tiles = [(0, 0, T), (1, 0, T)] + ([(2, LX, T), (3, LX, T)] if l == 0 else [])

                def scores(i, t):
                    b = i % 2
                    qt, ka, kz = tiles[t]
                    seq = i * len(tiles) + t
                    if t == 0:
                        pe.wait_ge(*after("q_roped", l, i))
                        pe.wait_ge(*after("k_roped", l, i))
                        if i == 0:
                            pe.wait_ge(*after("v_copied", l, 3))
                    if seq >= 2:
                        pe.wait_ge(*after("exp_done", l, seq - 2))
                    mm(ps[4 + seq % 2][:, 0:kz - ka], qh[0:QK, b, qt * P:qt * P + P], kh[0:QK, b, ka:kz],
                       True, True).then_inc(*now("scores", l, seq))

                def turn(i, t):
                    qt, ka, kz = tiles[t]
                    seq = i * len(tiles) + t
                    pe.wait_ge(*after("prob_ready", l, seq))
                    if seq >= 1:
                        pe.wait_ge(*after("prob_turned", l, seq - 1))
                    elif l == 0:
                        pe.wait_ge(*after("kvn_ready", l))
                    for c in range((kz - ka) // P):
                        last = nc.tensor.transpose(ps[6][:, c * P:c * P + P], prob[:, seq % 2, c * P:c * P + P], ident[:])
                    last.then_inc(*now("prob_turn", l, seq))

                def values(i, g):
                    nk = 4 if g == 0 else 2
                    r = (i % 2) * VD
                    seq = i * (len(tiles) // 2) + g
                    if seq >= 1:
                        pe.wait_ge(*after("a_done", l, seq - 1))
                    else:
                        pe.wait_ge(*after("kr_copied", l))
                    pe.wait_ge(*after("prob_turned", l, i * len(tiles) + 2 * g + 1))
                    for c in range(nk):
                        last = mm(ps[7][r:r + VD, 0:LX], V[:, 4 - nk + c, i * VD:i * VD + VD], pT[:, c, :], c == 0, c == nk - 1)
                    last.then_inc(*now("pv", l, seq))

                for i in range(HEADS + 1):
                    if i < HEADS:
                        heads_project(i)
                    if i > 0:
                        scores(i - 1, 0)
                        scores(i - 1, 1)
                    if i < HEADS:
                        heads_sum(i)
                    if i > 0:
                        turn(i - 1, 0)
                        turn(i - 1, 1)
                        if l == 0:
                            scores(i - 1, 2)
                            scores(i - 1, 3)
                        values(i - 1, 0)
                    if i < HEADS:
                        heads_rotate(i)
                    if i > 0 and l == 0:
                        turn(i - 1, 2)
                        turn(i - 1, 3)
                        values(i - 1, 1)
                    if i == HEADS - 1:
                        mm(ps[2][0:1, 0:1], ones[:, 0:1], ones[:, 0:1], True, True).then_inc(s_used, 1)
                        mm(ps[2][0:1, 0:1], ones[:, 0:1], ones[:, 0:1], True, True).then_inc(s_used, 1)

                for c in range(6):
                    if c % 2 == 0:
                        s = unit(4 + c // 2)
                    pe.wait_ge(*(after("pad_copied", l, c - 2) if c >= 2 else after("k_roped", l, HEADS - 1)))
                    last = project(ps[c % 2][:, 0:n], s, 256, (c % 2) * P, (c % 2) * P + P, n)
                    last.then_inc(*now("hy_mm", l, c))
                    if c % 2:
                        mm(ps[2][0:1, 0:1], ones[:, 0:1], ones[:, 0:1], True, True).then_inc(s_used, 1)
                s = unit(7)
                pe.wait_ge(*after("a_done", l, HEADS * (len(tiles) // 2) - 1))
                pe.wait_ge(*after("hy_last", l, (n // 256) - 1, 0)) if False else None
                for c in range(4):
                    last = project(ps[4 + c][:, 0:n], s, 512, c * P, c * P + P, n)
                    last.then_inc(*now("gm_mm", l, c))
                mm(ps[2][0:1, 0:1], ones[:, 0:1], ones[:, 0:1], True, True).then_inc(s_used, 1)

                for st in range(n // 256):
                    if st == 0:
                        pe.wait_ge(*after("u_ready", l))
                    else:
                        pe.wait_ge(*after("uR_copied", l, st - 1))
                    for tc in range(2):
                        for c in range(2):
                            last = nc.tensor.transpose(ps[2][:, tc * 256 + c * P:tc * 256 + c * P + P],
                                                       z[:, 2 + c, st * 256 + tc * P:st * 256 + tc * P + P], ident[:])
                    last.then_inc(*now("u_turned", l, st))
                    pe.wait_ge(*after("uR_copied", l, st))
                    if st == 0:
                        pe.wait_ge(*after("pad_copied", l, 5))
                    else:
                        pe.wait_ge(*after("U_copied", l, st - 1))
                    for part, table in ((0, cos_s), (1, sin_s)):
                        for f in range(2):
                            for tc in range(2):
                                last = mm(ps[part][:, f * 256:f * 256 + 256], table[:, tc, f * P:f * P + P], uR[:, tc, :],
                                          tc == 0, tc == 1)
                    last.then_inc(*now("u_spec", l, st))
                    pe.wait_ge(*after("Y_ready", l, st))
                    if st > 0:
                        pe.wait_ge(*after("b_done", l, st - 1))
                    for c in range(2):
                        q = 0
                        for part, table in ((0, cos_s), (1, sin_s)):
                            for f in range(2):
                                last = mm(ps[3][:, c * 256:c * 256 + 256], Y[:, part, f, c * P:c * P + P], table[:, f, :],
                                          q == 0, q == 3)
                                q += 1
                    last.then_inc(*now("y_back", l, st))

                for c in range(2):
                    pe.wait_ge(*after("gv_sq", l, c))
                    if c == 0:
                        pe.wait_ge(*after("U_copied", l, n // 256 - 1))
                    mm(ps[0][:, 0:n], ones[:], gsq[:, c, 0:n], c == 0, c == 1).then_inc(*now("gv_sum", l, c))
                pe.wait_ge(*after("gv_normed", l))
                pe.wait_ge(*after("uR_copied", l, n // 256 - 1))
                for tc in range(n // P):
                    bk = (1, 2)[tc % 2]
                    if tc >= 2:
                        pe.wait_ge(*after("vR_copied", l, tc - 2))
                    for c in range(2):
                        last = nc.tensor.transpose(ps[bk][:, c * P:c * P + P], vn[:, c, tc * P:tc * P + P], ident[:])
                    last.then_inc(*now("gv_turned", l, tc))
                pe.wait_ge(*(after("const_loaded", 9) if l == 0 else after("spatial_loaded", l, 1)))
                pe.wait_ge(*after("gm_gelu", l, 3))
                pe.wait_ge(*after("vR_copied", l, n // P - 1))
                for g in range(GROUPS):
                    r = (g % 2) * 64
                    o = ps[4 + g // 2]
                    for tc in range(n // P):
                        oo = o[r:r + 64, tc * P:tc * P + P]
                        mm(oo, vR[:, tc, g * 64:g * 64 + 64], ws[:, g, :], True, False)
                        last = mm(oo, ones[0:1, 0:64], bs[0:1, g * P:g * P + P], False, True)
                    last.then_inc(*now("gm_spatial", l, g))

                def y_of(half):
                    return ylo4 if half == 0 else yhi4

                chunk = 0
                for half in range(2):
                    s = unit(8 + 4 * half)
                    if half == 0:
                        pe.wait_ge(*after("a_done", l, HEADS * (len(tiles) // 2) - 1))
                        pe.wait_ge(*after("b_done", l, n // 256 - 1))
                        pe.wait_ge(*after("m_done", l, 1))
                        pe.wait_ge(*after("vR_copied", l, n // P - 1))
                    for b, (act, nk, base) in enumerate(((aT, 4, 0), (bT, 2, 2048), (mT, 2, 3072))):
                        for j in range(4):
                            if chunk >= 4:
                                pe.wait_ge(*after("merge_evac", l, chunk - 4))
                            last = project(ps[chunk % 4][:, 0:n], s, 512, j * P, j * P + P, n, nk=nk, base=base, act=act)
                            last.then_inc(*now("branch_mm", l, half, b, j))
                            chunk += 1
                    mm(ps[4][0:1, 0:1], ones[:, 0:1], ones[:, 0:1], True, True).then_inc(s_used, 1)
                    for b in range(3):
                        s = unit(9 + 4 * half + b)
                        for j in range(4):
                            pe.wait_ge(*after("merge_evac", l, chunk - 4))
                            project(ps[chunk % 4][:, 0:n], s, 512, j * P, j * P + P, n).then_inc(*now("gate_mm", l, half, b, j))
                            chunk += 1
                        mm(ps[4][0:1, 0:1], ones[:, 0:1], ones[:, 0:1], True, True).then_inc(s_used, 1)
                for half in range(2):
                    s = unit(16 + half)
                    for j in range(4):
                        c = 4 * half + j
                        pe.wait_ge(*(after("merge_evac", l, chunk - 4) if c < 4 else after("x_mixed", l, c - 4)))
                        for k in range(8):
                            if c == 0:
                                pe.wait_ge(*after("y_ready", l, k))
                            y = y_of(k // 4)
                            last = mm3(ps[chunk % 4][:, 0:n], weights(s, k, 512, j * P, j * P + P),
                                       (y[:, k % 4, 0, 0:n], y[:, k % 4, 1, 0:n]), k == 0, k == 7)
                        last.then_inc(*now("out_mm", l, c))
                        chunk += 1
                    mm(ps[4][0:1, 0:1], ones[:, 0:1], ones[:, 0:1], True, True).then_inc(s_used, 1)

                norm_sum(1)
                pe.wait_ge(*after("x_mixed", l, 7))
                for k in range(KD):
                    pe.wait_ge(*after("hf_ready", l, k))
                    mm(ps[0][0:NE, 0:n], rw[:, k, :], hf[:, k % 2, 0:n], k == 0, k == KD - 1).then_inc(*now("logits", l, k))
                pe.wait_ge(*after("logits_copied", l))
                for tc in range(n // P):
                    last = nc.tensor.transpose(ps[2][:, tc * NE:tc * NE + NE], lgT[0:NE, tc * P:tc * P + P], ident[0:NE, 0:NE])
                last.then_inc(*now("logits_turned", l))
                pe.wait_ge(*after("comb", l))
                for tc in range(n // P):
                    last = nc.tensor.transpose(ps[3][0:NE, tc * P:tc * P + P], rt[:, 256 + tc * NE:256 + tc * NE + NE], ident[:])
                last.then_inc(*now("comb_turned", l))
                pe.wait_ge(*after("comb_split", l))

                gate_ev, up_ev = sem_of(f"silu_gate{l}"), sem_of(f"up_used{l}")
                spread, spread_mm = sem_of(f"comb_spread{l}"), sem_of(f"comb_mm{l}")
                gate_mm, up_mm, down_mm = sem_of(f"expert_gate_mm{l}"), sem_of(f"expert_up_mm{l}"), sem_of(f"expert_down_mm{l}")
                hid_s, down_ev = sem_of(f"hidden_split{l}"), sem_of(f"down_added{l}")
                su0, _ = expert_unit(l, 0, 0)

                def expert(e, first=False):
                    pe.wait_ge(s_lo, e * 3 + (su0 + 1))
                    for i in range(KF):
                        if not first:
                            pe.wait_ge(down_ev, e * 8 + (i + 1 - 8))
                        project(ps[i][:, 0:n], 0, 512, i * P, i * P + P, n).then_inc(gate_mm, 1)
                        if i == 1:
                            if not first:
                                pe.wait_ge(down_ev, e * 8)
                            for q in range(3):
                                last = mm(ps[7][:, 0:n], esel[:, bass.ds(e * P, P)] if not isinstance(e, int) else esel[:, e * P:e * P + P],
                                          combT[0:NE, q, 0:n], q == 0, q == 2)
                            last.then_inc(spread_mm, 1)
                    mm(ps[6][0:1, 0:1], ones[:, 0:1], ones[:, 0:1], True, True).then_inc(s_used, 1)
                    pe.wait_ge(s_lo, e * 3 + (su0 + 2))
                    for i in range(KF):
                        if i == KF - 1:
                            pe.wait_ge(spread, e + 1)
                        project(ps[4 + i][:, 0:n], 1, 512, i * P, i * P + P, n).then_inc(up_mm, 1)
                    pe.wait_ge(gate_ev, e * KF + 1)
                    mm(ps[0][0:1, 0:1], ones[:, 0:1], ones[:, 0:1], True, True).then_inc(s_used, 1)
                    pe.wait_ge(s_lo, e * 3 + (su0 + 3))
                    for j in range(8):
                        if j < KF:
                            pe.wait_ge(gate_ev, e * KF + (j + 1))
                        else:
                            pe.wait_ge(up_ev, e * KF + (j - KF + 1))
                        for k in range(KF):
                            if j == 0:
                                pe.wait_ge(hid_s, e * KF + (k + 1))
                            last = mm3(ps[j][:, 0:n], weights(2, k, 1024, j * P, j * P + P),
                                       (hid[:, k, 0, 0:n], hid[:, k, 1, 0:n]), k == 0, k == KF - 1)
                        last.then_inc(down_mm, 1)
                    pe.wait_ge(down_ev, e * 8 + 1)
                    mm(ps[0][0:1, 0:1], ones[:, 0:1], ones[:, 0:1], True, True).then_inc(s_used, 1)

                expert(0, True)
                with pe.Fori(1, NE) as e:
                    expert(e)

        @block.scalar
        def _(act):
            def f(o, i, func, **kw):
                return nc.scalar.activation(o, i, func, **kw)

            def split_hi(i, su, n_landed, width, slot):
                act.wait_ge(*n_landed)
                if su >= RING:
                    act.wait_ge(s_used, su - RING + 1)
                f(whi[:, slot, 0:width], stage[:, slot, 0:width], ACT.Copy).then_inc(s_hi, 1)

            def split(l, i):
                if i < NMIX:
                    su, _ = mix_unit(l, i)
                    split_hi(i, su, landed(l, NMOD + i), unit_width(l, MIX_UNITS[i]), su % RING)
                else:
                    su, _ = expert_unit(l, 0, i - NMIX)
                    split_hi(i, su, landed(l, NMOD + i), UNIT, su % RING)

            act.wait_ge(*after("small_loaded", 3))
            f(cT[:], cT[:], ACT.Silu).then_inc(*now("silu_c"))
            for l in range(DEPTH):
                for i in range(2):
                    act.wait_ge(*after("filt_arg", l, i))
                    f(fh[0:HID, i, :], fr_[0:HID, :], ACT.Sin).then_inc(*now("filt_sin", l, i))
                for c in range(2):
                    act.wait_ge(*after("filt_mm", l, 2 + c))
                    f(decay[:, c, :], ps[4 + c][:, :], ACT.Exp).then_inc(*now("filt_decay", l, c))
                for c in range(2):
                    act.wait_ge(*after("filt_k", l, c))
                    f(ksq[:, c, :], kf[:, c, :], ACT.Square).then_inc(*now("filt_sq", l, c))
                act.wait_ge(*after("filt_eps", l))
                f(krs[:, :], krs[:, :], ACT.Sqrt).then_inc(*now("filt_root", l))

            for l in range(DEPTH):
                n = T if l == 0 else LX

                def squares(which):
                    m = T if which == 0 else n
                    for k in range(KD):
                        if which == 0 and l == 0 and k == 0:
                            act.wait_ge(*after("x_loaded", 1))
                            act.wait_ge(*after("filt_spec", DEPTH - 1, 1))
                            act.wait_ge(*after("filt_copied", DEPTH - 1, 1))
                        elif which == 0 and k == 0:
                            act.wait_ge(*after("moe_added", l - 1, NE - 1, 7, 1))
                        elif which == 1:
                            act.wait_ge(*after("x_mixed", l, k))
                            if k == 0:
                                act.wait_ge(*after("y_ready", l, 7))
                        if k >= 2:
                            act.wait_ge(*after("x_summed", l, which, k - 2))
                        f(sq[:, k % 2, 0:m], xT[:, k, 0:m], ACT.Square).then_inc(*now("x_squared", l, which, k))
                    act.wait_ge(*after("x_summed", l, which, 7))
                    act.wait_ge(*after("eps_set"))
                    f(rstd[:, 0:m], ps[1][:, 0:m], ACT.Sqrt, bias=small[:, 60:61], scale=1.0 / D).then_inc(*now("x_root", l, which))

                squares(0)
                split(l, 0)
                split(l, 1)
                for m in range(3):
                    act.wait_ge(*after("q_low", l, 2 if m == 2 else m))
                    if m == 0:
                        act.wait_ge(*after("h_ready", l, 0, 7))
                    if m == 2:
                        act.wait_ge(*after("q_low_sum", l, 0))
                    f(pq[:, m, 0:n], ps[2 + m][:, 0:n], ACT.Copy).then_inc(*now("q_low_copied", l, m))
                    act.wait_ge(*after("q_low_copied", l, m))
                    f(tmp[:, m % 2, 0:n], pq[:, m, 0:n], ACT.Square).then_inc(*now("q_low_sq", l, m))
                split(l, 2)
                for m in range(2):
                    act.wait_ge(*after("kv_low", l, m))
                    act.wait_ge(*after("q_low_sum", l, 1 + m))
                    f(pkv[:, m, :], ps[5 + m][:, :], ACT.Copy).then_inc(*now("kv_low_copied", l, m))
                    act.wait_ge(*after("kv_low_copied", l, m))
                    f(tmp[:, (m + 1) % 2, :], pkv[:, m, :], ACT.Square).then_inc(*now("kv_low_sq", l, m))
                act.wait_ge(*after("kv_low", l, 2))
                f(kr[NOPE:QK, :], ps[7][NOPE:QK, :], ACT.Copy).then_inc(*now("kr_copied", l))
                act.wait_ge(*after("q_low_sum", l, 2))
                f(rq[:, 0, 0:n], ps[0][:, 0:n], ACT.Sqrt, bias=small[:, 60:61], scale=1.0 / QR).then_inc(*now("q_low_root", l))
                act.wait_ge(*after("kv_low_sum", l, 1))
                f(rq[:, 1, :], ps[1][:, :], ACT.Sqrt, bias=small[:, 60:61], scale=1.0 / KVR).then_inc(*now("kv_low_root", l))
                split(l, 3)
                for tc in range(4):
                    act.wait_ge(*after("v_mm", l, tc))
                    f(V[:, tc, :], ps[2 + tc][:, :], ACT.Copy).then_inc(*now("v_copied", l, tc))
                split(l, 4)

                ntile = 4 if l == 0 else 2

                def head_copies(i):
                    b = i % 2
                    act.wait_ge(*after("q_mm", l, i))
                    if i == 0:
                        act.wait_ge(*after("qn_ready", l))
                        act.wait_ge(*after("kvn_ready", l))
                    if i >= 2:
                        act.wait_ge(*after("scores", l, (i - 1) * ntile - 1))
                    f(qh[0:QK, b, 0:n], ps[0][0:QK, 0:n], ACT.Copy).then_inc(*now("q_copied", l, i))
                    act.wait_ge(*after("k_mm", l, i))
                    f(kh[0:NOPE, b, :], ps[1][0:NOPE, :], ACT.Copy).then_inc(*now("k_copied", l, i))
                    act.wait_ge(*after("kr_copied", l))
                    f(kh[NOPE:QK, b, :], kr[NOPE:QK, :], ACT.Copy).then_inc(*now("kr_placed", l, i))
                    act.wait_ge(*after("q_copied", l, i))
                    if i == 0:
                        act.wait_ge(*after("kv_low_sum", l, 1))
                    else:
                        act.wait_ge(*after("q_roped", l, i - 1))
                        act.wait_ge(*after("k_roped", l, i - 1))
                    f(tmp[0:QK, 0, 0:n], qh[0:QK, b, 0:n], ACT.Square).then_inc(*now("q_squared", l, i))
                    act.wait_ge(*after("kr_placed", l, i))
                    f(tmp[0:QK, 1, :], kh[0:QK, b, :], ACT.Square).then_inc(*now("k_squared", l, i))

                def head_roots(i):
                    act.wait_ge(*after("q_sum", l, i))
                    if i > 0:
                        act.wait_ge(*after("k_normed", l, i - 1))
                    f(rq[0:QK, 0, 0:n], ps[2][0:QK, 0:n], ACT.Sqrt, bias=small[0:QK, 60:61], scale=1.0 / QK).then_inc(*now("q_root", l, i))
                    act.wait_ge(*after("k_sum", l, i))
                    f(rq[0:QK, 1, :], ps[3][0:QK, :], ACT.Sqrt, bias=small[0:QK, 60:61], scale=1.0 / QK).then_inc(*now("k_root", l, i))

                def exps(i, t):
                    seq = i * ntile + t
                    nk = T if t < 2 else LC
                    act.wait_ge(*after("max_ready", l, seq))
                    if seq >= 2:
                        act.wait_ge(*after("prob_turn", l, seq - 2))
                    elif seq == 0:
                        act.wait_ge(*after("kvn_ready", l))
                    s2 = 4 * (seq % 2)
                    f(prob[:, seq % 2, 0:nk], ps[4 + seq % 2][:, 0:nk], ACT.Exp, bias=small[:, s2:s2 + 1],
                      scale=SCALE, accum_out=small[:, s2 + 1:s2 + 2]).then_inc(*now("exp_done", l, seq))

                def turned(i, t):
                    seq = i * ntile + t
                    nk = 4 if t < 2 else 2
                    act.wait_ge(*after("prob_turn", l, seq))
                    if t % 2 == 0:
                        if seq > 0:
                            act.wait_ge(*after("pv", l, seq // 2 - 1))
                    f(pT[:, 0:nk, (t % 2) * P:(t % 2) * P + P],
                      ps[6][:, 0:nk * P].rearrange("p (c q) -> p c q", c=nk), ACT.Copy).then_inc(*now("prob_turned", l, seq))

                for i in range(HEADS + 1):
                    if i < HEADS:
                        head_copies(i)
                    if i > 0:
                        exps(i - 1, 0)
                        exps(i - 1, 1)
                    if i < HEADS:
                        head_roots(i)
                    if i > 0:
                        turned(i - 1, 0)
                        turned(i - 1, 1)
                        if l == 0:
                            exps(i - 1, 2)
                            exps(i - 1, 3)
                            turned(i - 1, 2)
                            turned(i - 1, 3)

                split(l, 5)
                split(l, 6)
                for c in range(6):
                    act.wait_ge(*after("hy_mm", l, c))
                    if c >= 2:
                        act.wait_ge(*after("conv_done", l, c - 2))
                    else:
                        act.wait_ge(*after("pads_zero", l))
                    f(pad[:, c % 2, 0:n // 256, 1:257], ps[c % 2][:, 0:n].rearrange("p (s t) -> p s t", t=256),
                      ACT.Copy).then_inc(*now("pad_copied", l, c))
                    if c == 1:
                        split(l, 7)
                    if c == 3:
                        split(l, 8)
                    if c == 5:
                        split(l, 9)

                for st in range(n // 256):
                    act.wait_ge(*after("u_turned", l, st))
                    f(uR, ps[2][:, :].rearrange("p (c t) -> p c t", c=2), ACT.Copy).then_inc(*now("uR_copied", l, st))
                    act.wait_ge(*after("u_spec", l, st))
                    if st > 0:
                        act.wait_ge(*after("Y_ready", l, st - 1))
                    f(U[:, 0], ps[0][:, :].rearrange("p (f c) -> p f c", f=2), ACT.Copy)
                    f(U[:, 1], ps[1][:, :].rearrange("p (f c) -> p f c", f=2), ACT.Copy).then_inc(*now("U_copied", l, st))
                act.wait_ge(*after("b_done", l, n // 256 - 1))
                for c in range(4):
                    act.wait_ge(*after("gm_mm", l, c))
                    f(gl[:, c, 0:n], ps[4 + c][:, 0:n], ACT.Gelu_apprx_tanh).then_inc(*now("gm_gelu", l, c))
                for c in range(2):
                    act.wait_ge(*after("gm_gelu", l, 2 + c))
                    f(gsq[:, c, 0:n], gl[:, 2 + c, 0:n], ACT.Square).then_inc(*now("gv_sq", l, c))
                act.wait_ge(*after("gv_sum", l, 1))
                f(grs[:, 0:n], ps[0][:, 0:n], ACT.Sqrt, bias=small[:, 60:61], scale=1.0 / GM).then_inc(*now("gv_root", l))
                for tc in range(n // P):
                    act.wait_ge(*after("gv_turned", l, tc))
                    f(vR[:, tc, :], ps[(1, 2)[tc % 2]][:, 0:256], ACT.Copy).then_inc(*now("vR_copied", l, tc))

                chunk = 0
                for half in range(2):
                    for b in range(3):
                        for j in range(4):
                            act.wait_ge(*after("branch_mm", l, half, b, j))
                            if b == 0 and j == 0:
                                act.wait_ge(*(after("m_done", l, 1) if half == 0 else after("y_ready", l, 3)))
                            f(br[:, b, j, 0:n], ps[chunk % 4][:, 0:n], ACT.Copy).then_inc(*now("merge_evac", l, chunk))
                            chunk += 1
                    for b in range(3):
                        split(l, 10 + 4 * half + b)
                        for j in range(4):
                            act.wait_ge(*after("gate_mm", l, half, b, j))
                            g = half * 12 + b * 4 + j
                            if g >= 2:
                                act.wait_ge(*after("gated", l, g - 2))
                            f(sig[:, g % 2, 0:n], ps[chunk % 4][:, 0:n], ACT.Sigmoid).then_inc(*now("merge_evac", l, chunk))
                            chunk += 1
                    split(l, 13 + 4 * half)
                split(l, 18)
                squares(1)
                split(l, 19)
                act.wait_ge(*after("logits_turned", l))
                m4 = n // P
                f(rt[:, 0:NE * m4], ps[2][:, 0:NE * m4], ACT.Sigmoid).then_inc(*now("aff", l))

                gate_mm, up_mm = sem_of(f"expert_gate_mm{l}"), sem_of(f"expert_up_mm{l}")
                gate_ev, wgt = sem_of(f"silu_gate{l}"), sem_of(f"gate_weighted{l}")
                hid_hi, up_used = sem_of(f"hidden_hi{l}"), sem_of(f"up_used{l}")
                spread_mm, spread = sem_of(f"comb_mm{l}"), sem_of(f"comb_spread{l}")
                su0, _ = expert_unit(l, 0, 0)
                base = [landed(l, NMOD + NMIX + i)[1] for i in range(3)]

                def split_expert(e, i, off):
                    act.wait_ge(s_stage[i], e * 16 + (base[i] + 16 * off))
                    act.wait_ge(s_used, e * 3 + (su0 + i + 3 * off - RING + 1))
                    f(whi[:, i, :], stage[:, i, :], ACT.Copy).then_inc(s_hi, 1)

                def expert(e, first=False, last=False):
                    split_expert(e, 2, 0)
                    for i in range(KF):
                        act.wait_ge(gate_mm, e * KF + (i + 1))
                        if not first:
                            act.wait_ge(up_used, e * KF + (i + 1 - KF))
                        f(sg[:, i, 0:n], ps[i][:, 0:n], ACT.Silu).then_inc(gate_ev, 1)
                        if i == 1:
                            act.wait_ge(spread_mm, e + 1)
                            if not first:
                                act.wait_ge(wgt, e * KF)
                            f(cb[:, 0, 0:n], ps[7][:, 0:n], ACT.Copy).then_inc(spread, 1)
                    if not last:
                        split_expert(e, 0, 1)
                    for i in range(KF):
                        act.wait_ge(up_used, e * KF + (i + 1))
                        if not first and i == 0:
                            act.wait_ge(sem_of(f"expert_down_mm{l}"), e * 8)
                        f(hid[:, i, 0, 0:n], th[:, i, 0:n], ACT.Copy).then_inc(hid_hi, 1)
                    if not last:
                        split_expert(e, 1, 1)

                expert(0, True)
                with act.Fori(1, NE - 1) as e:
                    expert(e)
                expert(NE - 1, False, True)

        @block.vector
        def _(dve):
            chain = sem_of("vector_step")
            steps = [0]

            def link(ins_):
                steps[0] += 1
                ins_.then_inc(chain, 1)
                dve.wait_ge(chain, steps[0])

            def tt(o, a, b, op):
                return nc.vector.tensor_tensor(o, a, b, op)

            def ts(o, a, s1, s2, op0, op1=None):
                if op1 is None:
                    return nc.vector.tensor_scalar(o, a, s1, None, op0)
                return nc.vector.tensor_scalar(o, a, s1, s2, op0, op1)

            def stt(o, a, s, b, op0, op1):
                return nc.vector.scalar_tensor_tensor(out=o, in0=a, scalar=s, in1=b, op0=op0, op1=op1)

            def split(l, i):
                if i < NMIX:
                    su, _ = mix_unit(l, i)
                    width = unit_width(l, MIX_UNITS[i])
                else:
                    su, _ = expert_unit(l, 0, i - NMIX)
                    width = UNIT
                slot = su % RING
                dve.wait_ge(s_hi, su + 1)
                tt(wlo[:, slot, 0:width], stage[:, slot, 0:width], whi[:, slot, 0:width], ALU.subtract).then_inc(s_lo, 1)

            link(nc.vector.memset(small[:, 60:61], EPS))
            nc.vector.memset(small[:, 61:62], 0.0).then_inc(*now("eps_set"))
            for l in range(DEPTH):
                for i in range(2):
                    dve.wait_ge(*after("filt_mm", l, i))
                    if i == 0:
                        dve.wait_ge(*after("filter_loaded", l, 5))
                        if l > 0:
                            dve.wait_ge(*after("filt_spec", l - 1, 1))
                    else:
                        dve.wait_ge(*after("filt_sin", l, 0))
                    w = slice(0, HID)
                    bcol = col(l, "b1" if i == 0 else "b2")[w]
                    link(ts(fa[w, :], ps[i][w, 0:256], bcol, col(l, "freq")[w], ALU.add, ALU.mult))
                    link(ts(fk[w, :], fa[w, :], float(1 / (2 * np.pi)), ROUND, ALU.mult, ALU.add))
                    link(ts(fk[w, :], fk[w, :], ROUND, None, ALU.subtract))
                    link(stt(fa[w, :], fk[w, :], -TWO_PI_HI, fa[w, :], ALU.mult, ALU.add))
                    link(stt(fa[w, :], fk[w, :], -TWO_PI_LO, fa[w, :], ALU.mult, ALU.add))
                    ts(fr_[w, :], fa[w, :], 3.1415925, -3.1415925, ALU.min, ALU.max).then_inc(*now("filt_arg", l, i))
                link(nc.vector.memset(fh[HID:HID + 1, 1, :], 1.0))
                stt(dec[0:1, :], dec[0:1, :], -1.0, dec[0:1, :], ALU.mult, ALU.max).then_inc(*now("decay_abs", l))
                for c in range(2):
                    dve.wait_ge(*after("filt_decay", l, c))
                    tt(kf[:, c, :], ps[2 + c][:, :], decay[:, c, :], ALU.mult).then_inc(*now("filt_k", l, c))
                dve.wait_ge(*after("filt_ssq", l))
                ts(krs[:, :], ps[0][:, 0:256], EPS, None, ALU.add).then_inc(*now("filt_eps", l))
                dve.wait_ge(*after("filt_root", l))
                link(nc.vector.reciprocal(krs[:, :], krs[:, :]))
                for c in range(2):
                    for d in range(2):
                        link(stt(kf[:, c, d * HY:d * HY + HY], kf[:, c, d * HY:d * HY + HY], 1.0 / 256, krs[:, :], ALU.mult, ALU.mult))
                link(ts(kf[0:1, 0, HY:2 * HY], kf[0:1, 0, HY:2 * HY], 0.0, None, ALU.mult))
                for c in range(2):
                    link(tt(kab[:, 0, c, :], kf[:, c, 0:HY], kf[:, c, HY:2 * HY], ALU.add))
                    last = tt(kab[:, 1, c, :], kf[:, c, HY:2 * HY], kf[:, c, 0:HY], ALU.subtract)
                    if c == 0:
                        link(last)
                last.then_inc(*now("filt_ab", l))
                for fch in range(2):
                    dve.wait_ge(*after("filt_spec", l, fch))
                    nc.vector.tensor_copy(kfilt[:, l, :, fch, :], ps[6 + fch][:, :].rearrange("p (r c) -> p r c", r=2)
                                          ).then_inc(*now("filt_copied", l, fch))

            for l in range(DEPTH):
                n = T if l == 0 else LX

                dve.wait_ge(s_mod, (l + 1) * NMOD)
                a, b_ = COLS["bmod"]
                link(tt(modc[:].rearrange("p a b -> p (a b)"), ps[0][:, 0:96], cols[:, l, a:b_], ALU.add))
                for w, (name, at) in enumerate((("g1", 8), ("g2", 32))):
                    link(stt(gs[:, w].rearrange("p a b -> p (a b)"), modc[:, at:at + 8, :].rearrange("p a b -> p (a b)"), 1.0,
                             col(l, name), ALU.add, ALU.mult))

                def normed(which):
                    m = T if which == 0 else n
                    dve.wait_ge(*after("x_root", l, which))
                    link(nc.vector.reciprocal(rstd[:, 0:m], rstd[:, 0:m]))
                    for k in range(KD):
                        if which == 1 and k >= 2:
                            dve.wait_ge(*after("logits", l, k - 2))
                        link(tt(hf[:, k % 2, 0:m], xT[:, k, 0:m], rstd[:, 0:m], ALU.mult))
                        for st in range(m // 256):
                            c = slice(st * 256, st * 256 + 256)
                            last = ts(hf[:, k % 2, c], hf[:, k % 2, c], gs[:, which, k, st:st + 1],
                                      modc[:, 24 * which + k, st:st + 1], ALU.mult, ALU.add)
                            if st < m // 256 - 1:
                                link(last)
                        if which == 1:
                            last.then_inc(*now("hf_ready", l, k))
                            dve.wait_ge(*after("hf_ready", l, k))
                        else:
                            link(last)
                        link(nc.vector.tensor_copy(h[:, k, 0, 0:m], hf[:, k % 2, 0:m]))
                        tt(h[:, k, 1, 0:m], hf[:, k % 2, 0:m], h[:, k, 0, 0:m], ALU.subtract).then_inc(*now("h_ready", l, which, k))
                        dve.wait_ge(*after("h_ready", l, which, k))

                normed(0)
                split(l, 0)
                split(l, 1)
                split(l, 2)

                def low_norm(src, r, gname, dst, nk, m, done):
                    link(nc.vector.reciprocal(r, r))
                    for k in range(nk):
                        link(stt(src[:, k, 0:m], src[:, k, 0:m], col(l, gname)[:, k:k + 1], r, ALU.mult, ALU.mult))
                        link(nc.vector.tensor_copy(dst[:, k, 0, 0:m], src[:, k, 0:m]))
                        last = tt(dst[:, k, 1, 0:m], src[:, k, 0:m], dst[:, k, 0, 0:m], ALU.subtract)
                        if k < nk - 1:
                            link(last)
                    last.then_inc(*now(done, l))
                    dve.wait_ge(*after(done, l))

                dve.wait_ge(*after("q_low_root", l))
                dve.wait_ge(*after("q_low_copied", l, 2))
                low_norm(pq, rq[:, 0, 0:n], "gqa", qn, 3, n, "qn_ready")
                dve.wait_ge(*after("kv_low_root", l))
                low_norm(pkv, rq[:, 1, :], "gkva", kvn, 2, T, "kvn_ready")
                split(l, 3)
                split(l, 4)

                ntile = 4 if l == 0 else 2

                def head_norms(i):
                    b = i % 2
                    for which, (x, m, root, copied, g) in enumerate((
                            (qh, n, "q_root", "q_copied", "gqn"), (kh, T, "k_root", "kr_placed", "gkn"))):
                        dve.wait_ge(*after(root, l, i))
                        dve.wait_ge(*after(("q_squared", "k_squared")[which], l, i))
                        dve.wait_ge(*after(copied, l, i))
                        link(nc.vector.reciprocal(rq[0:QK, which, 0:m], rq[0:QK, which, 0:m]))
                        stt(x[0:QK, b, 0:m], x[0:QK, b, 0:m], col(l, g)[0:QK], rq[0:QK, which, 0:m],
                            ALU.mult, ALU.mult).then_inc(*now(("q_normed", "k_normed")[which], l, i))

                def head_ropes(i):
                    b = i % 2
                    for which, (x, name) in enumerate(((qh, "q"), (kh, "k"))):
                        dve.wait_ge(*after(name + "_rot", l, i))
                        dve.wait_ge(*after(name + "_sum", l, i))
                        link(tt(x[0:QK, b, 0:LX], x[0:QK, b, 0:LX], rope[:, 0, :], ALU.mult))
                        link(tt(tmp[0:QK, which, 0:LX], ps[which][0:QK, 0:LX], rope[:, 1, :], ALU.mult))
                        tt(x[0:QK, b, 0:LX], x[0:QK, b, 0:LX], tmp[0:QK, which, 0:LX], ALU.add).then_inc(*now(name + "_roped", l, i))

                def maxes(i, t):
                    seq = i * ntile + t
                    nk = T if t < 2 else LC
                    s2 = 4 * (seq % 2)
                    dve.wait_ge(*after("scores", l, seq))
                    if seq >= 2:
                        dve.wait_ge(*after("prob_ready", l, seq - 2))
                    nc.vector.tensor_reduce(small[:, s2 + 2:s2 + 3], ps[4 + seq % 2][:, 0:nk], AX.X, ALU.max).then_inc(*now("max_raw", l, seq))
                    dve.wait_ge(*after("max_raw", l, seq))
                    ts(small[:, s2:s2 + 1], small[:, s2 + 2:s2 + 3], -SCALE, None, ALU.mult).then_inc(*now("max_ready", l, seq))

                def normalised(i, t):
                    seq = i * ntile + t
                    nk = T if t < 2 else LC
                    s2 = 4 * (seq % 2)
                    dve.wait_ge(*after("exp_done", l, seq))
                    link(nc.vector.reciprocal(small[:, s2 + 3:s2 + 4], small[:, s2 + 1:s2 + 2]))
                    ts(prob[:, seq % 2, 0:nk], prob[:, seq % 2, 0:nk], small[:, s2 + 3:s2 + 4], None,
                       ALU.mult).then_inc(*now("prob_ready", l, seq))

                def head_out(i, g):
                    r = slice((i % 2) * VD, (i % 2) * VD + VD)
                    seq = i * (ntile // 2) + g
                    c = slice(g * 256, g * 256 + 256)
                    dve.wait_ge(*after("pv", l, seq))
                    link(nc.vector.tensor_copy(aT[r, i // 2, 0, c], ps[7][r, 0:256]))
                    tt(aT[r, i // 2, 1, c], ps[7][r, 0:256], aT[r, i // 2, 0, c], ALU.subtract).then_inc(*now("a_done", l, seq))

                dve.wait_ge(*after("const_loaded", 9))
                for i in range(HEADS + 1):
                    if i > 0:
                        maxes(i - 1, 0)
                        maxes(i - 1, 1)
                        normalised(i - 1, 0)
                        normalised(i - 1, 1)
                    if i < HEADS:
                        head_norms(i)
                    if i > 0 and l == 0:
                        maxes(i - 1, 2)
                        maxes(i - 1, 3)
                    if i < HEADS:
                        pass
                    if i > 0:
                        head_out(i - 1, 0)
                    if i < HEADS:
                        head_ropes(i)
                    if i > 0 and l == 0:
                        normalised(i - 1, 2)
                        normalised(i - 1, 3)
                        head_out(i - 1, 1)

                split(l, 5)
                split(l, 6)
                ns = n // 256
                dve.wait_ge(*after("v_copied", l, 3))
                dve.wait_ge(*after("pv", l, HEADS * (ntile // 2) - 1))
                for b in range(2):
                    for e in (0, 257):
                        last = nc.vector.memset(pad[:, b, :, e:e + 1], 0.0)
                        if (b, e) != (1, 257):
                            link(last)
                last.then_inc(*now("pads_zero", l))
                cw, cbias = col(l, "convw"), col(l, "convb")
                for c in range(6):
                    dve.wait_ge(*after("pad_copied", l, c))
                    zz = z[:, c, 0:n].rearrange("p (s t) -> p s t", t=256)
                    p = pad[:, c % 2, 0:ns]
                    link(ts(zz, p[:, :, 0:256], cw[:, c:c + 1], cbias[:, c:c + 1], ALU.mult, ALU.add))
                    link(stt(zz, p[:, :, 1:257], cw[:, 6 + c:7 + c], zz, ALU.mult, ALU.add))
                    stt(zz, p[:, :, 2:258], cw[:, 12 + c:13 + c], zz, ALU.mult, ALU.add).then_inc(*now("conv_done", l, c))
                    dve.wait_ge(*after("conv_done", l, c))
                    if c == 1:
                        split(l, 7)
                    if c == 3:
                        split(l, 8)
                    if c == 5:
                        split(l, 9)
                tt(z[:, 2:4, 0:n], z[:, 2:4, 0:n], z[:, 4:6, 0:n], ALU.mult).then_inc(*now("u_ready", l))
                for st in range(ns):
                    cs = slice(st * 256, st * 256 + 256)
                    dve.wait_ge(*after("U_copied", l, st))
                    if st > 0:
                        dve.wait_ge(*after("y_back", l, st - 1))
                    K = kfilt[:, l]
                    link(tt(Y[:, 0], U[:, 0], K[:, 0], ALU.mult))
                    link(tt(hyt[:, 0], U[:, 1], K[:, 1], ALU.mult))
                    link(tt(Y[:, 0], Y[:, 0], hyt[:, 0], ALU.add))
                    link(tt(Y[:, 1], U[:, 1], K[:, 0], ALU.mult))
                    link(tt(hyt[:, 1], U[:, 0], K[:, 1], ALU.mult))
                    tt(Y[:, 1], Y[:, 1], hyt[:, 1], ALU.subtract).then_inc(*now("Y_ready", l, st))
                    dve.wait_ge(*after("y_back", l, st))
                    dve.wait_ge(*after("u_ready", l))
                    for c in range(2):
                        link(stt(hyb[:, c, :], z[:, 2 + c, cs], col(l, "hybias")[:, c:c + 1], ps[3][:, c * 256:c * 256 + 256],
                                 ALU.mult, ALU.add))
                        link(tt(hyb[:, c, :], hyb[:, c, :], z[:, c, cs], ALU.mult))
                        link(nc.vector.tensor_copy(bT[:, c, 0, cs], hyb[:, c, :]))
                        last = tt(bT[:, c, 1, cs], hyb[:, c, :], bT[:, c, 0, cs], ALU.subtract)
                        if c == 0:
                            link(last)
                    last.then_inc(*now("b_done", l, st))
                    dve.wait_ge(*after("b_done", l, st))

                dve.wait_ge(*after("gv_root", l))
                link(nc.vector.reciprocal(grs[:, 0:n], grs[:, 0:n]))
                for c in range(2):
                    last = stt(vn[:, c, 0:n], gl[:, 2 + c, 0:n], col(l, "gmg")[:, c:c + 1], grs[:, 0:n], ALU.mult, ALU.mult)
                    if c == 0:
                        link(last)
                last.then_inc(*now("gv_normed", l))
                for c in range(2):
                    dve.wait_ge(*after("gm_spatial", l, 2 * c + 1))
                    link(tt(gmt[:, c, 0:n], gl[:, c, 0:n], ps[4 + c][:, 0:n], ALU.mult))
                    link(nc.vector.tensor_copy(mT[:, c, 0, 0:n], gmt[:, c, 0:n]))
                    tt(mT[:, c, 1, 0:n], gmt[:, c, 0:n], mT[:, c, 0, 0:n], ALU.subtract).then_inc(*now("m_done", l, c))

                chunk = 0
                for half in range(2):
                    y = ylo4 if half == 0 else yhi4
                    chunk += 12
                    for b in range(3):
                        split(l, 10 + 4 * half + b)
                        for j in range(4):
                            dve.wait_ge(*after("merge_evac", l, chunk))
                            chunk += 1
                            g = half * 12 + b * 4 + j
                            tt(br[:, b, j, 0:n], br[:, b, j, 0:n], sig[:, g % 2, 0:n], ALU.mult).then_inc(*now("gated", l, g))
                            if b == 2:
                                dve.wait_ge(*after("gated", l, g))
                                link(tt(br[:, 0, j, 0:n], br[:, 0, j, 0:n], br[:, 1, j, 0:n], ALU.add))
                                link(tt(br[:, 0, j, 0:n], br[:, 0, j, 0:n], br[:, 2, j, 0:n], ALU.add))
                                link(nc.vector.tensor_copy(y[:, j, 0, 0:n], br[:, 0, j, 0:n]))
                                tt(y[:, j, 1, 0:n], br[:, 0, j, 0:n], y[:, j, 0, 0:n], ALU.subtract).then_inc(*now("y_ready", l, 4 * half + j))
                    split(l, 13 + 4 * half)
                split(l, 18)
                for c in range(8):
                    dve.wait_ge(*after("out_mm", l, c))
                    for st in range(ns):
                        cs = slice(st * 256, st * 256 + 256)
                        last = stt(xT[:, c, cs], ps[(48 + c) % 4][:, cs], modc[:, 16 + c, st:st + 1], xT[:, c, cs], ALU.mult, ALU.add)
                        if st < ns - 1:
                            link(last)
                    last.then_inc(*now("x_mixed", l, c))

                dve.wait_ge(*after("x_mixed", l, 7))
                normed(1)
                split(l, 19)
                dve.wait_ge(*after("logits", l, 7))
                dve.wait_ge(*after("y_ready", l, 7))
                nc.vector.tensor_copy(lgT[0:NE, 0:n], ps[0][0:NE, 0:n]).then_inc(*now("logits_copied", l))
                m4 = n // P
                W = NE * m4

                def rv(a, w=16):
                    return rt[:, a:a + w * m4].rearrange("p (t e) -> p t e", t=m4)

                aff, sel = rv(0), rv(64)
                hi1, lo1, hi2, lo2, gsc = rv(128, 4), rv(144, 4), rv(160, 4), rv(176, 4), rv(192, 4)
                gmax, comb = rv(208, 1), rv(256)
                msk, pick = rv(320), rv(384)
                pick2 = rv(448)
                dve.wait_ge(*after("aff", l))
                rbb = rb[:].unsqueeze(1).to_broadcast([P, m4, NE])
                link(tt(sel, aff, rbb, ALU.add))
                s4 = sel.rearrange("p t (g j) -> p t g j", g=4)
                link(tt(hi1, s4[:, :, :, 0], s4[:, :, :, 1], ALU.max))
                link(tt(lo1, s4[:, :, :, 0], s4[:, :, :, 1], ALU.min))
                link(tt(hi2, s4[:, :, :, 2], s4[:, :, :, 3], ALU.max))
                link(tt(lo2, s4[:, :, :, 2], s4[:, :, :, 3], ALU.min))
                link(tt(gsc, hi1, hi2, ALU.max))
                link(tt(hi1, hi1, hi2, ALU.min))
                link(tt(lo1, lo1, lo2, ALU.max))
                link(tt(hi1, hi1, lo1, ALU.max))
                link(tt(gsc, gsc, hi1, ALU.add))

                def first_max(dst, src, w, orders):
                    link(nc.vector.tensor_reduce(gmax, src, AX.X, ALU.max))
                    link(tt(dst, src, gmax.to_broadcast([P, m4, w]), ALU.is_equal))
                    link(tt(dst, dst, orders.unsqueeze(1).to_broadcast([P, m4, w]), ALU.mult))
                    link(nc.vector.tensor_reduce(gmax, dst, AX.X, ALU.max))
                    link(tt(dst, dst, gmax.to_broadcast([P, m4, w]), ALU.is_equal))

                first_max(hi2, gsc, 4, order[:, 0:4])
                m4v = msk.rearrange("p t (g j) -> p t g j", g=4)
                g4 = hi2.unsqueeze(3).to_broadcast([P, m4, 4, 4])
                link(tt(m4v, s4, g4, ALU.mult))
                link(ts(hi2, hi2, BIG, -BIG, ALU.mult, ALU.add))
                link(tt(m4v, m4v, g4, ALU.add))
                first_max(pick, msk, NE, order[:, 4:4 + NE])
                link(stt(msk, pick, -2 * BIG, msk, ALU.mult, ALU.add))
                first_max(pick2, msk, NE, order[:, 4:4 + NE])
                link(tt(pick, pick, pick2, ALU.add))
                link(tt(pick, pick, aff, ALU.mult))
                link(nc.vector.tensor_reduce(gmax, pick, AX.X, ALU.add))
                link(nc.vector.reciprocal(gmax, gmax))
                tt(comb, pick, gmax.to_broadcast([P, m4, NE]), ALU.mult).then_inc(*now("comb", l))
                dve.wait_ge(*after("comb_turned", l))
                cf = lgT[0:NE, 0:n]
                link(nc.vector.tensor_copy(combT[0:NE, 0, 0:n], ps[3][0:NE, 0:n]))
                link(tt(cf, ps[3][0:NE, 0:n], combT[0:NE, 0, 0:n], ALU.subtract))
                link(nc.vector.tensor_copy(combT[0:NE, 1, 0:n], cf))
                link(tt(cf, cf, combT[0:NE, 1, 0:n], ALU.subtract))
                nc.vector.tensor_copy(combT[0:NE, 2, 0:n], cf).then_inc(*now("comb_split", l))

                up_mm, wgt = sem_of(f"expert_up_mm{l}"), sem_of(f"gate_weighted{l}")
                up_used, hid_hi, hid_s = sem_of(f"up_used{l}"), sem_of(f"hidden_hi{l}"), sem_of(f"hidden_split{l}")
                down_mm, down_ev = sem_of(f"expert_down_mm{l}"), sem_of(f"down_added{l}")
                su0, _ = expert_unit(l, 0, 0)
                added = sem_of("moe_half_added")

                def split_expert(e, i, off):
                    dve.wait_ge(s_hi, e * 3 + (su0 + i + 3 * off + 1))
                    tt(wlo[:, i, :], stage[:, i, :], whi[:, i, :], ALU.subtract).then_inc(s_lo, 1)

                def expert(e, first=False, last=False):
                    split_expert(e, 2, 0)
                    if not last:
                        split_expert(e, 0, 1)
                    for i in range(KF):
                        dve.wait_ge(up_mm, e * KF + (i + 1))
                        dve.wait_ge(wgt, e * KF + (i + 1))
                        if not first:
                            dve.wait_ge(hid_s, e * KF + (i + 1 - KF))
                        tt(th[:, i, 0:n], ps[4 + i][:, 0:n], sg[:, i, 0:n], ALU.mult).then_inc(up_used, 1)
                    for i in range(KF):
                        dve.wait_ge(hid_hi, e * KF + (i + 1))
                        tt(hid[:, i, 1, 0:n], th[:, i, 0:n], hid[:, i, 0, 0:n], ALU.subtract).then_inc(hid_s, 1)
                    if not last:
                        split_expert(e, 1, 1)
                    for j in range(8):
                        dve.wait_ge(down_mm, e * 8 + (j + 1))
                        if not first:
                            dve.wait_ge(down_ev, e * 8 + (j + 1 - 8))
                        for st in range(ns):
                            cs = slice(st * 256, st * 256 + 256)
                            q = stt(xT[:, j, cs], ps[j][:, cs], modc[:, 40 + j, st:st + 1], xT[:, j, cs], ALU.mult, ALU.add)
                        q.then_inc(down_ev, 1)

                dve.wait_ge(*after("x_mixed", l, 7))
                expert(0, True)
                with dve.Fori(1, NE - 1) as e:
                    expert(e)
                expert(NE - 1, False, True)
                if known is None or True:
                    dve.wait_ge(down_ev, NE * 8)
                    for k in range(8):
                        for which in range(2):
                            nc.vector.memset(small[:, 62:63], 0.0).then_inc(*now("moe_added", l, NE - 1, k, which))
                            dve.wait_ge(*after("moe_added", l, NE - 1, k, which))
            if dump is not None:
                pass

    return found


def host_tables():
    f = np.float32
    t = np.arange(LX, dtype=np.float64)
    fr = np.arange(256, dtype=np.float64)
    k_ang = 2 * np.pi * np.outer(t, fr + 0.5) / 512
    s_ang = 2 * np.pi * np.outer(t + 0.5, fr + 0.5) / 512

    def two(a):
        return np.ascontiguousarray(a.astype(f).reshape(2, P, 256).transpose(1, 0, 2))

    rows = LX // GRID_W
    row = np.repeat(np.arange(rows, dtype=f), GRID_W)
    col = np.tile(np.arange(GRID_W, dtype=f), rows)
    nf = ROPE // 4
    inv = (f(10000.0) ** (-np.arange(nf, dtype=f) / f(nf))).astype(f)
    ang = np.concatenate([row[:, None] * inv, col[:, None] * inv], axis=-1)
    rope = np.zeros((QK, 2, LX), f)
    rope[:NOPE, 0] = 1
    rope[NOPE:, 0] = np.repeat(np.cos(ang).astype(f), 2, axis=1).T
    rope[NOPE:, 1] = np.repeat(np.sin(ang).astype(f), 2, axis=1).T
    rot = np.zeros((QK, QK), f)
    for j in range(NOPE, QK, 2):
        rot[j + 1, j] = -1
        rot[j, j + 1] = 1
    tu = (np.arange(LX, dtype=f) / f(LX - 1)).astype(f)
    bands = np.linspace(1e-4, BANDS - 1, BANDS, dtype=f)
    a = (f(2 * np.pi / LX) * np.arange(LX, dtype=f))[:, None] * bands[None]
    zt = np.concatenate([tu[:, None], np.cos(a), -np.sin(a)], axis=-1).astype(f).T
    esel = np.repeat(np.eye(NE, dtype=f), P, axis=1)
    order = np.tile(np.concatenate([np.arange(4, 0, -1), np.arange(NE, 0, -1)]).astype(f), (P, 1))
    return {"cosk": two(np.cos(k_ang)), "sink": two(np.sin(k_ang)), "cos_s": two(np.cos(s_ang)), "sin_s": two(np.sin(s_ang)),
            "rope": rope, "rot": rot, "zT": np.ascontiguousarray(zt), "tneg": -tu[None], "esel": esel,
            "order": order, "ident": np.eye(P, dtype=f), "ones": np.ones((P, P), f)}


def host_layout(a):
    f = np.float32

    def chunks(v):
        v = np.asarray(v)
        return np.moveaxis(v.reshape(*v.shape[:-1], -1, P), -1, 0)

    def short(v):
        o = np.zeros((P, 1), f)
        o[:v.shape[0], 0] = v
        return o

    cols = np.zeros((P, DEPTH, NCOLS), f)
    for l in range(DEPTH):
        def put(name, v):
            s, e = COLS[name]
            cols[:, l, s:e] = v.reshape(P, e - s)

        put("g1", np.repeat(chunks(a["norm1_g"][l]), 2, axis=1))
        put("g2", np.repeat(chunks(a["norm2_g"][l]), 2, axis=1))
        put("bmod", np.repeat(chunks(a["b_mod"][l]), 2, axis=1))
        put("gqa", chunks(a["g_qa"][l]))
        put("gkva", chunks(a["g_kva"][l]))
        put("gqn", short(a["g_qn"][l]))
        put("gkn", short(a["g_kn"][l]))
        put("convw", chunks(a["hy_conv_w"][l]))
        put("convb", chunks(a["hy_conv_b"][l]))
        put("hybias", chunks(a["hy_bias"][l]))
        put("gmg", chunks(a["gm_norm_g"][l]))
        put("b1", short(a["hy_b1"][l]))
        put("b2", short(a["hy_b2"][l]))
        put("freq", short(a["hy_freq"][l]))
    fw = np.zeros((DEPTH, P, FW), f)
    fw[:, :EMB, 0:HID] = a["hy_w1"]
    fw[:, :HID, HID:2 * HID] = a["hy_w2"]
    fw[:, :HID, 2 * HID:] = a["hy_w3"]
    fw[:, HID, 2 * HID:] = a["hy_b3"]
    c = np.ascontiguousarray
    return {
        "cT": c(np.stack([chunks(a["c"][0]), chunks(a["c_ctx"])], axis=-1)),
        "cols": cols, "fw": fw, "decay": c(a["hy_decay"].reshape(DEPTH, 2 * HY)),
        "xT": c(a["x"][0].T.reshape(KD, P, LX).transpose(1, 0, 2)),
        "ctxT": c(a["ctx"][0].T.reshape(KD, P, LC).transpose(1, 0, 2)),
        "rw": c(a["router_w"].reshape(KD, P, NE).transpose(1, 0, 2)),
        "rb": c(np.broadcast_to(a["router_b"], (P, NE))),
        "ws": c(a["gm_ws"].transpose(0, 3, 1, 2)), "bs": c(a["gm_bs"].reshape(DEPTH, GROUPS * P)),
        **{k: a[k] for k in ("w_mod", "w_in", "w_uq", "w_ukv", "w_pa", "w_pb", "w_pc", "w_out",
                             "moe_w_gate", "moe_w_up", "moe_w_down")},
    }


def kernel(**inputs):
    import concourse.bacc as bacc
    from concourse.bass_utils import run_bass_kernel_spmd

    a = {k: np.asarray(v) for k, v in inputs.items()}
    arrays = host_layout(a)
    arrays.update(host_tables())
    arrays["esel"] = arrays["esel"].astype(mybir.dt.np(BF16))

    def program(known):
        nc = bacc.Bacc("TRN2", target_bir_lowering=False, num_devices=1)
        ins = {k: nc.dram_tensor(f"in_{k}", v.shape, mybir.dt.from_np(v.dtype), kind="ExternalInput").ap()
               for k, v in arrays.items()}
        out = nc.dram_tensor("out_xT", (P, KD, LX), F32, kind="ExternalOutput").ap()
        return nc, build(nc, ins, out, known)

    _, known = program(None)
    nc, _ = program(known)
    r = run_bass_kernel_spmd(nc, [{f"in_{k}": v for k, v in arrays.items()}], core_ids=[0])
    o = r.results[0]["out_xT"]
    return np.ascontiguousarray(o.transpose(2, 1, 0).reshape(1, LX, D))
```

```python
from contextlib import ExitStack

import numpy as np

import concourse.bass as bass
from concourse import mybir

F32 = mybir.dt.float32
BF16 = mybir.dt.bfloat16
ALU = mybir.AluOpType
ACT = mybir.ActivationFunctionType
AX = mybir.AxisListType

P = 128
D = 1024
KD = D // P
DEPTH = 2
LX = 256
LC = 256
T = LX + LC
GRID_W = 64
EPS = 1e-6
HEADS, NOPE, ROPE, VD = 8, 64, 32, 64
QK = NOPE + ROPE
QR, KVR = 384, 256
HY = 256
BANDS = 16
EMB = 1 + 2 * BANDS
HID = 64
GM = 256
GROUPS = 4
OFF_KV = QR
OFF_HY = QR + KVR + ROPE
OFF_GM = OFF_HY + 3 * HY
OFF_GT = OFF_GM + 2 * GM
NE, FE = 16, 512
KF = FE // P
SCALE = float(QK) ** -0.5
UNIT = 4096
RING = 3
MOD_BEFORE = 3
BIG = 1e30
SLOTS = P
SPARE = 3 * NE
MORE = 2 * T // SLOTS - 1
TABLES = {}
_at = 0
for _name, _n in (("groups", 4), ("experts", NE), ("iota", SLOTS), ("limit", SPARE), ("row", SPARE),
                  ("expert_of", SPARE), ("count", MORE)):
    TABLES[_name] = (_at, _at + _n)
    _at += _n
NTABLE = _at
ROUND = 12582912.0
TWO_PI_HI = 6.28125
TWO_PI_LO = float(np.float32(2 * np.pi - 6.28125))

COLS = {}
_at = 0
for _name, _n in (("g1", 16), ("g2", 16), ("bmod", 96), ("gqa", 3), ("gkva", 2), ("gqn", 1), ("gkn", 1),
                  ("convw", 18), ("convb", 6), ("hybias", 2), ("gmg", 2), ("b1", 1), ("b2", 1), ("freq", 1)):
    COLS[_name] = (_at, _at + _n)
    _at += _n
NCOLS = _at
FW = 2 * HID + 2 * HY

MIX_UNITS = ["q", "kv", "uq", "ukv", "hy0", "hy1", "hy2", "gm", "p0", "gt00", "gt01", "gt02",
             "p1", "gt10", "gt11", "gt12", "out0", "out1"]
NMOD = 12
NMIX = len(MIX_UNITS)
NEXP = 3 * NE
SEQ = ([("mod", g) for g in range(4)] + [("mix", i) for i in range(5)] + [("mod", g) for g in range(4, NMOD)]
       + [("mix", i) for i in range(5, NMIX)])
NSPLIT = NMIX + 2 * NE


def build(nc, ins, out, known, dump=None):
    counts, found = {}, {}
    ctx = ExitStack()
    with ctx:
        def sb(name, shape, dt=F32):
            return ctx.enter_context(nc.sbuf_tensor(name, shape, dt))

        stage = sb("stage", [P, RING, UNIT])
        whi = sb("whi", [P, RING, UNIT], BF16)
        wlo = sb("wlo", [P, RING, UNIT], BF16)
        xT = sb("xT", [P, KD, T])
        h = sb("h", [P, KD, 2, T], BF16)
        cos_s = sb("cos_s", [P, 2, 256])
        sin_s = sb("sin_s", [P, 2, 256])
        ident = sb("ident", [P, P])
        ones = sb("ones", [P, P])
        rope = sb("rope", [QK, 2, LX])
        rot = sb("rot", [QK, QK])
        rw = sb("rw", [P, KD, NE])
        rb = sb("rb", [P, NE])
        tables = sb("tables", [P, NTABLE])
        halves = sb("halves", [P, 3, P], BF16)
        cols = sb("cols", [P, DEPTH, NCOLS])
        cT = sb("cT", [P, KD, 2])
        modc = sb("modc", [P, 48, 2])
        gs = sb("gs", [P, 2, KD, 2])
        ws = sb("ws", [P, GROUPS, P])
        bs = sb("bs", [1, GROUPS * P])
        kfilt = sb("kfilt", [P, DEPTH, 2, 2, HY])
        small = sb("small", [P, 64])
        arena = sb("arena", [P, 52 * 256])
        ps = [ctx.enter_context(nc.psum_tensor(f"bank{i}", [P, 512], F32)) for i in range(8)]

        def kb(a, b):
            return arena[:, a * 256:b * 256]

        def pair(a, n):
            return kb(a, a + 2 * n).bitcast(BF16).rearrange("p (c s t) -> p c s t", c=n, s=2)

        def f32v(a, b, **dims):
            n = list(dims.values())
            if len(n) == 1:
                return kb(a, b).rearrange("p (a t) -> p a t", a=n[0])
            return kb(a, b).rearrange("p (a b t) -> p a b t", a=n[0], b=n[1])

        aT, bT, mT = pair(0, 4), pair(8, 2), pair(12, 2)
        sq, rstd, hf = f32v(16, 20, n=2), kb(20, 22), f32v(22, 26, n=2)
        pT, tmp = f32v(8, 12, n=4), f32v(12, 16, n=2)
        qn, kvn = pair(16, 3), pair(22, 2)
        kr, V = kb(26, 28), f32v(28, 36, n=4)
        qh, kh = f32v(36, 40, n=2), f32v(40, 44, n=2)
        prob = f32v(44, 48, n=2)
        rq = f32v(48, 52, n=2)
        pq, pkv = f32v(36, 42, n=3), f32v(44, 48, n=2)
        z = f32v(16, 28, n=6)
        pad = arena[:, 28 * 256:28 * 256 + 2 * 2 * 258].rearrange("p (b s t) -> p b s t", b=2, s=2)
        uR, U, Y = f32v(33, 35, n=2), f32v(35, 39, n=2, m=2), f32v(39, 43, n=2, m=2)
        hyt = f32v(43, 47, n=2, m=2)
        hyb = f32v(47, 49, n=2)
        gl, gsq, grs = f32v(16, 24, n=4), f32v(24, 28, n=2), kb(28, 30)
        vn, vR = f32v(30, 34, n=2), f32v(34, 38, n=4)
        gmt = f32v(38, 42, n=2)
        br, sig = f32v(16, 40, n=3, m=4), f32v(40, 44, n=2)
        ylo4, yhi4 = pair(44, 4), pair(0, 4)
        hR = kb(0, 16).bitcast(BF16).rearrange("p (t s c) -> p t s c", t=4, s=2)
        he = kb(16, 20).bitcast(BF16).rearrange("p (k s t) -> p k s t", k=KD, s=2)
        sel = kb(20, 21).bitcast(BF16).rearrange("p (t s) -> p t s", t=4)
        selT = kb(21, 22).bitcast(BF16)
        sg, hid = kb(22, 24), kb(24, 26)
        yR = kb(28, 32).bitcast(BF16).rearrange("p (s c) -> p s c", s=2)
        rank = kb(32, 33)
        comb3, pickh = kb(33, 34).bitcast(BF16)[:, 0:NE * 4 * 3], kb(34, 35).bitcast(BF16)[:, 0:4 * NE]
        csum = kb(35, 36)[:, 0:1]
        spare_list = kb(36, 37).bitcast(mybir.dt.int32)
        flagA, flagB, hits = kb(37, 38)[:, 0:32 + SPARE], kb(38, 39)[:, 0:32 + SPARE], kb(39, 41)[:, 0:MORE * SPARE]
        lgT, rt = kb(44, 46), kb(46, 48)
        fw = kb(16, 19)[:, 0:FW]
        zT, tneg = kb(19, 20), kb(20, 21)
        cosk, sink = f32v(21, 23, n=2), f32v(23, 25, n=2)
        fa, fk, fr_, fh = kb(25, 26), kb(26, 27), kb(27, 28), f32v(28, 30, n=2)
        dec, decay, kf = kb(30, 32), f32v(32, 36, n=2), f32v(36, 40, n=2)
        ksq, krs, kab = f32v(40, 44, n=2), kb(44, 45), f32v(45, 49, n=2, m=2)

        sems = {}

        def sem_of(kind):
            if kind not in sems:
                sems[kind] = ctx.enter_context(nc.semaphore(kind))
            return sems[kind]

        def now(kind, *which, by=1):
            counts[kind] = counts.get(kind, 0) + by
            assert (kind, *which) not in found, (kind, which)
            found[(kind, *which)] = counts[kind]
            return sem_of(kind), by

        def after(kind, *which):
            if known is None:
                return sem_of(kind), 1
            return sem_of(kind), known[(kind, *which)]

        s_stage = [sem_of(f"stage_loaded{i}") for i in range(RING)]
        s_hi, s_lo, s_used = sem_of("hi_split"), sem_of("lo_split"), sem_of("unit_used")
        s_mod = sem_of("mod_unit_used")

        def dma_unit(l, i):
            return l * (NMOD + NMIX + NEXP) + i

        def where(i):
            return SEQ.index(("mix", i)) if i < NMIX else NMOD + i

        def mix_unit(l, i):
            return l * NSPLIT + i, dma_unit(l, where(i))

        def expert_unit(l, e, i):
            return l * NSPLIT + NMIX + 2 * e + i, dma_unit(l, NMOD + NMIX + 3 * e + i)

        def col(l, name):
            a, b = COLS[name]
            return cols[:, l, a:b]

        def unit_source(l, name):
            w = ins["w_in"][l]
            if name == "q":
                return [(0, 8 * QR, w[:, 0:QR], 8)]
            if name == "kv":
                return [(0, 8 * (KVR + ROPE), w[:, OFF_KV:OFF_HY], 8)]
            if name == "uq":
                return [(0, 3 * HEADS * QK, ins["w_uq"][l], 3)]
            if name == "ukv":
                return [(0, 2 * HEADS * (NOPE + VD), ins["w_ukv"][l], 2)]
            if name[:2] == "hy":
                a = OFF_HY + 256 * int(name[2])
                return [(0, 8 * 256, w[:, a:a + 256], 8)]
            if name == "gm":
                return [(0, UNIT, w[:, OFF_GM:OFF_GT], 8)]
            if name[0] == "p":
                c = slice(512 * int(name[1]), 512 * int(name[1]) + 512)
                return [(0, 2048, ins["w_pa"][l][:, c], 4), (2048, 3072, ins["w_pb"][l][:, c], 2),
                        (3072, 4096, ins["w_pc"][l][:, c], 2)]
            if name[:2] == "gt":
                a = OFF_GT + D * int(name[3]) + 512 * int(name[2])
                return [(0, UNIT, w[:, a:a + 512], 8)]
            return [(0, UNIT, ins["w_out"][l][:, 512 * int(name[3]):512 * int(name[3]) + 512], 8)]

        def unit_width(l, name):
            return max(b for _, b, _, _ in unit_source(l, name))

        block = ctx.enter_context(nc.Block())

        def spare_loaded(l):
            return sem_of(f"spare_loaded{l}")

        def spare_pe(l):
            return sem_of(f"spare_tensor{l}")

        def spare_act(l):
            return sem_of(f"spare_scalar{l}")

        def spare_dve(l):
            return sem_of(f"spare_vector{l}")

        SPARE_PE, SPARE_ACT, SPARE_DVE = 5, 6, 8

        def reached(l, e, per=1, i=0):
            return e * per + (l * NE * per + i + 1)

        X = {k: sem_of("expert_" + k) for k in (
            "tokens_chosen", "gathered", "input_hi", "input_lo", "gate_mm", "up_mm", "gate_silu", "hidden", "choice_turned", "choice_copied", "weight_ready", "down_mm", "result_hi", "result_lo",
            "scattered", "added")}
        ident_h, before_h, ones_h = halves[:, 0, :], halves[:, 1, :], halves[:, 2, :]

        def table(name):
            a, b = TABLES[name]
            return tables[:, a:b]

        @block.sync
        def _(sp):
            for l in range(DEPTH):
                def mod_source(g):
                    return ins["w_mod"][l].rearrange("(k p) (g n) -> g p k n", p=P, n=512)[g]

                for p, (kind, i) in enumerate(SEQ):
                    n = dma_unit(l, p)
                    if p >= RING:
                        k0, i0 = SEQ[p - RING]
                        if k0 == "mod":
                            sp.wait_ge(s_mod, l * NMOD + i0 + 1)
                        else:
                            sp.wait_ge(s_lo, mix_unit(l, i0)[0] + 1)
                    if kind == "mod":
                        sp.dma_start(stage[:, n % RING, :].rearrange("p (k n) -> p k n", k=8),
                                     mod_source(i)).then_inc(s_stage[n % RING], 16)
                        continue
                    name = MIX_UNITS[i]
                    parts = unit_source(l, name)
                    for j, (a, b, src, k) in enumerate(parts):
                        ins_ = sp.dma_start(stage[:, n % RING, a:b].rearrange("p (k n) -> p k n", k=k),
                                            src.rearrange("(k p) n -> p k n", p=P))
                        ins_.then_inc(s_stage[n % RING], 16)
                gate, up, down = (ins[w][l].rearrange("e (k p) n -> e p k n", p=P)
                                  for w in ("moe_w_gate", "moe_w_up", "moe_w_down"))
                su0, _ = expert_unit(l, 0, 0)

                def fetch_expert(e, i, w, k):
                    if isinstance(e, int) and e == 0:
                        sp.wait_ge(s_lo, su0 + i - RING + 1)
                    elif i == 2:
                        sp.wait_ge(X["down_mm"], reached(l, e, 2, -1))
                    else:
                        sp.wait_ge(s_lo, e * 2 + (su0 + i - 1))
                    src = w[e] if isinstance(e, int) else w[bass.ds(e, 1)].rearrange("a p k n -> (a p) k n")
                    sp.dma_start(stage[:, i, :].rearrange("p (k n) -> p k n", k=k), src).then_inc(s_stage[i], 16)

                fetch_expert(0, 0, gate, 8)
                fetch_expert(0, 1, up, 8)
                fetch_expert(0, 2, down, 4)
                fetch_expert(1, 0, gate, 8)
                fetch_expert(1, 1, up, 8)
                with sp.Fori(2, NE) as e:
                    fetch_expert(e, 0, gate, 8)
                    fetch_expert(e - 1, 2, down, 4)
                    fetch_expert(e, 1, up, 8)
                fetch_expert(NE - 1, 2, down, 4)
                sp.wait_ge(s_lo, su0 + 2 * NE)
                sp.wait_ge(X["down_mm"], reached(l, NE - 1, 2, 1))
                sp.wait_ge(*after("spare_listed", l))
                with sp.Fori(0, MORE) as j:
                    row = sp.value_load(spare_list[0:1, bass.ds(j, 1)], min_val=0, max_val=SPARE + NE - 1)
                    e = sp.value_load(spare_list[0:1, bass.ds(j + MORE, 1)], min_val=0, max_val=NE - 1)
                    with sp.If(row > 0):
                        sp.wait_ge(spare_dve(l), j * SPARE_DVE + 1)
                        for i, (w, k) in enumerate(((gate, 8), (up, 8), (down, 4))):
                            sp.dma_start(stage[:, i, :].rearrange("p (k n) -> p k n", k=k),
                                         w[bass.ds(e, 1)].rearrange("a p k n -> (a p) k n")).then_inc(spare_loaded(l), 16)
                sp.wait_ge(*after("moe_added", l))
            for k in range(KD):
                if k % 4 == 0:
                    sp.wait_ge(*after("moe_added", DEPTH - 1))
                    sp.dma_start(out[:, k:k + 4, :], xT[:, k:k + 4, 0:LX]).then_inc(*now("stored", k, by=16))
            sp.wait_ge(*after("stored", 4))

        def landed(l, i):
            n = dma_unit(l, i)
            total = 0
            for m in range(n % RING, n + 1, RING):
                kind, j = SEQ[m % (NMOD + NMIX + NEXP)] if m % (NMOD + NMIX + NEXP) < len(SEQ) else ("expert", 0)
                parts = 3 if kind == "mix" and MIX_UNITS[j][0] == "p" else 1
                total += 16 * parts
            return s_stage[n % RING], total

        @block.gpsimd
        def _(pool):
            for k, (dst, src) in enumerate(((cT[:], ins["cT"]), (cols[:], ins["cols"]),
                                            (ident[:], ins["ident"]), (ones[:], ins["ones"]))):
                pool.dma_start(dst, src).then_inc(*now("small_loaded", k, by=16))
            pool.wait_ge(*after("small_loaded", 3))
            for k, (dst, src) in enumerate((
                    (zT[0:EMB, :], ins["zT"]), (tneg[0:1, :], ins["tneg"]), (cosk, ins["cosk"]),
                    (sink, ins["sink"]), (fw, ins["fw"][0]), (dec[0:1, :], ins["decay"][0:1]))):
                pool.dma_start(dst, src).then_inc(*now("filter_loaded", 0, k, by=16))
            pool.dma_start(xT[:, :, 0:LX], ins["xT"]).then_inc(*now("x_loaded", 0, by=16))
            pool.dma_start(xT[:, :, LX:T], ins["ctxT"]).then_inc(*now("x_loaded", 1, by=16))
            for k, (dst, src) in enumerate((
                    (cos_s[:], ins["cos_s"]), (sin_s[:], ins["sin_s"]), (rope[:], ins["rope"]),
                    (rot[:], ins["rot"]), (rw[:], ins["rw"]), (rb[:], ins["rb"]), (tables[:], ins["tables"]),
                    (halves[:], ins["halves"]), (ws[:], ins["ws"][0]), (bs[:], ins["bs"][0:1]))):
                pool.dma_start(dst, src).then_inc(*now("const_loaded", k, by=16))
            pool.wait_ge(*after("filt_spec", 0, 1))
            pool.dma_start(fw, ins["fw"][1]).then_inc(*now("filter_loaded", 1, 4, by=16))
            pool.dma_start(dec[0:1, :], ins["decay"][1:2]).then_inc(*now("filter_loaded", 1, 5, by=16))
            for l in range(DEPTH):
                if l > 0:
                    pool.wait_ge(*after("gm_spatial", l - 1, 3))
                    pool.dma_start(ws[:], ins["ws"][l]).then_inc(*now("spatial_loaded", l, 0, by=16))
                    pool.dma_start(bs[:], ins["bs"][l:l + 1]).then_inc(*now("spatial_loaded", l, 1, by=16))

        @block.tensor
        def _(pe):
            def mm(o, a, b, start, stop):
                return nc.tensor.matmul(o, a, b, start=start, stop=stop)

            def mm3(o, w, act, first, last):
                mm(o, w[0], act[0], first, False)
                mm(o, w[0], act[1], False, False)
                return mm(o, w[1], act[0], False, last)

            def weights(slot, k, kn, a, b, base=0):
                w = kn
                return (whi[:, slot, base + k * w + a:base + k * w + b], wlo[:, slot, base + k * w + a:base + k * w + b])

            def project(o, slot, width, a, b, n, hn=None, nk=8, base=0, act=None):
                act = h if act is None else act
                for k in range(nk):
                    last = mm3(o, weights(slot, k, width, a, b, base), (act[:, k, 0, 0:n], act[:, k, 1, 0:n]),
                               k == 0, k == nk - 1)
                return last

            def modulation(l, g, m):
                p = SEQ.index(("mod", g))
                if m == 0:
                    pe.wait_ge(*landed(l, p))
                    if g == 0 and l == 0:
                        pe.wait_ge(*after("silu_c"))
                at = g * 8 + m * 2
                o = ps[1][:, at:at + 2] if g < 4 else ps[7][:, 256 + at:258 + at]
                for k in range(KD):
                    last = mm(o, stage[:, p % RING, k * 512 + m * P:k * 512 + m * P + P], cT[:, k, :], k == 0, k == KD - 1)
                if m == 3:
                    last.then_inc(s_mod, 1)

            pe.wait_ge(*after("small_loaded", 3))
            pe.wait_ge(*after("filter_loaded", 0, 5))
            for l in range(DEPTH):
                def modulate(g, half):
                    modulation(0, g, 2 * half)
                    modulation(0, g, 2 * half + 1)

                if l > 0:
                    pe.wait_ge(*after("filter_loaded", l, 5))
                mm(ps[0][0:HID, 0:256], fw[0:EMB, 0:HID], zT[0:EMB, 0:256], True, True).then_inc(*now("filt_mm", l, 0))
                modulate(2 * l, 0)
                pe.wait_ge(*after("filt_sin", l, 0))
                mm(ps[0][0:HID, 256:512], fw[0:HID, HID:2 * HID], fh[0:HID, 0, :], True, True).then_inc(*now("filt_mm", l, 1))
                modulate(2 * l, 1)
                pe.wait_ge(*after("filt_sin", l, 1))
                pe.wait_ge(*after("decay_abs", l))
                for c in range(2):
                    mm(ps[2 + c][:, :], fh[0:HID + 1, 1, c * P:c * P + P], fw[0:HID + 1, 2 * HID:FW], True, True)
                    mm(ps[4 + c][:, :], tneg[0:1, c * P:c * P + P], dec[0:1, :], True, True).then_inc(*now("filt_mm", l, 2 + c))
                modulate(2 * l + 1, 0)
                for c in range(2):
                    pe.wait_ge(*after("filt_sq", l, c))
                    for d in range(2):
                        last = mm(ps[0][:, 0:256], ones[:], ksq[:, c, d * HY:d * HY + HY], c == 0 and d == 0, c == 1 and d == 1)
                last.then_inc(*now("filt_ssq", l))
                modulate(2 * l + 1, 1)
                pe.wait_ge(*after("filt_ab", l))
                for f in range(2):
                    for part, table in ((0, cosk), (1, sink)):
                        if part == 0 and f == 0 and False:
                            pass
                        for c in range(2):
                            last = mm(ps[6 + f][:, part * 256:part * 256 + 256], table[:, c, f * P:f * P + P],
                                      kab[:, part, c, :], c == 0, c == 1)
                    last.then_inc(*now("filt_spec", l, f))

            for l in range(DEPTH):
                n = T if l == 0 else LX
                if l > 0:
                    pe.wait_ge(*after("moe_added", l - 1))
                    for g in range(4):
                        for m in range(4):
                            modulation(l, g, m)

                def norm_sum(which):
                    m = T if which == 0 else n
                    for k in range(KD):
                        if k == 0:
                            pe.wait_ge(*(after("x_mixed", l, 7) if which == 1 else after("mod_added", l, 0)))
                        pe.wait_ge(*after("x_squared", l, which, k))
                        mm(ps[1][:, 0:m], ones[:], sq[:, k % 2, 0:m], k == 0, k == KD - 1).then_inc(*now("x_summed", l, which, k))

                norm_sum(0)
                for k in range(KD):
                    pe.wait_ge(*after("h_ready", l, 0, k))

                def unit(i):
                    su, _ = mix_unit(l, i)
                    pe.wait_ge(s_lo, su + 1)
                    return i % RING

                s = unit(0)
                for m in range(3):
                    last = project(ps[2 + m][:, 0:n], s, QR, m * P, m * P + P, n)
                    last.then_inc(*now("q_low", l, m)) if m < 2 else None
                last.then_inc(s_used, 1)
                mm(ps[0][0:1, 0:1], ones[:, 0:1], ones[:, 0:1], True, True).then_inc(*now("q_low", l, 2))
                s = unit(1)
                for m in range(2):
                    project(ps[5 + m][:, 0:T], s, KVR + ROPE, m * P, m * P + P, T).then_inc(*now("kv_low", l, m))
                o = ps[7][NOPE:QK, 0:T]
                for k in range(8):
                    last = mm3(o, weights(s, k, KVR + ROPE, KVR, KVR + ROPE), (h[:, k, 0, 0:T], h[:, k, 1, 0:T]), k == 0, k == 7)
                last.then_inc(s_used, 1)
                mm(ps[0][0:1, 1:2], ones[:, 0:1], ones[:, 0:1], True, True).then_inc(*now("kv_low", l, 2))
                for m in range(3):
                    pe.wait_ge(*after("q_low_sq", l, m))
                    mm(ps[0][:, 0:n], ones[:], tmp[:, m % 2, 0:n], m == 0, m == 2).then_inc(*now("q_low_sum", l, m))
                for m in range(2):
                    pe.wait_ge(*after("kv_low_sq", l, m))
                    mm(ps[1][:, 0:T], ones[:], tmp[:, (m + 1) % 2, 0:T], m == 0, m == 1).then_inc(*now("kv_low_sum", l, m))

                sq_, skv = unit(2), unit(3)
                pe.wait_ge(*after("kvn_ready", l))
                for tc in range(4):
                    b = 2 + tc
                    for k in range(2):
                        v = [w[:, skv, k * 1024:k * 1024 + 1024].rearrange("p (h c) -> p h c", h=HEADS)[:, :, NOPE:NOPE + VD]
                             for w in (whi, wlo)]
                        c = slice(tc * P, tc * P + P)
                        mm(ps[b][:, :], kvn[:, k, 0, c], v[0], k == 0, False)
                        mm(ps[b][:, :], kvn[:, k, 1, c], v[0], False, False)
                        last = mm(ps[b][:, :], kvn[:, k, 0, c], v[1], False, k == 1)
                    last.then_inc(*now("v_mm", l, tc))

                def heads_project(i):
                    if i == 0:
                        pe.wait_ge(*after("kvn_ready", l))
                        pe.wait_ge(*after("qn_ready", l))
                    else:
                        pe.wait_ge(*after("q_roped", l, i - 1))
                        pe.wait_ge(*after("k_roped", l, i - 1))
                    for k in range(3):
                        last = mm3(ps[0][0:QK, 0:n], weights(sq_, k, HEADS * QK, i * QK, i * QK + QK),
                                   (qn[:, k, 0, 0:n], qn[:, k, 1, 0:n]), k == 0, k == 2)
                    last.then_inc(*now("q_mm", l, i))
                    for k in range(2):
                        last = mm3(ps[1][0:NOPE, 0:T], weights(skv, k, 1024, i * P, i * P + NOPE),
                                   (kvn[:, k, 0, 0:T], kvn[:, k, 1, 0:T]), k == 0, k == 1)
                    last.then_inc(*now("k_mm", l, i))

                def heads_sum(i):
                    if i == 0:
                        pe.wait_ge(*after("v_copied", l, 1))
                    else:
                        pe.wait_ge(*after("k_root", l, i - 1))
                    pe.wait_ge(*after("q_squared", l, i))
                    mm(ps[2][0:QK, 0:n], ones[0:QK, 0:QK], tmp[0:QK, 0, 0:n], True, True).then_inc(*now("q_sum", l, i))
                    pe.wait_ge(*after("k_squared", l, i))
                    mm(ps[3][0:QK, 0:T], ones[0:QK, 0:QK], tmp[0:QK, 1, 0:T], True, True).then_inc(*now("k_sum", l, i))

                def heads_rotate(i):
                    b = i % 2
                    pe.wait_ge(*after("q_normed", l, i))
                    mm(ps[0][0:QK, 0:LX], rot[:], qh[0:QK, b, 0:LX], True, True).then_inc(*now("q_rot", l, i))
                    pe.wait_ge(*after("k_normed", l, i))
                    mm(ps[1][0:QK, 0:LX], rot[:], kh[0:QK, b, 0:LX], True, True).then_inc(*now("k_rot", l, i))

                tiles = [(0, 0, T), (1, 0, T)] + ([(2, LX, T), (3, LX, T)] if l == 0 else [])

                def scores(i, t):
                    b = i % 2
                    qt, ka, kz = tiles[t]
                    seq = i * len(tiles) + t
                    if t == 0:
                        pe.wait_ge(*after("q_roped", l, i))
                        pe.wait_ge(*after("k_roped", l, i))
                        if i == 0:
                            pe.wait_ge(*after("v_copied", l, 3))
                    if seq >= 2:
                        pe.wait_ge(*after("exp_done", l, seq - 2))
                    mm(ps[4 + seq % 2][:, 0:kz - ka], qh[0:QK, b, qt * P:qt * P + P], kh[0:QK, b, ka:kz],
                       True, True).then_inc(*now("scores", l, seq))

                def turn(i, t):
                    qt, ka, kz = tiles[t]
                    seq = i * len(tiles) + t
                    pe.wait_ge(*after("prob_ready", l, seq))
                    if seq >= 1:
                        pe.wait_ge(*after("prob_turned", l, seq - 1))
                    elif l == 0:
                        pe.wait_ge(*after("kvn_ready", l))
                    for c in range((kz - ka) // P):
                        last = nc.tensor.transpose(ps[6][:, c * P:c * P + P], prob[:, seq % 2, c * P:c * P + P], ident[:])
                    last.then_inc(*now("prob_turn", l, seq))

                def values(i, g):
                    nk = 4 if g == 0 else 2
                    r = (i % 2) * VD
                    seq = i * (len(tiles) // 2) + g
                    if seq >= 1:
                        pe.wait_ge(*after("a_done", l, seq - 1))
                    else:
                        pe.wait_ge(*after("kr_copied", l))
                    pe.wait_ge(*after("prob_turned", l, i * len(tiles) + 2 * g + 1))
                    for c in range(nk):
                        last = mm(ps[7][r:r + VD, 0:LX], V[:, 4 - nk + c, i * VD:i * VD + VD], pT[:, c, :], c == 0, c == nk - 1)
                    last.then_inc(*now("pv", l, seq))

                for i in range(HEADS + 1):
                    if i < HEADS:
                        heads_project(i)
                    if i > 0:
                        scores(i - 1, 0)
                        scores(i - 1, 1)
                    if i < HEADS:
                        heads_sum(i)
                    if i < HEADS and i == 0:
                        pe.wait_ge(*after("kr_copied", l))
                        for m in range(4):
                            modulation(l, 4, m)
                    if i > 0:
                        turn(i - 1, 0)
                        if i < HEADS:
                            if i > 1:
                                pe.wait_ge(*after("a_done", l, (i - 1) * (len(tiles) // 2) - 1))
                            for m in range(MOD_BEFORE):
                                modulation(l, 4 + i, m)
                        turn(i - 1, 1)
                        if i < HEADS:
                            for m in range(MOD_BEFORE, 4):
                                modulation(l, 4 + i, m)
                        if l == 0:
                            scores(i - 1, 2)
                            scores(i - 1, 3)
                        values(i - 1, 0)
                    if i < HEADS:
                        heads_rotate(i)
                    if i > 0 and l == 0:
                        turn(i - 1, 2)
                        turn(i - 1, 3)
                        values(i - 1, 1)
                    if i == HEADS - 1:
                        mm(ps[2][0:1, 0:1], ones[:, 0:1], ones[:, 0:1], True, True).then_inc(s_used, 1)
                        mm(ps[2][0:1, 0:1], ones[:, 0:1], ones[:, 0:1], True, True).then_inc(s_used, 1)

                for c in range(6):
                    if c % 2 == 0:
                        s = unit(4 + c // 2)
                    pe.wait_ge(*(after("pad_copied", l, c - 2) if c >= 2 else after("k_roped", l, HEADS - 1)))
                    last = project(ps[c % 2][:, 0:n], s, 256, (c % 2) * P, (c % 2) * P + P, n)
                    last.then_inc(*now("hy_mm", l, c))
                    if c % 2:
                        mm(ps[2][0:1, 0:1], ones[:, 0:1], ones[:, 0:1], True, True).then_inc(s_used, 1)
                s = unit(7)
                pe.wait_ge(*after("a_done", l, HEADS * (len(tiles) // 2) - 1))
                pe.wait_ge(*after("mod_added", l, 1))
                for c in range(4):
                    last = project(ps[4 + c][:, 0:n], s, 512, c * P, c * P + P, n)
                    last.then_inc(*now("gm_mm", l, c))
                mm(ps[2][0:1, 0:1], ones[:, 0:1], ones[:, 0:1], True, True).then_inc(s_used, 1)

                for st in range(n // 256):
                    if st == 0:
                        pe.wait_ge(*after("u_ready", l))
                    else:
                        pe.wait_ge(*after("uR_copied", l, st - 1))
                    for tc in range(2):
                        for c in range(2):
                            last = nc.tensor.transpose(ps[2][:, tc * 256 + c * P:tc * 256 + c * P + P],
                                                       z[:, 2 + c, st * 256 + tc * P:st * 256 + tc * P + P], ident[:])
                    last.then_inc(*now("u_turned", l, st))
                    pe.wait_ge(*after("uR_copied", l, st))
                    if st == 0:
                        pe.wait_ge(*after("pad_copied", l, 5))
                    else:
                        pe.wait_ge(*after("U_copied", l, st - 1))
                    for part, table in ((0, cos_s), (1, sin_s)):
                        for f in range(2):
                            for tc in range(2):
                                last = mm(ps[part][:, f * 256:f * 256 + 256], table[:, tc, f * P:f * P + P], uR[:, tc, :],
                                          tc == 0, tc == 1)
                    last.then_inc(*now("u_spec", l, st))
                    pe.wait_ge(*after("Y_ready", l, st))
                    if st > 0:
                        pe.wait_ge(*after("b_done", l, st - 1))
                    for c in range(2):
                        q = 0
                        for part, table in ((0, cos_s), (1, sin_s)):
                            for f in range(2):
                                last = mm(ps[3][:, c * 256:c * 256 + 256], Y[:, part, f, c * P:c * P + P], table[:, f, :],
                                          q == 0, q == 3)
                                q += 1
                    last.then_inc(*now("y_back", l, st))

                for c in range(2):
                    pe.wait_ge(*after("gv_sq", l, c))
                    if c == 0:
                        pe.wait_ge(*after("U_copied", l, n // 256 - 1))
                    mm(ps[0][:, 0:n], ones[:], gsq[:, c, 0:n], c == 0, c == 1).then_inc(*now("gv_sum", l, c))
                pe.wait_ge(*after("gv_normed", l))
                pe.wait_ge(*after("uR_copied", l, n // 256 - 1))
                for tc in range(n // P):
                    bk = (1, 2)[tc % 2]
                    if tc >= 2:
                        pe.wait_ge(*after("vR_copied", l, tc - 2))
                    for c in range(2):
                        last = nc.tensor.transpose(ps[bk][:, c * P:c * P + P], vn[:, c, tc * P:tc * P + P], ident[:])
                    last.then_inc(*now("gv_turned", l, tc))
                pe.wait_ge(*(after("const_loaded", 9) if l == 0 else after("spatial_loaded", l, 1)))
                pe.wait_ge(*after("gm_gelu", l, 3))
                pe.wait_ge(*after("vR_copied", l, n // P - 1))
                for g in range(GROUPS):
                    r = (g % 2) * 64
                    o = ps[4 + g // 2]
                    for tc in range(n // P):
                        oo = o[r:r + 64, tc * P:tc * P + P]
                        mm(oo, vR[:, tc, g * 64:g * 64 + 64], ws[:, g, :], True, False)
                        last = mm(oo, ones[0:1, 0:64], bs[0:1, g * P:g * P + P], False, True)
                    last.then_inc(*now("gm_spatial", l, g))

                def y_of(half):
                    return ylo4 if half == 0 else yhi4

                chunk = 0
                for half in range(2):
                    s = unit(8 + 4 * half)
                    if half == 0:
                        pe.wait_ge(*after("a_done", l, HEADS * (len(tiles) // 2) - 1))
                        pe.wait_ge(*after("b_done", l, n // 256 - 1))
                        pe.wait_ge(*after("m_done", l, 1))
                        pe.wait_ge(*after("vR_copied", l, n // P - 1))
                    for b, (act, nk, base) in enumerate(((aT, 4, 0), (bT, 2, 2048), (mT, 2, 3072))):
                        for j in range(4):
                            if chunk >= 4:
                                pe.wait_ge(*after("merge_evac", l, chunk - 4))
                            last = project(ps[chunk % 4][:, 0:n], s, 512, j * P, j * P + P, n, nk=nk, base=base, act=act)
                            last.then_inc(*now("branch_mm", l, half, b, j))
                            chunk += 1
                    mm(ps[4][0:1, 0:1], ones[:, 0:1], ones[:, 0:1], True, True).then_inc(s_used, 1)
                    for b in range(3):
                        s = unit(9 + 4 * half + b)
                        for j in range(4):
                            pe.wait_ge(*after("merge_evac", l, chunk - 4))
                            project(ps[chunk % 4][:, 0:n], s, 512, j * P, j * P + P, n).then_inc(*now("gate_mm", l, half, b, j))
                            chunk += 1
                        mm(ps[4][0:1, 0:1], ones[:, 0:1], ones[:, 0:1], True, True).then_inc(s_used, 1)
                for half in range(2):
                    s = unit(16 + half)
                    for j in range(4):
                        c = 4 * half + j
                        pe.wait_ge(*(after("merge_evac", l, chunk - 4) if c < 4 else after("x_mixed", l, c - 4)))
                        for k in range(8):
                            if c == 0:
                                pe.wait_ge(*after("y_ready", l, k))
                            y = y_of(k // 4)
                            last = mm3(ps[chunk % 4][:, 0:n], weights(s, k, 512, j * P, j * P + P),
                                       (y[:, k % 4, 0, 0:n], y[:, k % 4, 1, 0:n]), k == 0, k == 7)
                        last.then_inc(*now("out_mm", l, c))
                        chunk += 1
                    mm(ps[4][0:1, 0:1], ones[:, 0:1], ones[:, 0:1], True, True).then_inc(s_used, 1)

                norm_sum(1)
                pe.wait_ge(*after("x_mixed", l, 7))
                for k in range(KD):
                    pe.wait_ge(*after("hf_ready", l, k))
                    mm(ps[0][0:NE, 0:n], rw[:, k, :], hf[:, k % 2, 0:n], k == 0, k == KD - 1).then_inc(*now("logits", l, k))
                nt = n // P
                for q in range(nt * 4):
                    tc, sd, half = q // 4, q // 2 % 2, q % 2
                    if q >= 4:
                        pe.wait_ge(*after("tokens_copied", l, q - 4))
                    if q == 0:
                        pe.wait_ge(*after("h_ready", l, 1, 7))
                    for k in range(4):
                        last = mm(ps[4 + q % 4][:, k * P:k * P + P], h[:, 4 * half + k, sd, tc * P:tc * P + P], ident_h, True, True)
                    last.then_inc(*now("tokens_turned", l, q))
                pe.wait_ge(*after("logits_copied", l))
                for tc in range(nt):
                    last = nc.tensor.transpose(ps[2][:, tc * NE:tc * NE + NE], lgT[0:NE, tc * P:tc * P + P], ident[0:NE, 0:NE])
                last.then_inc(*now("logits_turned", l))
                pe.wait_ge(*after("picked", l))
                for tc in range(nt):
                    for t2 in range(tc + 1):
                        mm(ps[3][:, tc * NE:tc * NE + NE], before_h if t2 == tc else ones_h, pickh[:, t2 * NE:t2 * NE + NE],
                           t2 == 0, t2 == tc)
                for tc in range(nt):
                    last = mm(ps[3][:, 4 * NE:5 * NE], ones_h, pickh[:, tc * NE:tc * NE + NE], tc == 0, tc == nt - 1)
                last.then_inc(*now("ranked", l))

                su0, _ = expert_unit(l, 0, 0)

                def gather_mm(k):
                    for tc in range(nt):
                        for sd in range(2):
                            last = mm(ps[k // 4][:, (k % 4) * P:(k % 4) * P + P], hR[:, tc, sd, k * P:k * P + P], sel[:, tc, :],
                                      tc == 0 and sd == 0, tc == nt - 1 and sd == 1)
                    return last

                def turn_mm(weight_at):
                    for tc in range(nt):
                        mm(ps[4][:, tc * P:tc * P + P], sel[:, tc, :], ident_h, True, True)
                    for tc in range(nt):
                        last = mm(ps[5][:, 0:3], sel[:, tc, :], comb3[:, weight_at(tc)], tc == 0, tc == nt - 1)
                    return last

                def expert_in(slot, bank):
                    for m in range(KF):
                        last = project(ps[bank][:, m * P:m * P + P], slot, FE, m * P, m * P + P, P, act=he)
                    return last

                def down_product(half):
                    for k in range(KF):
                        last = mm(ps[4 + half][:, :], hid[:, k * P:k * P + P],
                                  stage[:, 2, k * D + 512 * half:k * D + 512 * half + 512], k == 0, k == KF - 1)
                    return last

                def scatter_mm(bank, c):
                    mm(ps[bank][:, 0:n], yR[:, 0, c * P:c * P + P], selT[:, 0:n], True, False)
                    return mm(ps[bank][:, 0:n], yR[:, 1, c * P:c * P + P], selT[:, 0:n], False, True)

                def gather(e, off):
                    pe.wait_ge(X["tokens_chosen"], reached(l, e, 1, off))
                    for k in range(KD):
                        last = gather_mm(k)
                        if k % 4 == 3:
                            last.then_inc(X["gathered"], 1)

                def scatter(e, off, c):
                    if c == 0:
                        pe.wait_ge(X["result_lo"], reached(l, e, 2, 2 * off + 1))
                    if not (isinstance(e, int) and e + off == 0 and c < 2):
                        pe.wait_ge(X["added"], reached(l, e, 8, 8 * off + c - 2))
                    scatter_mm(6 + c % 2, c).then_inc(X["scattered"], 1)

                def expert(e, first=False, last_one=False):
                    pe.wait_ge(s_lo, e * 2 + (su0 + 1))
                    pe.wait_ge(X["input_lo"], reached(l, e, 2, 1))
                    for m in range(KF):
                        project(ps[2][:, m * P:m * P + P], 0, FE, m * P, m * P + P, P, act=he).then_inc(X["gate_mm"], 1)
                        if not first:
                            scatter(e, -1, 2 * m)
                            scatter(e, -1, 2 * m + 1)
                    turn_mm(lambda tc: bass.ds(e * 12 + tc * 3, 3) if not isinstance(e, int)
                            else slice(e * 12 + tc * 3, e * 12 + tc * 3 + 3)).then_inc(X["choice_turned"], 1)
                    pe.wait_ge(s_lo, e * 2 + (su0 + 2))
                    expert_in(1, 3).then_inc(X["up_mm"], 1)
                    if not last_one:
                        gather(e, 1)
                    pe.wait_ge(X["hidden"], reached(l, e))
                    pe.wait_ge(X["choice_copied"], reached(l, e))
                    pe.wait_ge(X["weight_ready"], reached(l, e))
                    pe.wait_ge(s_stage[2], e * 16 + down_base)
                    for half in range(2):
                        down_product(half).then_inc(X["down_mm"], 1)

                down_base = landed(l, NMOD + NMIX + 2)[1]
                pe.wait_ge(*after("tokens_copied", l, nt * 4 - 1))
                gather(0, 0)
                expert(0, True)
                expert(1)
                with pe.Fori(2, NE - 1) as e:
                    expert(e)
                expert(NE - 1, False, True)
                for i in range(2 * NE // 16):
                    mm(ps[0][0:1, 0:1], ones[:, 0:1], ones[:, 0:1], True, True).then_inc(s_used, 16)
                for c in range(KD):
                    scatter(NE - 1, 0, c)

                pe.wait_ge(*after("spare_listed", l))
                with pe.Fori(0, MORE) as j:
                    row = pe.value_load(spare_list[0:1, bass.ds(j, 1)], min_val=0, max_val=SPARE + NE - 1)
                    e = pe.value_load(spare_list[0:1, bass.ds(j + MORE, 1)], min_val=0, max_val=NE - 1)
                    with pe.If(row > 0):
                        pe.wait_ge(spare_dve(l), j * SPARE_DVE + 2)
                        for k in range(KD):
                            last = gather_mm(k)
                        last.then_inc(spare_pe(l), 1)
                        turn_mm(lambda tc: bass.ds(e * 12 + tc * 3, 3)).then_inc(spare_pe(l), 1)
                        pe.wait_ge(spare_dve(l), j * SPARE_DVE + 5)
                        expert_in(0, 2)
                        expert_in(1, 3).then_inc(spare_pe(l), 1)
                        pe.wait_ge(spare_act(l), j * SPARE_ACT + 4)
                        pe.wait_ge(spare_dve(l), j * SPARE_DVE + 7)
                        pe.wait_ge(spare_loaded(l), j * 48 + 48)
                        down_product(0)
                        down_product(1).then_inc(spare_pe(l), 1)
                        pe.wait_ge(spare_dve(l), j * SPARE_DVE + 8)
                        for c in range(KD):
                            last = scatter_mm(c, c)
                        last.then_inc(spare_pe(l), 1)

        @block.scalar
        def _(act):
            def f(o, i, func, **kw):
                return nc.scalar.activation(o, i, func, **kw)

            def split_hi(i, su, n_landed, width, slot):
                act.wait_ge(*n_landed)
                if su >= RING:
                    act.wait_ge(s_used, su - RING + 1)
                f(whi[:, slot, 0:width], stage[:, where(i) % RING, 0:width], ACT.Copy).then_inc(s_hi, 1)

            def split(l, i):
                if i < NMIX:
                    su, _ = mix_unit(l, i)
                    split_hi(i, su, landed(l, where(i)), unit_width(l, MIX_UNITS[i]), i % RING)
                else:
                    su, _ = expert_unit(l, 0, i - NMIX)
                    split_hi(i, su, landed(l, NMOD + i), UNIT, i % RING)

            act.wait_ge(*after("small_loaded", 3))
            f(cT[:], cT[:], ACT.Silu).then_inc(*now("silu_c"))
            for l in range(DEPTH):
                for i in range(2):
                    act.wait_ge(*after("filt_arg", l, i))
                    f(fh[0:HID, i, :], fr_[0:HID, :], ACT.Sin).then_inc(*now("filt_sin", l, i))
                for c in range(2):
                    act.wait_ge(*after("filt_mm", l, 2 + c))
                    f(decay[:, c, :], ps[4 + c][:, :], ACT.Exp).then_inc(*now("filt_decay", l, c))
                for c in range(2):
                    act.wait_ge(*after("filt_k", l, c))
                    f(ksq[:, c, :], kf[:, c, :], ACT.Square).then_inc(*now("filt_sq", l, c))
                act.wait_ge(*after("filt_eps", l))
                f(krs[:, :], krs[:, :], ACT.Sqrt).then_inc(*now("filt_root", l))

            for l in range(DEPTH):
                n = T if l == 0 else LX

                def squares(which):
                    m = T if which == 0 else n
                    for k in range(KD):
                        if which == 0 and l == 0 and k == 0:
                            act.wait_ge(*after("x_loaded", 1))
                            act.wait_ge(*after("filt_spec", DEPTH - 1, 1))
                            act.wait_ge(*after("filt_copied", DEPTH - 1, 1))
                        elif which == 0 and k == 0:
                            act.wait_ge(*after("moe_added", l - 1))
                        elif which == 1:
                            act.wait_ge(*after("x_mixed", l, k))
                            if k == 0:
                                act.wait_ge(*after("y_ready", l, 7))
                        if k >= 2:
                            act.wait_ge(*after("x_summed", l, which, k - 2))
                        f(sq[:, k % 2, 0:m], xT[:, k, 0:m], ACT.Square).then_inc(*now("x_squared", l, which, k))
                    act.wait_ge(*after("x_summed", l, which, 7))
                    act.wait_ge(*after("eps_set"))
                    f(rstd[:, 0:m], ps[1][:, 0:m], ACT.Sqrt, bias=small[:, 60:61], scale=1.0 / D).then_inc(*now("x_root", l, which))

                squares(0)
                split(l, 0)
                split(l, 1)
                for m in range(3):
                    act.wait_ge(*after("q_low", l, 2 if m == 2 else m))
                    if m == 0:
                        act.wait_ge(*after("h_ready", l, 0, 7))
                    if m == 2:
                        act.wait_ge(*after("q_low_sum", l, 0))
                    f(pq[:, m, 0:n], ps[2 + m][:, 0:n], ACT.Copy).then_inc(*now("q_low_copied", l, m))
                    act.wait_ge(*after("q_low_copied", l, m))
                    f(tmp[:, m % 2, 0:n], pq[:, m, 0:n], ACT.Square).then_inc(*now("q_low_sq", l, m))
                split(l, 2)
                for m in range(2):
                    act.wait_ge(*after("kv_low", l, m))
                    act.wait_ge(*after("q_low_sum", l, 1 + m))
                    f(pkv[:, m, :], ps[5 + m][:, :], ACT.Copy).then_inc(*now("kv_low_copied", l, m))
                    act.wait_ge(*after("kv_low_copied", l, m))
                    f(tmp[:, (m + 1) % 2, :], pkv[:, m, :], ACT.Square).then_inc(*now("kv_low_sq", l, m))
                act.wait_ge(*after("kv_low", l, 2))
                f(kr[NOPE:QK, :], ps[7][NOPE:QK, :], ACT.Copy).then_inc(*now("kr_copied", l))
                act.wait_ge(*after("q_low_sum", l, 2))
                f(rq[:, 0, 0:n], ps[0][:, 0:n], ACT.Sqrt, bias=small[:, 60:61], scale=1.0 / QR).then_inc(*now("q_low_root", l))
                act.wait_ge(*after("kv_low_sum", l, 1))
                f(rq[:, 1, :], ps[1][:, :], ACT.Sqrt, bias=small[:, 60:61], scale=1.0 / KVR).then_inc(*now("kv_low_root", l))
                split(l, 3)
                for tc in range(4):
                    act.wait_ge(*after("v_mm", l, tc))
                    f(V[:, tc, :], ps[2 + tc][:, :], ACT.Copy).then_inc(*now("v_copied", l, tc))
                split(l, 4)

                ntile = 4 if l == 0 else 2

                def head_copies(i):
                    b = i % 2
                    act.wait_ge(*after("q_mm", l, i))
                    if i == 0:
                        act.wait_ge(*after("qn_ready", l))
                        act.wait_ge(*after("kvn_ready", l))
                    if i >= 2:
                        act.wait_ge(*after("scores", l, (i - 1) * ntile - 1))
                    f(qh[0:QK, b, 0:n], ps[0][0:QK, 0:n], ACT.Copy).then_inc(*now("q_copied", l, i))
                    act.wait_ge(*after("k_mm", l, i))
                    f(kh[0:NOPE, b, :], ps[1][0:NOPE, :], ACT.Copy).then_inc(*now("k_copied", l, i))
                    act.wait_ge(*after("kr_copied", l))
                    f(kh[NOPE:QK, b, :], kr[NOPE:QK, :], ACT.Copy).then_inc(*now("kr_placed", l, i))
                    act.wait_ge(*after("q_copied", l, i))
                    if i == 0:
                        act.wait_ge(*after("kv_low_sum", l, 1))
                    else:
                        act.wait_ge(*after("q_roped", l, i - 1))
                        act.wait_ge(*after("k_roped", l, i - 1))
                    f(tmp[0:QK, 0, 0:n], qh[0:QK, b, 0:n], ACT.Square).then_inc(*now("q_squared", l, i))
                    act.wait_ge(*after("kr_placed", l, i))
                    f(tmp[0:QK, 1, :], kh[0:QK, b, :], ACT.Square).then_inc(*now("k_squared", l, i))

                def head_roots(i):
                    act.wait_ge(*after("q_sum", l, i))
                    if i > 0:
                        act.wait_ge(*after("k_normed", l, i - 1))
                    f(rq[0:QK, 0, 0:n], ps[2][0:QK, 0:n], ACT.Sqrt, bias=small[0:QK, 60:61], scale=1.0 / QK).then_inc(*now("q_root", l, i))
                    act.wait_ge(*after("k_sum", l, i))
                    f(rq[0:QK, 1, :], ps[3][0:QK, :], ACT.Sqrt, bias=small[0:QK, 60:61], scale=1.0 / QK).then_inc(*now("k_root", l, i))

                def exps(i, t):
                    seq = i * ntile + t
                    nk = T if t < 2 else LC
                    act.wait_ge(*after("max_ready", l, seq))
                    if seq >= 2:
                        act.wait_ge(*after("prob_turn", l, seq - 2))
                    elif seq == 0:
                        act.wait_ge(*after("kvn_ready", l))
                    s2 = 4 * (seq % 2)
                    f(prob[:, seq % 2, 0:nk], ps[4 + seq % 2][:, 0:nk], ACT.Exp, bias=small[:, s2:s2 + 1],
                      scale=SCALE, accum_out=small[:, s2 + 1:s2 + 2]).then_inc(*now("exp_done", l, seq))

                def turned(i, t):
                    seq = i * ntile + t
                    nk = 4 if t < 2 else 2
                    act.wait_ge(*after("prob_turn", l, seq))
                    if t % 2 == 0:
                        if seq > 0:
                            act.wait_ge(*after("pv", l, seq // 2 - 1))
                    f(pT[:, 0:nk, (t % 2) * P:(t % 2) * P + P],
                      ps[6][:, 0:nk * P].rearrange("p (c q) -> p c q", c=nk), ACT.Copy).then_inc(*now("prob_turned", l, seq))

                for i in range(HEADS + 1):
                    if i < HEADS:
                        head_copies(i)
                    if i > 0:
                        exps(i - 1, 0)
                        exps(i - 1, 1)
                    if i < HEADS:
                        head_roots(i)
                    if i > 0:
                        turned(i - 1, 0)
                        turned(i - 1, 1)
                        if l == 0:
                            exps(i - 1, 2)
                            exps(i - 1, 3)
                            turned(i - 1, 2)
                            turned(i - 1, 3)

                split(l, 5)
                split(l, 6)
                for c in range(6):
                    act.wait_ge(*after("hy_mm", l, c))
                    if c >= 2:
                        act.wait_ge(*after("conv_done", l, c - 2))
                    else:
                        act.wait_ge(*after("pads_zero", l))
                    f(pad[:, c % 2, 0:n // 256, 1:257], ps[c % 2][:, 0:n].rearrange("p (s t) -> p s t", t=256),
                      ACT.Copy).then_inc(*now("pad_copied", l, c))
                    if c == 1:
                        split(l, 7)
                    if c == 3:
                        split(l, 8)
                    if c == 5:
                        split(l, 9)

                for st in range(n // 256):
                    act.wait_ge(*after("u_turned", l, st))
                    f(uR, ps[2][:, :].rearrange("p (c t) -> p c t", c=2), ACT.Copy).then_inc(*now("uR_copied", l, st))
                    act.wait_ge(*after("u_spec", l, st))
                    if st > 0:
                        act.wait_ge(*after("Y_ready", l, st - 1))
                    f(U[:, 0], ps[0][:, :].rearrange("p (f c) -> p f c", f=2), ACT.Copy)
                    f(U[:, 1], ps[1][:, :].rearrange("p (f c) -> p f c", f=2), ACT.Copy).then_inc(*now("U_copied", l, st))
                act.wait_ge(*after("b_done", l, n // 256 - 1))
                for c in range(4):
                    act.wait_ge(*after("gm_mm", l, c))
                    f(gl[:, c, 0:n], ps[4 + c][:, 0:n], ACT.Gelu_apprx_tanh).then_inc(*now("gm_gelu", l, c))
                for c in range(2):
                    act.wait_ge(*after("gm_gelu", l, 2 + c))
                    f(gsq[:, c, 0:n], gl[:, 2 + c, 0:n], ACT.Square).then_inc(*now("gv_sq", l, c))
                act.wait_ge(*after("gv_sum", l, 1))
                f(grs[:, 0:n], ps[0][:, 0:n], ACT.Sqrt, bias=small[:, 60:61], scale=1.0 / GM).then_inc(*now("gv_root", l))
                for tc in range(n // P):
                    act.wait_ge(*after("gv_turned", l, tc))
                    f(vR[:, tc, :], ps[(1, 2)[tc % 2]][:, 0:256], ACT.Copy).then_inc(*now("vR_copied", l, tc))

                chunk = 0
                for half in range(2):
                    for b in range(3):
                        for j in range(4):
                            act.wait_ge(*after("branch_mm", l, half, b, j))
                            if b == 0 and j == 0:
                                act.wait_ge(*(after("m_done", l, 1) if half == 0 else after("y_ready", l, 3)))
                            f(br[:, b, j, 0:n], ps[chunk % 4][:, 0:n], ACT.Copy).then_inc(*now("merge_evac", l, chunk))
                            chunk += 1
                    for b in range(3):
                        split(l, 10 + 4 * half + b)
                        for j in range(4):
                            act.wait_ge(*after("gate_mm", l, half, b, j))
                            g = half * 12 + b * 4 + j
                            if g >= 2:
                                act.wait_ge(*after("gated", l, g - 2))
                            f(sig[:, g % 2, 0:n], ps[chunk % 4][:, 0:n], ACT.Sigmoid).then_inc(*now("merge_evac", l, chunk))
                            chunk += 1
                    split(l, 13 + 4 * half)
                split(l, 18)
                squares(1)
                split(l, 19)
                for q in range(n // P * 4):
                    tc, sd, half = q // 4, q // 2 % 2, q % 2
                    act.wait_ge(*after("tokens_turned", l, q))
                    if q == 0:
                        act.wait_ge(*after("out_mm", l, 7))
                    f(hR[:, tc, sd, 512 * half:512 * half + 512], ps[4 + q % 4][:, :], ACT.Copy).then_inc(*now("tokens_copied", l, q))
                act.wait_ge(*after("logits_turned", l))
                m4 = n // P
                f(rt[:, 0:NE * m4], ps[2][:, 0:NE * m4], ACT.Sigmoid).then_inc(*now("aff", l))

                su0, _ = expert_unit(l, 0, 0)
                base = [landed(l, NMOD + NMIX + i)[1] for i in range(2)]

                def split_expert(e, i, off):
                    act.wait_ge(s_stage[i], e * 16 + (base[i] + 16 * off))
                    if isinstance(e, int) and e + off == 0:
                        act.wait_ge(s_used, su0 + i - RING + 1)
                    else:
                        per = (KF, 1)[i]
                        act.wait_ge(X[("gate_mm", "up_mm")[i]], reached(l, e, per, per * off - 1))
                    f(whi[:, i, :], stage[:, i, :], ACT.Copy).then_inc(s_hi, 1)

                def input_hi(half):
                    return f(he[:, 4 * half:4 * half + 4, 0, :], ps[half][:, :].rearrange("p (k t) -> p k t", k=4), ACT.Copy)

                def result_hi(half):
                    return f(yR[:, 0, 512 * half:512 * half + 512], ps[4 + half][:, :], ACT.Identity, scale=csum)

                def gathered(e, off):
                    for half in range(2):
                        act.wait_ge(X["gathered"], reached(l, e, 2, 2 * off + half))
                        input_hi(half).then_inc(X["input_hi"], 1)

                def expert(e, last_one=False):
                    act.wait_ge(X["gate_mm"], reached(l, e, KF, KF - 1))
                    f(sg, ps[2][:, :], ACT.Silu).then_inc(X["gate_silu"], 1)
                    if not last_one:
                        split_expert(e, 0, 1)
                    act.wait_ge(X["choice_turned"], reached(l, e))
                    f(selT[:, 0:n], ps[4][:, 0:n], ACT.Copy).then_inc(X["choice_copied"], 1)
                    if not last_one:
                        split_expert(e, 1, 1)
                        gathered(e, 1)
                    act.wait_ge(X["weight_ready"], reached(l, e))
                    for half in range(2):
                        act.wait_ge(X["down_mm"], reached(l, e, 2, half))
                        result_hi(half).then_inc(X["result_hi"], 1)

                gathered(0, 0)
                expert(0)
                with act.Fori(1, NE - 1) as e:
                    expert(e)
                expert(NE - 1, True)

                act.wait_ge(*after("spare_listed", l))
                with act.Fori(0, MORE) as j:
                    row = act.value_load(spare_list[0:1, bass.ds(j, 1)], min_val=0, max_val=SPARE + NE - 1)
                    with act.If(row > 0):
                        for i in range(2):
                            act.wait_ge(spare_loaded(l), j * 48 + 48)
                            f(whi[:, i, :], stage[:, i, :], ACT.Copy).then_inc(spare_act(l), 1)
                        act.wait_ge(spare_pe(l), j * SPARE_PE + 1)
                        input_hi(0)
                        input_hi(1).then_inc(spare_act(l), 1)
                        act.wait_ge(spare_pe(l), j * SPARE_PE + 2)
                        f(selT[:, 0:n], ps[4][:, 0:n], ACT.Copy).then_inc(spare_act(l), 1)
                        act.wait_ge(spare_pe(l), j * SPARE_PE + 3)
                        f(sg, ps[2][:, :], ACT.Silu).then_inc(spare_act(l), 1)
                        act.wait_ge(spare_pe(l), j * SPARE_PE + 4)
                        result_hi(0)
                        result_hi(1).then_inc(spare_act(l), 1)

        @block.vector
        def _(dve):
            chain = sem_of("vector_step")
            steps = [0]

            def link(ins_):
                steps[0] += 1
                ins_.then_inc(chain, 1)
                dve.wait_ge(chain, steps[0])

            def tt(o, a, b, op):
                return nc.vector.tensor_tensor(o, a, b, op)

            def ts(o, a, s1, s2, op0, op1=None):
                if op1 is None:
                    return nc.vector.tensor_scalar(o, a, s1, None, op0)
                return nc.vector.tensor_scalar(o, a, s1, s2, op0, op1)

            def stt(o, a, s, b, op0, op1):
                return nc.vector.scalar_tensor_tensor(out=o, in0=a, scalar=s, in1=b, op0=op0, op1=op1)

            def split(l, i):
                if i < NMIX:
                    su, _ = mix_unit(l, i)
                    width = unit_width(l, MIX_UNITS[i])
                else:
                    su, _ = expert_unit(l, 0, i - NMIX)
                    width = UNIT
                slot = i % RING
                dve.wait_ge(s_hi, su + 1)
                tt(wlo[:, slot, 0:width], stage[:, where(i) % RING, 0:width], whi[:, slot, 0:width], ALU.subtract).then_inc(s_lo, 1)

            link(nc.vector.memset(small[:, 60:61], EPS))
            nc.vector.memset(small[:, 61:62], 0.0).then_inc(*now("eps_set"))
            for l in range(DEPTH):
                for i in range(2):
                    dve.wait_ge(*after("filt_mm", l, i))
                    if i == 0:
                        dve.wait_ge(*after("filter_loaded", l, 5))
                        if l > 0:
                            dve.wait_ge(*after("filt_spec", l - 1, 1))
                    else:
                        dve.wait_ge(*after("filt_sin", l, 0))
                    w = slice(0, HID)
                    bcol = col(l, "b1" if i == 0 else "b2")[w]
                    link(ts(fa[w, :], ps[0][w, 256 * i:256 * i + 256], bcol, col(l, "freq")[w], ALU.add, ALU.mult))
                    link(ts(fk[w, :], fa[w, :], float(1 / (2 * np.pi)), ROUND, ALU.mult, ALU.add))
                    link(ts(fk[w, :], fk[w, :], ROUND, None, ALU.subtract))
                    link(stt(fa[w, :], fk[w, :], -TWO_PI_HI, fa[w, :], ALU.mult, ALU.add))
                    link(stt(fa[w, :], fk[w, :], -TWO_PI_LO, fa[w, :], ALU.mult, ALU.add))
                    ts(fr_[w, :], fa[w, :], 3.1415925, -3.1415925, ALU.min, ALU.max).then_inc(*now("filt_arg", l, i))
                link(nc.vector.memset(fh[HID:HID + 1, 1, :], 1.0))
                stt(dec[0:1, :], dec[0:1, :], -1.0, dec[0:1, :], ALU.mult, ALU.max).then_inc(*now("decay_abs", l))
                for c in range(2):
                    dve.wait_ge(*after("filt_decay", l, c))
                    tt(kf[:, c, :], ps[2 + c][:, :], decay[:, c, :], ALU.mult).then_inc(*now("filt_k", l, c))
                dve.wait_ge(*after("filt_ssq", l))
                ts(krs[:, :], ps[0][:, 0:256], EPS, None, ALU.add).then_inc(*now("filt_eps", l))
                dve.wait_ge(*after("filt_root", l))
                link(nc.vector.reciprocal(krs[:, :], krs[:, :]))
                for c in range(2):
                    for d in range(2):
                        link(stt(kf[:, c, d * HY:d * HY + HY], kf[:, c, d * HY:d * HY + HY], 1.0 / 256, krs[:, :], ALU.mult, ALU.mult))
                link(ts(kf[0:1, 0, HY:2 * HY], kf[0:1, 0, HY:2 * HY], 0.0, None, ALU.mult))
                for c in range(2):
                    link(tt(kab[:, 0, c, :], kf[:, c, 0:HY], kf[:, c, HY:2 * HY], ALU.add))
                    last = tt(kab[:, 1, c, :], kf[:, c, HY:2 * HY], kf[:, c, 0:HY], ALU.subtract)
                    if c == 0:
                        link(last)
                last.then_inc(*now("filt_ab", l))
                for fch in range(2):
                    dve.wait_ge(*after("filt_spec", l, fch))
                    nc.vector.tensor_copy(kfilt[:, l, :, fch, :], ps[6 + fch][:, :].rearrange("p (r c) -> p r c", r=2)
                                          ).then_inc(*now("filt_copied", l, fch))

            for l in range(DEPTH):
                n = T if l == 0 else LX

                def modulated(part):
                    a, b = (0, 32) if part == 0 else (32, 96)
                    ab = COLS["bmod"][0]
                    dve.wait_ge(s_mod, l * NMOD + (4, NMOD)[part])
                    src = ps[1][:, a:b] if part == 0 else ps[7][:, 256 + a:256 + b]
                    tt(modc[:].rearrange("p a b -> p (a b)")[:, a:b], src, cols[:, l, ab + a:ab + b], ALU.add).then_inc(*now("mod_added", l, part))
                    dve.wait_ge(*after("mod_added", l, part))
                    at = (8, 32)[part]
                    link(stt(gs[:, part].rearrange("p a b -> p (a b)"), modc[:, at:at + 8, :].rearrange("p a b -> p (a b)"), 1.0,
                             col(l, ("g1", "g2")[part]), ALU.add, ALU.mult))

                modulated(0)

                def normed(which):
                    m = T if which == 0 else n
                    dve.wait_ge(*after("x_root", l, which))
                    link(nc.vector.reciprocal(rstd[:, 0:m], rstd[:, 0:m]))
                    for k in range(KD):
                        if which == 1 and k >= 2:
                            dve.wait_ge(*after("logits", l, k - 2))
                        link(tt(hf[:, k % 2, 0:m], xT[:, k, 0:m], rstd[:, 0:m], ALU.mult))
                        for st in range(m // 256):
                            c = slice(st * 256, st * 256 + 256)
                            last = ts(hf[:, k % 2, c], hf[:, k % 2, c], gs[:, which, k, st:st + 1],
                                      modc[:, 24 * which + k, st:st + 1], ALU.mult, ALU.add)
                            if st < m // 256 - 1:
                                link(last)
                        if which == 1:
                            last.then_inc(*now("hf_ready", l, k))
                            dve.wait_ge(*after("hf_ready", l, k))
                        else:
                            link(last)
                        link(nc.vector.tensor_copy(h[:, k, 0, 0:m], hf[:, k % 2, 0:m]))
                        tt(h[:, k, 1, 0:m], hf[:, k % 2, 0:m], h[:, k, 0, 0:m], ALU.subtract).then_inc(*now("h_ready", l, which, k))
                        dve.wait_ge(*after("h_ready", l, which, k))

                normed(0)
                split(l, 0)
                split(l, 1)
                split(l, 2)

                def low_norm(src, r, gname, dst, nk, m, done):
                    link(nc.vector.reciprocal(r, r))
                    for k in range(nk):
                        link(stt(src[:, k, 0:m], src[:, k, 0:m], col(l, gname)[:, k:k + 1], r, ALU.mult, ALU.mult))
                        link(nc.vector.tensor_copy(dst[:, k, 0, 0:m], src[:, k, 0:m]))
                        last = tt(dst[:, k, 1, 0:m], src[:, k, 0:m], dst[:, k, 0, 0:m], ALU.subtract)
                        if k < nk - 1:
                            link(last)
                    last.then_inc(*now(done, l))
                    dve.wait_ge(*after(done, l))

                dve.wait_ge(*after("q_low_root", l))
                dve.wait_ge(*after("q_low_copied", l, 2))
                low_norm(pq, rq[:, 0, 0:n], "gqa", qn, 3, n, "qn_ready")
                dve.wait_ge(*after("kv_low_root", l))
                low_norm(pkv, rq[:, 1, :], "gkva", kvn, 2, T, "kvn_ready")
                split(l, 3)
                split(l, 4)

                ntile = 4 if l == 0 else 2

                def head_norms(i):
                    b = i % 2
                    for which, (x, m, root, copied, g) in enumerate((
                            (qh, n, "q_root", "q_copied", "gqn"), (kh, T, "k_root", "kr_placed", "gkn"))):
                        dve.wait_ge(*after(root, l, i))
                        dve.wait_ge(*after(("q_squared", "k_squared")[which], l, i))
                        dve.wait_ge(*after(copied, l, i))
                        link(nc.vector.reciprocal(rq[0:QK, which, 0:m], rq[0:QK, which, 0:m]))
                        stt(x[0:QK, b, 0:m], x[0:QK, b, 0:m], col(l, g)[0:QK], rq[0:QK, which, 0:m],
                            ALU.mult, ALU.mult).then_inc(*now(("q_normed", "k_normed")[which], l, i))

                def head_ropes(i):
                    b = i % 2
                    for which, (x, name) in enumerate(((qh, "q"), (kh, "k"))):
                        dve.wait_ge(*after(name + "_rot", l, i))
                        dve.wait_ge(*after(name + "_sum", l, i))
                        link(tt(x[0:QK, b, 0:LX], x[0:QK, b, 0:LX], rope[:, 0, :], ALU.mult))
                        link(tt(tmp[0:QK, which, 0:LX], ps[which][0:QK, 0:LX], rope[:, 1, :], ALU.mult))
                        tt(x[0:QK, b, 0:LX], x[0:QK, b, 0:LX], tmp[0:QK, which, 0:LX], ALU.add).then_inc(*now(name + "_roped", l, i))

                def maxes(i, t):
                    seq = i * ntile + t
                    nk = T if t < 2 else LC
                    s2 = 4 * (seq % 2)
                    dve.wait_ge(*after("scores", l, seq))
                    if seq >= 2:
                        dve.wait_ge(*after("prob_ready", l, seq - 2))
                    nc.vector.tensor_reduce(small[:, s2 + 2:s2 + 3], ps[4 + seq % 2][:, 0:nk], AX.X, ALU.max).then_inc(*now("max_raw", l, seq))
                    dve.wait_ge(*after("max_raw", l, seq))
                    ts(small[:, s2:s2 + 1], small[:, s2 + 2:s2 + 3], -SCALE, None, ALU.mult).then_inc(*now("max_ready", l, seq))

                def normalised(i, t):
                    seq = i * ntile + t
                    nk = T if t < 2 else LC
                    s2 = 4 * (seq % 2)
                    dve.wait_ge(*after("exp_done", l, seq))
                    link(nc.vector.reciprocal(small[:, s2 + 3:s2 + 4], small[:, s2 + 1:s2 + 2]))
                    ts(prob[:, seq % 2, 0:nk], prob[:, seq % 2, 0:nk], small[:, s2 + 3:s2 + 4], None,
                       ALU.mult).then_inc(*now("prob_ready", l, seq))

                def head_out(i, g):
                    r = slice((i % 2) * VD, (i % 2) * VD + VD)
                    seq = i * (ntile // 2) + g
                    c = slice(g * 256, g * 256 + 256)
                    dve.wait_ge(*after("pv", l, seq))
                    link(nc.vector.tensor_copy(aT[r, i // 2, 0, c], ps[7][r, 0:256]))
                    tt(aT[r, i // 2, 1, c], ps[7][r, 0:256], aT[r, i // 2, 0, c], ALU.subtract).then_inc(*now("a_done", l, seq))

                dve.wait_ge(*after("const_loaded", 9))
                for i in range(HEADS + 1):
                    if i > 0:
                        maxes(i - 1, 0)
                        maxes(i - 1, 1)
                        normalised(i - 1, 0)
                        normalised(i - 1, 1)
                    if i < HEADS:
                        head_norms(i)
                    if i > 0 and l == 0:
                        maxes(i - 1, 2)
                        maxes(i - 1, 3)
                    if i < HEADS:
                        pass
                    if i > 0:
                        head_out(i - 1, 0)
                    if i < HEADS:
                        head_ropes(i)
                    if i > 0 and l == 0:
                        normalised(i - 1, 2)
                        normalised(i - 1, 3)
                        head_out(i - 1, 1)

                modulated(1)

                split(l, 5)
                split(l, 6)
                ns = n // 256
                dve.wait_ge(*after("v_copied", l, 3))
                dve.wait_ge(*after("pv", l, HEADS * (ntile // 2) - 1))
                for b in range(2):
                    for e in (0, 257):
                        last = nc.vector.memset(pad[:, b, :, e:e + 1], 0.0)
                        if (b, e) != (1, 257):
                            link(last)
                last.then_inc(*now("pads_zero", l))
                cw, cbias = col(l, "convw"), col(l, "convb")
                for c in range(6):
                    dve.wait_ge(*after("pad_copied", l, c))
                    zz = z[:, c, 0:n].rearrange("p (s t) -> p s t", t=256)
                    p = pad[:, c % 2, 0:ns]
                    link(ts(zz, p[:, :, 0:256], cw[:, c:c + 1], cbias[:, c:c + 1], ALU.mult, ALU.add))
                    link(stt(zz, p[:, :, 1:257], cw[:, 6 + c:7 + c], zz, ALU.mult, ALU.add))
                    stt(zz, p[:, :, 2:258], cw[:, 12 + c:13 + c], zz, ALU.mult, ALU.add).then_inc(*now("conv_done", l, c))
                    dve.wait_ge(*after("conv_done", l, c))
                    if c == 1:
                        split(l, 7)
                    if c == 3:
                        split(l, 8)
                    if c == 5:
                        split(l, 9)
                tt(z[:, 2:4, 0:n], z[:, 2:4, 0:n], z[:, 4:6, 0:n], ALU.mult).then_inc(*now("u_ready", l))
                for st in range(ns):
                    cs = slice(st * 256, st * 256 + 256)
                    dve.wait_ge(*after("U_copied", l, st))
                    if st > 0:
                        dve.wait_ge(*after("y_back", l, st - 1))
                    K = kfilt[:, l]
                    link(tt(Y[:, 0], U[:, 0], K[:, 0], ALU.mult))
                    link(tt(hyt[:, 0], U[:, 1], K[:, 1], ALU.mult))
                    link(tt(Y[:, 0], Y[:, 0], hyt[:, 0], ALU.add))
                    link(tt(Y[:, 1], U[:, 1], K[:, 0], ALU.mult))
                    link(tt(hyt[:, 1], U[:, 0], K[:, 1], ALU.mult))
                    tt(Y[:, 1], Y[:, 1], hyt[:, 1], ALU.subtract).then_inc(*now("Y_ready", l, st))
                    dve.wait_ge(*after("y_back", l, st))
                    dve.wait_ge(*after("u_ready", l))
                    for c in range(2):
                        link(stt(hyb[:, c, :], z[:, 2 + c, cs], col(l, "hybias")[:, c:c + 1], ps[3][:, c * 256:c * 256 + 256],
                                 ALU.mult, ALU.add))
                        link(tt(hyb[:, c, :], hyb[:, c, :], z[:, c, cs], ALU.mult))
                        link(nc.vector.tensor_copy(bT[:, c, 0, cs], hyb[:, c, :]))
                        last = tt(bT[:, c, 1, cs], hyb[:, c, :], bT[:, c, 0, cs], ALU.subtract)
                        if c == 0:
                            link(last)
                    last.then_inc(*now("b_done", l, st))
                    dve.wait_ge(*after("b_done", l, st))

                dve.wait_ge(*after("gv_root", l))
                link(nc.vector.reciprocal(grs[:, 0:n], grs[:, 0:n]))
                for c in range(2):
                    last = stt(vn[:, c, 0:n], gl[:, 2 + c, 0:n], col(l, "gmg")[:, c:c + 1], grs[:, 0:n], ALU.mult, ALU.mult)
                    if c == 0:
                        link(last)
                last.then_inc(*now("gv_normed", l))
                for c in range(2):
                    dve.wait_ge(*after("gm_spatial", l, 2 * c + 1))
                    link(tt(gmt[:, c, 0:n], gl[:, c, 0:n], ps[4 + c][:, 0:n], ALU.mult))
                    link(nc.vector.tensor_copy(mT[:, c, 0, 0:n], gmt[:, c, 0:n]))
                    tt(mT[:, c, 1, 0:n], gmt[:, c, 0:n], mT[:, c, 0, 0:n], ALU.subtract).then_inc(*now("m_done", l, c))

                chunk = 0
                for half in range(2):
                    y = ylo4 if half == 0 else yhi4
                    chunk += 12
                    for b in range(3):
                        split(l, 10 + 4 * half + b)
                        for j in range(4):
                            dve.wait_ge(*after("merge_evac", l, chunk))
                            chunk += 1
                            g = half * 12 + b * 4 + j
                            tt(br[:, b, j, 0:n], br[:, b, j, 0:n], sig[:, g % 2, 0:n], ALU.mult).then_inc(*now("gated", l, g))
                            if b == 2:
                                dve.wait_ge(*after("gated", l, g))
                                link(tt(br[:, 0, j, 0:n], br[:, 0, j, 0:n], br[:, 1, j, 0:n], ALU.add))
                                link(tt(br[:, 0, j, 0:n], br[:, 0, j, 0:n], br[:, 2, j, 0:n], ALU.add))
                                link(nc.vector.tensor_copy(y[:, j, 0, 0:n], br[:, 0, j, 0:n]))
                                tt(y[:, j, 1, 0:n], br[:, 0, j, 0:n], y[:, j, 0, 0:n], ALU.subtract).then_inc(*now("y_ready", l, 4 * half + j))
                    split(l, 13 + 4 * half)
                split(l, 18)
                for c in range(8):
                    dve.wait_ge(*after("out_mm", l, c))
                    for st in range(ns):
                        cs = slice(st * 256, st * 256 + 256)
                        last = stt(xT[:, c, cs], ps[(48 + c) % 4][:, cs], modc[:, 16 + c, st:st + 1], xT[:, c, cs], ALU.mult, ALU.add)
                        if st < ns - 1:
                            link(last)
                    last.then_inc(*now("x_mixed", l, c))

                dve.wait_ge(*after("x_mixed", l, 7))
                normed(1)
                split(l, 19)
                dve.wait_ge(*after("logits", l, 7))
                dve.wait_ge(*after("y_ready", l, 7))
                nc.vector.tensor_copy(lgT[0:NE, 0:n], ps[0][0:NE, 0:n]).then_inc(*now("logits_copied", l))
                m4 = n // P
                W = NE * m4

                def rv(a, w=16):
                    return rt[:, a:a + w * m4].rearrange("p (t e) -> p t e", t=m4)

                aff, score = rv(0), rv(64)
                hi1, lo1, hi2, lo2, gsc = rv(128, 4), rv(144, 4), rv(160, 4), rv(176, 4), rv(192, 4)
                gmax, comb = rv(208, 1), rv(256)
                msk, pick = rv(320), rv(384)
                pick2 = rv(448)
                dve.wait_ge(*after("aff", l))
                rbb = rb[:].unsqueeze(1).to_broadcast([P, m4, NE])
                link(tt(score, aff, rbb, ALU.add))
                s4 = score.rearrange("p t (g j) -> p t g j", g=4)
                link(tt(hi1, s4[:, :, :, 0], s4[:, :, :, 1], ALU.max))
                link(tt(lo1, s4[:, :, :, 0], s4[:, :, :, 1], ALU.min))
                link(tt(hi2, s4[:, :, :, 2], s4[:, :, :, 3], ALU.max))
                link(tt(lo2, s4[:, :, :, 2], s4[:, :, :, 3], ALU.min))
                link(tt(gsc, hi1, hi2, ALU.max))
                link(tt(hi1, hi1, hi2, ALU.min))
                link(tt(lo1, lo1, lo2, ALU.max))
                link(tt(hi1, hi1, lo1, ALU.max))
                link(tt(gsc, gsc, hi1, ALU.add))

                def first_max(dst, src, w, orders):
                    link(nc.vector.tensor_reduce(gmax, src, AX.X, ALU.max))
                    link(tt(dst, src, gmax.to_broadcast([P, m4, w]), ALU.is_equal))
                    link(tt(dst, dst, orders.unsqueeze(1).to_broadcast([P, m4, w]), ALU.mult))
                    link(nc.vector.tensor_reduce(gmax, dst, AX.X, ALU.max))
                    link(tt(dst, dst, gmax.to_broadcast([P, m4, w]), ALU.is_equal))

                first_max(hi2, gsc, 4, table("groups"))
                m4v = msk.rearrange("p t (g j) -> p t g j", g=4)
                g4 = hi2.unsqueeze(3).to_broadcast([P, m4, 4, 4])
                link(tt(m4v, s4, g4, ALU.mult))
                link(ts(hi2, hi2, BIG, -BIG, ALU.mult, ALU.add))
                link(tt(m4v, m4v, g4, ALU.add))
                first_max(pick, msk, NE, table("experts"))
                link(stt(msk, pick, -2 * BIG, msk, ALU.mult, ALU.add))
                first_max(pick2, msk, NE, table("experts"))
                link(tt(pick, pick, pick2, ALU.add))
                nt = n // P
                nc.vector.tensor_copy(pickh[:, 0:W].rearrange("p (t e) -> p t e", t=nt), pick).then_inc(*now("picked", l))
                link(tt(comb, pick, aff, ALU.mult))
                link(nc.vector.tensor_reduce(gmax, comb, AX.X, ALU.add))
                link(nc.vector.reciprocal(gmax, gmax))
                link(tt(comb, comb, gmax.to_broadcast([P, m4, NE]), ALU.mult))
                c3 = comb3.rearrange("p (e t q) -> p e t q", e=NE, t=4)[:, :, 0:nt, :]
                byexp, rest = comb.rearrange("p t e -> p e t"), msk.rearrange("p t e -> p (t e)").rearrange("p (e t) -> p e t", e=NE)
                link(nc.vector.tensor_copy(c3[:, :, :, 0], byexp))
                link(tt(rest, byexp, c3[:, :, :, 0], ALU.subtract))
                link(nc.vector.tensor_copy(c3[:, :, :, 1], rest))
                link(tt(rest, rest, c3[:, :, :, 1], ALU.subtract))
                link(nc.vector.tensor_copy(c3[:, :, :, 2], rest))
                dve.wait_ge(*after("ranked", l))
                rk = rank.rearrange("p (r e t) -> p r e t", r=4, e=NE)
                base_rank = rk[:, 0, :, 0:nt]
                link(stt(base_rank, ps[3][:, 0:W].rearrange("p (t e) -> p e t", t=nt), 1.0, pick.rearrange("p t e -> p e t"),
                         ALU.add, ALU.mult))
                link(ts(base_rank, base_rank, -1.0, None, ALU.add))
                for r in range(1, 4):
                    link(ts(rk[:, r, :, 0:nt], base_rank, -float(SLOTS * r), None, ALU.add))
                for w in (flagA, flagB):
                    link(nc.vector.memset(w, 0.0))
                cur, other = flagA, flagB
                link(tt(cur[:, 32:].rearrange("p (r e) -> p r e", r=3),
                        ps[3][:, 4 * NE:5 * NE].unsqueeze(1).to_broadcast([P, 3, NE]),
                        table("limit").rearrange("p (r e) -> p r e", r=3), ALU.is_gt))
                flag = hits[:, 0:SPARE]
                link(nc.vector.tensor_copy(flag, cur[:, 32:]))
                for step in (1, 2, 4, 8, 16, 32):
                    link(tt(other[:, 32:], cur[:, 32:], cur[:, 32 - step:32 + SPARE - step], ALU.add))
                    cur, other = other, cur
                link(tt(cur[:, 32:], cur[:, 32:], flag, ALU.mult))
                hv = hits.rearrange("p (j i) -> p j i", j=MORE)
                places = cur[:, 32:].unsqueeze(1).to_broadcast([P, MORE, SPARE])
                js = table("count").unsqueeze(2).to_broadcast([P, MORE, SPARE])
                listed = other[:, 0:2 * MORE]
                for q, name in enumerate(("row", "expert_of")):
                    link(tt(hv, places, js, ALU.is_equal))
                    link(tt(hv, hv, table(name).unsqueeze(1).to_broadcast([P, MORE, SPARE]), ALU.mult))
                    link(nc.vector.tensor_reduce(listed[:, q * MORE:q * MORE + MORE], hv, AX.X, ALU.add))
                nc.vector.tensor_copy(spare_list[:, 0:2 * MORE], listed).then_inc(*now("spare_listed", l))

                su0, _ = expert_unit(l, 0, 0)

                def split_expert(e, i, off):
                    dve.wait_ge(s_hi, e * 2 + (su0 + i + 2 * off + 1))
                    tt(wlo[:, i, :], stage[:, i, :], whi[:, i, :], ALU.subtract).then_inc(s_lo, 1)

                def choose(places):
                    return tt(sel[:, 0:nt, :], table("iota").unsqueeze(1).to_broadcast([P, nt, SLOTS]),
                              rank[:, places].unsqueeze(2).to_broadcast([P, nt, SLOTS]), ALU.is_equal)

                def input_lo(half):
                    c = slice(4 * half, 4 * half + 4)
                    return tt(he[:, c, 1, :], ps[half][:, :].rearrange("p (k t) -> p k t", k=4), he[:, c, 0, :], ALU.subtract)

                def result_lo(half):
                    c = slice(512 * half, 512 * half + 512)
                    return stt(yR[:, 1, c], ps[4 + half][:, :], csum, yR[:, 0, c], ALU.mult, ALU.subtract)

                def add(bank, c):
                    for st in range(ns):
                        cs = slice(st * 256, st * 256 + 256)
                        q = stt(xT[:, c, cs], ps[bank][:, cs], modc[:, 40 + c, st:st + 1], xT[:, c, cs], ALU.mult, ALU.add)
                    return q

                def chosen(e, off):
                    e4 = bass.ds(e * 4 + 4 * off, nt) if not isinstance(e, int) else slice(4 * (e + off), 4 * (e + off) + nt)
                    choose(e4).then_inc(X["tokens_chosen"], 1)

                def gathered(e, off):
                    for half in range(2):
                        dve.wait_ge(X["input_hi"], reached(l, e, 2, 2 * off + half))
                        input_lo(half).then_inc(X["input_lo"], 1)

                def adds(e, off):
                    for c in range(KD):
                        dve.wait_ge(X["scattered"], reached(l, e, 8, 8 * off + c))
                        if not (isinstance(e, int) and e + off == 0):
                            dve.wait_ge(X["added"], reached(l, e, 8, 8 * off - 8 + c))
                        add(6 + c % 2, c).then_inc(X["added"], 1)

                def expert(e, first=False, last_one=False):
                    if not first:
                        adds(e, -1)
                    dve.wait_ge(X["choice_turned"], reached(l, e))
                    nc.vector.tensor_reduce(csum, ps[5][:, 0:3], AX.X, ALU.add).then_inc(X["weight_ready"], 1)
                    if not last_one:
                        chosen(e, 1)
                        split_expert(e, 0, 1)
                    dve.wait_ge(X["gate_silu"], reached(l, e))
                    dve.wait_ge(X["up_mm"], reached(l, e))
                    tt(hid, sg, ps[3][:, :], ALU.mult).then_inc(X["hidden"], 1)
                    if not last_one:
                        split_expert(e, 1, 1)
                        gathered(e, 1)
                    dve.wait_ge(X["weight_ready"], reached(l, e))
                    for half in range(2):
                        dve.wait_ge(X["result_hi"], reached(l, e, 2, half))
                        result_lo(half).then_inc(X["result_lo"], 1)

                chosen(0, 0)
                gathered(0, 0)
                expert(0, True)
                expert(1)
                with dve.Fori(2, NE - 1) as e:
                    expert(e)
                nc.vector.memset(small[:, 63:64], 0.0).then_inc(spare_dve(l), 1)
                expert(NE - 1, False, True)
                adds(NE - 1, 0)

                dve.wait_ge(*after("spare_listed", l))
                dve.wait_ge(X["added"], reached(l, NE - 1, 8, 7))
                with dve.Fori(0, MORE) as j:
                    row = dve.value_load(spare_list[0:1, bass.ds(j, 1)], min_val=0, max_val=SPARE + NE - 1)
                    with dve.If(row > 0):
                        choose(bass.ds(row * 4, nt)).then_inc(spare_dve(l), 1)
                        for i in range(2):
                            dve.wait_ge(spare_act(l), j * SPARE_ACT + (1 + i))
                            tt(wlo[:, i, :], stage[:, i, :], whi[:, i, :], ALU.subtract).then_inc(spare_dve(l), 1)
                        dve.wait_ge(spare_act(l), j * SPARE_ACT + 3)
                        input_lo(0)
                        input_lo(1).then_inc(spare_dve(l), 1)
                        dve.wait_ge(spare_pe(l), j * SPARE_PE + 2)
                        nc.vector.tensor_reduce(csum, ps[5][:, 0:3], AX.X, ALU.add).then_inc(spare_dve(l), 1)
                        dve.wait_ge(spare_act(l), j * SPARE_ACT + 5)
                        tt(hid, sg, ps[3][:, :], ALU.mult).then_inc(spare_dve(l), 1)
                        dve.wait_ge(spare_dve(l), j * SPARE_DVE + 7)
                        dve.wait_ge(spare_act(l), j * SPARE_ACT + 6)
                        result_lo(0)
                        result_lo(1).then_inc(spare_dve(l), 1)
                        dve.wait_ge(spare_pe(l), j * SPARE_PE + 5)
                        for c in range(KD):
                            last = add(c, c)
                        last.then_inc(spare_dve(l), 1)
                        dve.wait_ge(spare_dve(l), j * SPARE_DVE + (SPARE_DVE + 1))
                        nc.vector.memset(small[:, 63:64], 0.0)
                nc.vector.memset(small[:, 62:63], 0.0).then_inc(*now("moe_added", l))

    return found


def host_tables():
    f = np.float32
    t = np.arange(LX, dtype=np.float64)
    fr = np.arange(256, dtype=np.float64)
    k_ang = 2 * np.pi * np.outer(t, fr + 0.5) / 512
    s_ang = 2 * np.pi * np.outer(t + 0.5, fr + 0.5) / 512

    def two(a):
        return np.ascontiguousarray(a.astype(f).reshape(2, P, 256).transpose(1, 0, 2))

    rows = LX // GRID_W
    row = np.repeat(np.arange(rows, dtype=f), GRID_W)
    col = np.tile(np.arange(GRID_W, dtype=f), rows)
    nf = ROPE // 4
    inv = (f(10000.0) ** (-np.arange(nf, dtype=f) / f(nf))).astype(f)
    ang = np.concatenate([row[:, None] * inv, col[:, None] * inv], axis=-1)
    rope = np.zeros((QK, 2, LX), f)
    rope[:NOPE, 0] = 1
    rope[NOPE:, 0] = np.repeat(np.cos(ang).astype(f), 2, axis=1).T
    rope[NOPE:, 1] = np.repeat(np.sin(ang).astype(f), 2, axis=1).T
    rot = np.zeros((QK, QK), f)
    for j in range(NOPE, QK, 2):
        rot[j + 1, j] = -1
        rot[j, j + 1] = 1
    tu = (np.arange(LX, dtype=f) / f(LX - 1)).astype(f)
    bands = np.linspace(1e-4, BANDS - 1, BANDS, dtype=f)
    a = (f(2 * np.pi / LX) * np.arange(LX, dtype=f))[:, None] * bands[None]
    zt = np.concatenate([tu[:, None], np.cos(a), -np.sin(a)], axis=-1).astype(f).T
    r, e = np.divmod(np.arange(SPARE), NE)
    tables = np.tile(np.concatenate([np.arange(4, 0, -1), np.arange(NE, 0, -1), np.arange(SLOTS), SLOTS * (r + 1),
                                     NE * (r + 1) + e, e, np.arange(1, MORE + 1)]).astype(f), (P, 1))
    eye = np.eye(P, dtype=f)
    halves = np.stack([eye, np.triu(np.ones((P, P), f), 1), np.ones((P, P), f)], axis=1)
    return {"cosk": two(np.cos(k_ang)), "sink": two(np.sin(k_ang)), "cos_s": two(np.cos(s_ang)), "sin_s": two(np.sin(s_ang)),
            "rope": rope, "rot": rot, "zT": np.ascontiguousarray(zt), "tneg": -tu[None], "halves": halves,
            "tables": tables, "ident": np.eye(P, dtype=f), "ones": np.ones((P, P), f)}


def host_layout(a):
    f = np.float32

    def chunks(v):
        v = np.asarray(v)
        return np.moveaxis(v.reshape(*v.shape[:-1], -1, P), -1, 0)

    def short(v):
        o = np.zeros((P, 1), f)
        o[:v.shape[0], 0] = v
        return o

    cols = np.zeros((P, DEPTH, NCOLS), f)
    for l in range(DEPTH):
        def put(name, v):
            s, e = COLS[name]
            cols[:, l, s:e] = v.reshape(P, e - s)

        put("g1", np.repeat(chunks(a["norm1_g"][l]), 2, axis=1))
        put("g2", np.repeat(chunks(a["norm2_g"][l]), 2, axis=1))
        put("bmod", np.repeat(chunks(a["b_mod"][l]), 2, axis=1))
        put("gqa", chunks(a["g_qa"][l]))
        put("gkva", chunks(a["g_kva"][l]))
        put("gqn", short(a["g_qn"][l]))
        put("gkn", short(a["g_kn"][l]))
        put("convw", chunks(a["hy_conv_w"][l]))
        put("convb", chunks(a["hy_conv_b"][l]))
        put("hybias", chunks(a["hy_bias"][l]))
        put("gmg", chunks(a["gm_norm_g"][l]))
        put("b1", short(a["hy_b1"][l]))
        put("b2", short(a["hy_b2"][l]))
        put("freq", short(a["hy_freq"][l]))
    fw = np.zeros((DEPTH, P, FW), f)
    fw[:, :EMB, 0:HID] = a["hy_w1"]
    fw[:, :HID, HID:2 * HID] = a["hy_w2"]
    fw[:, :HID, 2 * HID:] = a["hy_w3"]
    fw[:, HID, 2 * HID:] = a["hy_b3"]
    c = np.ascontiguousarray
    return {
        "cT": c(np.stack([chunks(a["c"][0]), chunks(a["c_ctx"])], axis=-1)),
        "cols": cols, "fw": fw, "decay": c(a["hy_decay"].reshape(DEPTH, 2 * HY)),
        "xT": c(a["x"][0].T.reshape(KD, P, LX).transpose(1, 0, 2)),
        "ctxT": c(a["ctx"][0].T.reshape(KD, P, LC).transpose(1, 0, 2)),
        "rw": c(a["router_w"].reshape(KD, P, NE).transpose(1, 0, 2)),
        "rb": c(np.broadcast_to(a["router_b"], (P, NE))),
        "ws": c(a["gm_ws"].transpose(0, 3, 1, 2)), "bs": c(a["gm_bs"].reshape(DEPTH, GROUPS * P)),
        **{k: a[k] for k in ("w_mod", "w_in", "w_uq", "w_ukv", "w_pa", "w_pb", "w_pc", "w_out",
                             "moe_w_gate", "moe_w_up", "moe_w_down")},
    }


def kernel(**inputs):
    import concourse.bacc as bacc
    from concourse.bass_utils import run_bass_kernel_spmd

    a = {k: np.asarray(v) for k, v in inputs.items()}
    arrays = host_layout(a)
    arrays.update(host_tables())
    arrays["halves"] = arrays["halves"].astype(mybir.dt.np(BF16))

    def program(known):
        nc = bacc.Bacc("TRN2", target_bir_lowering=False, num_devices=1)
        ins = {k: nc.dram_tensor(f"in_{k}", v.shape, mybir.dt.from_np(v.dtype), kind="ExternalInput").ap()
               for k, v in arrays.items()}
        out = nc.dram_tensor("out_xT", (P, KD, LX), F32, kind="ExternalOutput").ap()
        return nc, build(nc, ins, out, known)

    _, known = program(None)
    nc, _ = program(known)
    r = run_bass_kernel_spmd(nc, [{f"in_{k}": v for k, v in arrays.items()}], core_ids=[0])
    o = r.results[0]["out_xT"]
    return np.ascontiguousarray(o.transpose(2, 1, 0).reshape(1, LX, D))
```

```python
from contextlib import ExitStack

import numpy as np

import concourse.bass as bass
from concourse import mybir

F32 = mybir.dt.float32
BF16 = mybir.dt.bfloat16
ALU = mybir.AluOpType
ACT = mybir.ActivationFunctionType
AX = mybir.AxisListType

P = 128
D = 1024
KD = D // P
DEPTH = 2
LX = 256
LC = 256
T = LX + LC
GRID_W = 64
EPS = 1e-6
HEADS, NOPE, ROPE, VD = 8, 64, 32, 64
QK = NOPE + ROPE
QR, KVR = 384, 256
HY = 256
BANDS = 16
EMB = 1 + 2 * BANDS
HID = 64
GM = 256
GROUPS = 4
OFF_KV = QR
OFF_HY = QR + KVR + ROPE
OFF_GM = OFF_HY + 3 * HY
OFF_GT = OFF_GM + 2 * GM
NE, FE = 16, 512
KF = FE // P
SCALE = float(QK) ** -0.5
UNIT = 4096
RING = 3
BIG = 1e30
SLOTS = P
SPARE = 3 * NE
MORE = 2 * T // SLOTS - 1
TABLES = {}
_at = 0
for _name, _n in (("groups", 4), ("experts", NE), ("iota", SLOTS), ("limit", SPARE), ("row", SPARE),
                  ("expert_of", SPARE), ("count", MORE)):
    TABLES[_name] = (_at, _at + _n)
    _at += _n
NTABLE = _at
ROUND = 12582912.0
TWO_PI_HI = 6.28125
TWO_PI_LO = float(np.float32(2 * np.pi - 6.28125))

COLS = {}
_at = 0
for _name, _n in (("g1", 16), ("g2", 16), ("bmod", 96), ("gqa", 3), ("gkva", 2), ("gqn", 1), ("gkn", 1),
                  ("convw", 18), ("convb", 6), ("hybias", 2), ("gmg", 2), ("b1", 1), ("b2", 1), ("freq", 1)):
    COLS[_name] = (_at, _at + _n)
    _at += _n
NCOLS = _at
FW = 2 * HID + 2 * HY

MIX_UNITS = ["q", "kv", "uq", "ukv", "hy0", "hy1", "hy2", "gm", "p0", "gt00", "gt01", "gt02",
             "p1", "gt10", "gt11", "gt12", "out0", "out1"]
NMOD = 12
NMIX = len(MIX_UNITS)
NEXP = 3 * NE
SEQ = ([("mod", g) for g in range(4)] + [("mix", i) for i in range(4)] + [("mod", g) for g in range(4, NMOD)]
       + [("mix", i) for i in range(4, NMIX)])
NSPLIT = NMIX + 2 * NE


def build(nc, ins, out, known):
    counts, found = {}, {}
    ctx = ExitStack()
    with ctx:
        def sb(name, shape, dt=F32):
            return ctx.enter_context(nc.sbuf_tensor(name, shape, dt))

        stage = sb("stage", [P, RING, UNIT])
        whi = sb("whi", [P, RING, UNIT], BF16)
        wlo = sb("wlo", [P, RING, UNIT], BF16)
        xT = sb("xT", [P, KD, T])
        h = sb("h", [P, KD, 2, T], BF16)
        cos_s = sb("cos_s", [P, 2, 256])
        sin_s = sb("sin_s", [P, 2, 256])
        ident = sb("ident", [P, P])
        ones = sb("ones", [P, P])
        rope = sb("rope", [QK, 2, LX])
        rot = sb("rot", [QK, QK])
        rw = sb("rw", [P, KD, NE])
        rb = sb("rb", [P, NE])
        tables = sb("tables", [P, NTABLE])
        halves = sb("halves", [P, 3, P], BF16)
        cols = sb("cols", [P, DEPTH, NCOLS])
        cT = sb("cT", [P, KD, 2])
        chl = sb("chl", [P, KD, 2, 2], BF16)
        modc = sb("modc", [P, 48, 2])
        gs = sb("gs", [P, 2, KD, 2])
        ws = sb("ws", [P, GROUPS, P])
        bs = sb("bs", [1, GROUPS * P])
        kfilt = sb("kfilt", [P, DEPTH, 2, 2, HY])
        small = sb("small", [P, 64])
        arena = sb("arena", [P, 52 * 256])
        ps = [ctx.enter_context(nc.psum_tensor(f"bank{i}", [P, 512], F32)) for i in range(8)]

        def kb(a, b):
            return arena[:, a * 256:b * 256]

        def pair(a, n):
            return kb(a, a + 2 * n).bitcast(BF16).rearrange("p (c s t) -> p c s t", c=n, s=2)

        def f32v(a, b, **dims):
            n = list(dims.values())
            if len(n) == 1:
                return kb(a, b).rearrange("p (a t) -> p a t", a=n[0])
            return kb(a, b).rearrange("p (a b t) -> p a b t", a=n[0], b=n[1])

        aT, bT, mT = pair(0, 4), pair(8, 2), pair(12, 2)
        norm_sq, norm_rstd, norm_h = ((f32v(0, 4, n=2), f32v(16, 20, n=2)), (kb(4, 6), kb(20, 22)),
                                      (f32v(6, 10, n=2), f32v(22, 26, n=2)))
        norm_bank = (3, 1)
        pT, tmp = f32v(8, 12, n=4), f32v(12, 16, n=2)
        qn, kvn = pair(16, 3), pair(22, 2)
        kr, V = kb(26, 28), f32v(28, 36, n=4)
        qh, kh = f32v(36, 40, n=2), f32v(40, 44, n=2)
        prob = f32v(44, 48, n=2)
        rq = f32v(48, 52, n=2)
        pq, pkv = f32v(36, 42, n=3), f32v(44, 48, n=2)
        z = f32v(16, 28, n=6)
        pad = arena[:, 28 * 256:28 * 256 + 2 * 2 * 258].rearrange("p (b s t) -> p b s t", b=2, s=2)
        uR, U, Y = f32v(33, 35, n=2), f32v(35, 39, n=2, m=2), f32v(39, 43, n=2, m=2)
        hyt = f32v(43, 47, n=2, m=2)
        hyb = f32v(47, 49, n=2)
        gl, gsq, grs = f32v(24, 32, n=4), f32v(12, 16, n=2), kb(49, 51)
        vn, vR, gmt = gl[:, 2:4], f32v(12, 16, n=4), gl[:, 0:2]
        br, sig = f32v(16, 40, n=3, m=4), f32v(40, 44, n=2)
        ylo4, yhi4 = pair(44, 4), pair(0, 4)
        hR = kb(0, 16).bitcast(BF16).rearrange("p (t s c) -> p t s c", t=4, s=2)
        he = kb(16, 20).bitcast(BF16).rearrange("p (k s t) -> p k s t", k=KD, s=2)
        sel = kb(20, 21).bitcast(BF16).rearrange("p (t s) -> p t s", t=4)
        selT = kb(21, 22).bitcast(BF16)
        sg, hid = kb(22, 24), kb(24, 26)
        yR = kb(28, 32).bitcast(BF16).rearrange("p (s c) -> p s c", s=2)
        rank = kb(32, 33)
        comb3, pickh = kb(33, 34).bitcast(BF16)[:, 0:NE * 4 * 3], kb(34, 35).bitcast(BF16)[:, 0:4 * NE]
        csum = kb(35, 36)[:, 0:1]
        spare_list = kb(36, 37).bitcast(mybir.dt.int32)
        flagA, flagB, hits = kb(37, 38)[:, 0:32 + SPARE], kb(38, 39)[:, 0:32 + SPARE], kb(39, 41)[:, 0:MORE * SPARE]
        lgT, rt = kb(44, 46), kb(46, 48)
        fw = kb(16, 19)[:, 0:FW]
        zT, tneg = kb(19, 20), kb(20, 21)
        cosk, sink = f32v(21, 23, n=2), f32v(23, 25, n=2)
        fa, fk, fr_, fh = kb(25, 26), kb(26, 27), kb(27, 28), f32v(28, 30, n=2)
        dec, decay, kf = kb(30, 32), f32v(32, 36, n=2), f32v(36, 40, n=2)
        ksq, krs, kab = f32v(40, 44, n=2), kb(44, 45), f32v(45, 49, n=2, m=2)

        sems = {}

        def sem_of(kind):
            if kind not in sems:
                sems[kind] = ctx.enter_context(nc.semaphore(kind))
            return sems[kind]

        def now(kind, *which, by=1):
            counts[kind] = counts.get(kind, 0) + by
            assert (kind, *which) not in found, (kind, which)
            found[(kind, *which)] = counts[kind]
            return sem_of(kind), by

        def after(kind, *which):
            if known is None:
                return sem_of(kind), 1
            return sem_of(kind), known[(kind, *which)]

        s_stage = [sem_of(f"stage_loaded{i}") for i in range(RING)]
        s_hi, s_lo, s_used = sem_of("hi_split"), sem_of("lo_split"), sem_of("unit_used")
        s_mod, s_mod_hi, s_mod_lo = sem_of("mod_unit_used"), sem_of("mod_hi_split"), sem_of("mod_lo_split")

        def mod_slot(g):
            return g % RING if g < 4 else 1


        def dma_unit(l, i):
            return l * (NMOD + NMIX + NEXP) + i

        def where(i):
            return SEQ.index(("mix", i)) if i < NMIX else NMOD + i

        def mix_unit(l, i):
            return l * NSPLIT + i, dma_unit(l, where(i))

        def expert_unit(l, e, i):
            return l * NSPLIT + NMIX + 2 * e + i, dma_unit(l, NMOD + NMIX + 3 * e + i)

        def col(l, name):
            a, b = COLS[name]
            return cols[:, l, a:b]

        def unit_source(l, name):
            w = ins["w_in"][l]
            if name == "q":
                return [(0, 8 * QR, w[:, 0:QR], 8)]
            if name == "kv":
                return [(0, 8 * (KVR + ROPE), w[:, OFF_KV:OFF_HY], 8)]
            if name == "uq":
                return [(0, 3 * HEADS * QK, ins["w_uq"][l], 3)]
            if name == "ukv":
                return [(0, 2 * HEADS * (NOPE + VD), ins["w_ukv"][l], 2)]
            if name[:2] == "hy":
                a = OFF_HY + 256 * int(name[2])
                return [(0, 8 * 256, w[:, a:a + 256], 8)]
            if name == "gm":
                return [(0, UNIT, w[:, OFF_GM:OFF_GT], 8)]
            if name[0] == "p":
                c = slice(512 * int(name[1]), 512 * int(name[1]) + 512)
                return [(0, 2048, ins["w_pa"][l][:, c], 4), (2048, 3072, ins["w_pb"][l][:, c], 2),
                        (3072, 4096, ins["w_pc"][l][:, c], 2)]
            if name[:2] == "gt":
                a = OFF_GT + D * int(name[3]) + 512 * int(name[2])
                return [(0, UNIT, w[:, a:a + 512], 8)]
            return [(0, UNIT, ins["w_out"][l][:, 512 * int(name[3]):512 * int(name[3]) + 512], 8)]

        def unit_width(l, name):
            return max(b for _, b, _, _ in unit_source(l, name))

        block = ctx.enter_context(nc.Block())

        def spare_loaded(l):
            return sem_of(f"spare_loaded{l}")

        def spare_blocks(l):
            return 2 * (T if l == 0 else LX) // SLOTS - 1

        def spare_down_loaded(l):
            return sem_of(f"spare_down_loaded{l}")

        def spare_pe(l):
            return sem_of(f"spare_tensor{l}")

        def spare_act(l):
            return sem_of(f"spare_scalar{l}")

        def spare_dve(l):
            return sem_of(f"spare_vector{l}")

        SPARE_PE, SPARE_ACT, SPARE_DVE = 5, 6, 8

        def reached(l, e, per=1, i=0):
            return e * per + (l * NE * per + i + 1)

        X = {k: sem_of("expert_" + k) for k in (
            "tokens_chosen", "gathered", "input_hi", "input_lo", "gate_mm", "up_mm", "gate_silu", "hidden", "choice_turned", "choice_copied", "weight_ready", "down_mm", "result_hi", "result_lo",
            "scattered", "added")}
        ident_h, before_h, ones_h = halves[:, 0, :], halves[:, 1, :], halves[:, 2, :]

        def table(name):
            a, b = TABLES[name]
            return tables[:, a:b]

        @block.sync
        def _(sp):
            for l in range(DEPTH):
                def mod_source(g):
                    return ins["w_mod"][l].rearrange("(k p) (g n) -> g p k n", p=P, n=512)[g]

                for k, (dst, src) in enumerate((
                        (zT[0:EMB, :], ins["zT"]), (fw, ins["fw"][l]), (tneg[0:1, :], ins["tneg"]),
                        (dec[0:1, :], ins["decay"][l:l + 1]), (cosk, ins["cosk"]), (sink, ins["sink"]))):
                    sp.dma_start(dst, src).then_inc(*now("filter_loaded", l, k, by=16))
                    if l == 0 and k == 1:
                        for q, (d, small_src) in enumerate(((cols[:], ins["cols"]), (cT[:], ins["cT"]), (ident[:], ins["ident"]),
                                                            (ones[:], ins["ones"]))):
                            sp.dma_start(d, small_src).then_inc(*now("small_loaded", q, by=16))
                for p, (kind, i) in enumerate(SEQ):
                    n = dma_unit(l, p)
                    if p >= RING:
                        k0, i0 = SEQ[p - RING]
                        if k0 == "mod":
                            sp.wait_ge(s_mod_lo, l * NMOD + i0 + 1)
                        else:
                            sp.wait_ge(s_lo, mix_unit(l, i0)[0] + 1)
                    if kind == "mod":
                        sp.dma_start(stage[:, n % RING, :].rearrange("p (k n) -> p k n", k=8),
                                     mod_source(i)).then_inc(s_stage[n % RING], 16)
                        continue
                    name = MIX_UNITS[i]
                    parts = unit_source(l, name)
                    for j, (a, b, src, k) in enumerate(parts):
                        ins_ = sp.dma_start(stage[:, n % RING, a:b].rearrange("p (k n) -> p k n", k=k),
                                            src.rearrange("(k p) n -> p k n", p=P))
                        ins_.then_inc(s_stage[n % RING], 16)
                gate, up, down = (ins[w][l].rearrange("e (k p) n -> e p k n", p=P)
                                  for w in ("moe_w_gate", "moe_w_up", "moe_w_down"))
                su0, _ = expert_unit(l, 0, 0)

                def fetch_expert(e, i, w, k):
                    if isinstance(e, int) and e == 0:
                        sp.wait_ge(s_lo, su0 + i - RING + 1)
                    elif i == 2:
                        sp.wait_ge(X["down_mm"], reached(l, e, 2, -1))
                    else:
                        sp.wait_ge(s_lo, e * 2 + (su0 + i - 1))
                    src = w[e] if isinstance(e, int) else w[bass.ds(e, 1)].rearrange("a p k n -> (a p) k n")
                    sp.dma_start(stage[:, i, :].rearrange("p (k n) -> p k n", k=k), src).then_inc(s_stage[i], 16)

                fetch_expert(0, 0, gate, 8)
                fetch_expert(0, 1, up, 8)
                fetch_expert(0, 2, down, 4)
                fetch_expert(1, 0, gate, 8)
                fetch_expert(1, 1, up, 8)
                with sp.Fori(2, NE) as e:
                    fetch_expert(e, 0, gate, 8)
                    fetch_expert(e - 1, 2, down, 4)
                    fetch_expert(e, 1, up, 8)
                fetch_expert(NE - 1, 2, down, 4)
                sp.wait_ge(s_lo, su0 + 2 * NE)
                sp.wait_ge(*after("spare_listed", l))
                with sp.Fori(0, spare_blocks(l)) as j:
                    row = sp.value_load(spare_list[0:1, bass.ds(j, 1)], min_val=0, max_val=SPARE + NE - 1)
                    e = sp.value_load(spare_list[0:1, bass.ds(j + MORE, 1)], min_val=0, max_val=NE - 1)
                    with sp.If(row > 0):
                        sp.wait_ge(spare_dve(l), j * SPARE_DVE + 1)
                        for i, (w, k) in enumerate(((gate, 8), (up, 8), (down, 4))):
                            if i == 2:
                                sp.wait_ge(X["down_mm"], reached(l, NE - 1, 2, 1))
                            sp.dma_start(stage[:, i, :].rearrange("p (k n) -> p k n", k=k),
                                         w[bass.ds(e, 1)].rearrange("a p k n -> (a p) k n")
                                         ).then_inc(spare_loaded(l) if i < 2 else spare_down_loaded(l), 16)
                sp.wait_ge(*after("moe_added", l))
            for k in range(KD):
                if k % 4 == 0:
                    sp.wait_ge(*after("moe_added", DEPTH - 1))
                    sp.dma_start(out[:, k:k + 4, :], xT[:, k:k + 4, 0:LX]).then_inc(*now("stored", k, by=16))
            sp.wait_ge(*after("stored", 4))

        def landed(l, i):
            n = dma_unit(l, i)
            total = 0
            for m in range(n % RING, n + 1, RING):
                kind, j = SEQ[m % (NMOD + NMIX + NEXP)] if m % (NMOD + NMIX + NEXP) < len(SEQ) else ("expert", 0)
                parts = 3 if kind == "mix" and MIX_UNITS[j][0] == "p" else 1
                total += 16 * parts
            return s_stage[n % RING], total

        @block.gpsimd
        def _(pool):
            pool.dma_start(xT[:, :, 0:LX], ins["xT"]).then_inc(*now("x_loaded", 0, by=16))
            pool.dma_start(xT[:, :, LX:T], ins["ctxT"]).then_inc(*now("x_loaded", 1, by=16))
            for k, (dst, src) in enumerate((
                    (cos_s[:], ins["cos_s"]), (sin_s[:], ins["sin_s"]), (rope[:], ins["rope"]),
                    (rot[:], ins["rot"]), (rw[:], ins["rw"]), (rb[:], ins["rb"]), (tables[:], ins["tables"]),
                    (halves[:], ins["halves"]), (ws[:], ins["ws"][0]), (bs[:], ins["bs"][0:1]))):
                pool.dma_start(dst, src).then_inc(*now("const_loaded", k, by=16))
            for l in range(DEPTH):
                if l > 0:
                    pool.wait_ge(*after("gm_spatial", l - 1, 3))
                    pool.dma_start(ws[:], ins["ws"][l]).then_inc(*now("spatial_loaded", l, 0, by=16))
                    pool.dma_start(bs[:], ins["bs"][l:l + 1]).then_inc(*now("spatial_loaded", l, 1, by=16))

        @block.tensor
        def _(pe):
            def mm(o, a, b, start, stop):
                return nc.tensor.matmul(o, a, b, start=start, stop=stop)

            def mm3(o, w, act, first, last):
                mm(o, w[0], act[0], first, False)
                mm(o, w[0], act[1], False, False)
                return mm(o, w[1], act[0], False, last)

            def weights(slot, k, kn, a, b, base=0):
                w = kn
                return (whi[:, slot, base + k * w + a:base + k * w + b], wlo[:, slot, base + k * w + a:base + k * w + b])

            def project(o, slot, width, a, b, n, hn=None, nk=8, base=0, act=None):
                act = h if act is None else act
                for k in range(nk):
                    last = mm3(o, weights(slot, k, width, a, b, base), (act[:, k, 0, 0:n], act[:, k, 1, 0:n]),
                               k == 0, k == nk - 1)
                return last

            def modulation(l, g, m):
                if m == 0:
                    pe.wait_ge(s_mod_lo, l * NMOD + g + 1)
                    if g == 0 and l == 0:
                        pe.wait_ge(*after("c_split"))
                at = g * 8 + m * 2
                o = ps[1][:, at:at + 2] if g < 4 else ps[7][:, 256 + at:258 + at]
                for k in range(KD):
                    last = mm3(o, weights(mod_slot(g), k, 512, m * P, m * P + P), (chl[:, k, 0, :], chl[:, k, 1, :]),
                               k == 0, k == KD - 1)
                if m == 3:
                    last.then_inc(s_mod, 1)

            for l in range(DEPTH):
                n = T if l == 0 else LX
                if l == 0:
                    pe.wait_ge(*after("small_loaded", 3))
                else:
                    pe.wait_ge(*after("moe_added", l - 1))

                def modulate(g):
                    for m in range(4):
                        modulation(l, g, m)

                pe.wait_ge(*after("filter_loaded", l, 5))
                mm(ps[0][0:HID, 0:256], fw[0:EMB, 0:HID], zT[0:EMB, 0:256], True, True).then_inc(*now("filt_mm", l, 0))
                pe.wait_ge(*after("filt_sin", l, 0))
                mm(ps[0][0:HID, 256:512], fw[0:HID, HID:2 * HID], fh[0:HID, 0, :], True, True).then_inc(*now("filt_mm", l, 1))
                modulate(0)
                pe.wait_ge(*after("filt_sin", l, 1))
                pe.wait_ge(*after("decay_abs", l))
                for c in range(2):
                    mm(ps[2 + c][:, :], fh[0:HID + 1, 1, c * P:c * P + P], fw[0:HID + 1, 2 * HID:FW], True, True)
                    mm(ps[4 + c][:, :], tneg[0:1, c * P:c * P + P], dec[0:1, :], True, True).then_inc(*now("filt_mm", l, 2 + c))
                modulate(1)
                for c in range(2):
                    pe.wait_ge(*after("filt_sq", l, c))
                    for d in range(2):
                        last = mm(ps[0][:, 0:256], ones[:], ksq[:, c, d * HY:d * HY + HY], c == 0 and d == 0, c == 1 and d == 1)
                last.then_inc(*now("filt_ssq", l))
                modulate(2)
                pe.wait_ge(*after("filt_ab", l))
                for f in range(2):
                    for part, table in ((0, cosk), (1, sink)):
                        for c in range(2):
                            last = mm(ps[6 + f][:, part * 256:part * 256 + 256], table[:, c, f * P:f * P + P],
                                      kab[:, part, c, :], c == 0, c == 1)
                    last.then_inc(*now("filt_spec", l, f))

                def norm_sum(which):
                    m = T if which == 0 else n
                    for k in range(KD):
                        if which == 1 and k == 0:
                            pe.wait_ge(*after("x_mixed", l, 7))
                        pe.wait_ge(*after("x_squared", l, which, k))
                        mm(ps[norm_bank[which]][:, 0:m], ones[:], norm_sq[which][:, k % 2, 0:m], k == 0, k == KD - 1).then_inc(*now("x_summed", l, which, k))

                norm_sum(0)
                modulate(3)

                def unit(i):
                    su, _ = mix_unit(l, i)
                    pe.wait_ge(s_lo, su + 1)
                    return i % RING

                s = unit(0)
                for k in range(KD):
                    pe.wait_ge(*after("h_ready", l, 0, k))
                    last = mm3(ps[2][:, 0:n], weights(s, k, QR, 0, P), (h[:, k, 0, 0:n], h[:, k, 1, 0:n]), k == 0, k == KD - 1)
                last.then_inc(*now("q_low", l, 0))
                project(ps[3][:, 0:n], s, QR, P, 2 * P, n).then_inc(*now("q_low", l, 1))
                project(ps[4][:, 0:n], s, QR, 2 * P, 3 * P, n).then_inc(s_used, 1)
                mm(ps[0][0:1, 0:1], ones[:, 0:1], ones[:, 0:1], True, True).then_inc(*now("q_low", l, 2))

                def q_low_sum(m):
                    pe.wait_ge(*after("q_low_sq", l, m))
                    mm(ps[0][:, 0:n], ones[:], tmp[:, m % 2, 0:n], m == 0, m == 2).then_inc(*now("q_low_sum", l, m))

                s = unit(1)
                project(ps[5][:, 0:T], s, KVR + ROPE, 0, P, T).then_inc(*now("kv_low", l, 0))
                q_low_sum(0)
                q_low_sum(1)
                project(ps[6][:, 0:T], s, KVR + ROPE, P, 2 * P, T).then_inc(*now("kv_low", l, 1))
                q_low_sum(2)
                o = ps[7][NOPE:QK, 0:T]
                for k in range(8):
                    last = mm3(o, weights(s, k, KVR + ROPE, KVR, KVR + ROPE), (h[:, k, 0, 0:T], h[:, k, 1, 0:T]), k == 0, k == 7)
                last.then_inc(s_used, 1)
                pe.wait_ge(*after("q_low_copied", l, 0))
                mm(ps[2][0:1, 0:1], ones[:, 0:1], ones[:, 0:1], True, True).then_inc(*now("kv_low", l, 2))
                for m in range(2):
                    pe.wait_ge(*after("kv_low_sq", l, m))
                    mm(ps[1][:, 0:T], ones[:], tmp[:, (m + 1) % 2, 0:T], m == 0, m == 1).then_inc(*now("kv_low_sum", l, m))

                sq_, skv = unit(2), unit(3)
                pe.wait_ge(*after("kvn_ready", l))
                for tc in range(4):
                    b = 2 + tc
                    for k in range(2):
                        v = [w[:, skv, k * 1024:k * 1024 + 1024].rearrange("p (h c) -> p h c", h=HEADS)[:, :, NOPE:NOPE + VD]
                             for w in (whi, wlo)]
                        c = slice(tc * P, tc * P + P)
                        mm(ps[b][:, :], kvn[:, k, 0, c], v[0], k == 0, False)
                        mm(ps[b][:, :], kvn[:, k, 1, c], v[0], False, False)
                        last = mm(ps[b][:, :], kvn[:, k, 0, c], v[1], False, k == 1)
                    last.then_inc(*now("v_mm", l, tc))

                def heads_project(i):
                    if i == 0:
                        pe.wait_ge(*after("kvn_ready", l))
                        pe.wait_ge(*after("qn_ready", l))
                    else:
                        pe.wait_ge(*after("q_normed", l, i - 1))
                        pe.wait_ge(*after("k_normed", l, i - 1))
                    for k in range(3):
                        last = mm3(ps[0][0:QK, 0:n], weights(sq_, k, HEADS * QK, i * QK, i * QK + QK),
                                   (qn[:, k, 0, 0:n], qn[:, k, 1, 0:n]), k == 0, k == 2)
                    last.then_inc(*now("q_mm", l, i))
                    for k in range(2):
                        last = mm3(ps[1][0:NOPE, 0:T], weights(skv, k, 1024, i * P, i * P + NOPE),
                                   (kvn[:, k, 0, 0:T], kvn[:, k, 1, 0:T]), k == 0, k == 1)
                    last.then_inc(*now("k_mm", l, i))

                def heads_sum(i):
                    if i == 0:
                        pe.wait_ge(*after("v_copied", l, 1))
                    else:
                        pe.wait_ge(*after("k_roped", l, i - 1))
                    pe.wait_ge(*after("q_squared", l, i))
                    mm(ps[2][0:QK, 0:n], ones[0:QK, 0:QK], tmp[0:QK, 0, 0:n], True, True).then_inc(*now("q_sum", l, i))
                    pe.wait_ge(*after("k_squared", l, i))
                    pe.wait_ge(*after("kr_squared", l))
                    mm(ps[3][0:QK, 0:T], ones[0:QK, 0:QK], tmp[0:QK, 1, 0:T], True, True).then_inc(*now("k_sum", l, i))

                def heads_rotate(i):
                    b = i % 2
                    pe.wait_ge(*after("q_normed", l, i))
                    mm(ps[2][0:QK, 0:LX], rot[:], qh[0:QK, b, 0:LX], True, True).then_inc(*now("q_rot", l, i))
                    pe.wait_ge(*after("k_normed", l, i))
                    mm(ps[3][0:QK, 0:LX], rot[:], kh[0:QK, b, 0:LX], True, True).then_inc(*now("k_rot", l, i))

                tiles = [(0, 0, T), (1, 0, T)] + ([(2, LX, T), (3, LX, T)] if l == 0 else [])

                def scores(i, t):
                    b = i % 2
                    qt, ka, kz = tiles[t]
                    seq = i * len(tiles) + t
                    if t == 0:
                        pe.wait_ge(*after("q_roped", l, i))
                        pe.wait_ge(*after("k_roped", l, i))
                        if i == 0:
                            pe.wait_ge(*after("v_copied", l, 3))
                    if seq >= 2:
                        pe.wait_ge(*after("exp_done", l, seq - 2))
                    mm(ps[4 + seq % 2][:, 0:kz - ka], qh[0:QK, b, qt * P:qt * P + P], kh[0:QK, b, ka:kz],
                       True, True).then_inc(*now("scores", l, seq))

                def turn(i, t):
                    qt, ka, kz = tiles[t]
                    seq = i * len(tiles) + t
                    pe.wait_ge(*after("prob_ready", l, seq))
                    if seq >= 1:
                        pe.wait_ge(*after("prob_turned", l, seq - 1))
                    elif l == 0:
                        pe.wait_ge(*after("kvn_ready", l))
                    for c in range((kz - ka) // P):
                        last = nc.tensor.transpose(ps[6][:, c * P:c * P + P], prob[:, seq % 2, c * P:c * P + P], ident[:])
                    last.then_inc(*now("prob_turn", l, seq))

                def values(i, g):
                    nk = 4 if g == 0 else 2
                    r = (i % 2) * VD
                    seq = i * (len(tiles) // 2) + g
                    if seq >= 1:
                        pe.wait_ge(*after("a_done", l, seq - 1))
                    else:
                        pe.wait_ge(*after("kr_copied", l))
                    pe.wait_ge(*after("prob_turned", l, i * len(tiles) + 2 * g + 1))
                    for c in range(nk):
                        last = mm(ps[7][r:r + VD, 0:LX], V[:, 4 - nk + c, i * VD:i * VD + VD], pT[:, c, :], c == 0, c == nk - 1)
                    last.then_inc(*now("pv", l, seq))

                for i in range(HEADS + 1):
                    if i == 0:
                        heads_project(0)
                    if i > 0:
                        scores(i - 1, 0)
                        scores(i - 1, 1)
                    if i < HEADS:
                        heads_sum(i)
                    if i == 0:
                        pe.wait_ge(*after("kr_copied", l))
                        modulate(4)
                    if i > 0:
                        turn(i - 1, 0)
                        if i < HEADS:
                            if i > 1:
                                pe.wait_ge(*after("a_done", l, (i - 1) * (len(tiles) // 2) - 1))
                            modulate(4 + i)
                        turn(i - 1, 1)
                        if l == 0:
                            scores(i - 1, 2)
                            scores(i - 1, 3)
                        values(i - 1, 0)
                    if i < HEADS:
                        heads_rotate(i)
                    if i + 1 < HEADS:
                        heads_project(i + 1)
                    if i > 0 and l == 0:
                        turn(i - 1, 2)
                        turn(i - 1, 3)
                        values(i - 1, 1)
                    if i == HEADS - 1:
                        pe.wait_ge(*after("q_roped", l, i))
                        mm(ps[2][0:1, 0:1], ones[:, 0:1], ones[:, 0:1], True, True).then_inc(s_used, 1)
                        mm(ps[2][0:1, 0:1], ones[:, 0:1], ones[:, 0:1], True, True).then_inc(s_used, 1)

                for c in range(6):
                    if c % 2 == 0:
                        s = unit(4 + c // 2)
                    pe.wait_ge(*(after("pad_copied", l, c - 2) if c >= 2 else after("k_roped", l, HEADS - 1)))
                    last = project(ps[c % 2][:, 0:n], s, 256, (c % 2) * P, (c % 2) * P + P, n)
                    last.then_inc(*now("hy_mm", l, c))
                    if c % 2:
                        mm(ps[2][0:1, 0:1], ones[:, 0:1], ones[:, 0:1], True, True).then_inc(s_used, 1)
                s = unit(7)
                pe.wait_ge(*after("a_done", l, HEADS * (len(tiles) // 2) - 1))
                pe.wait_ge(*after("mod_added", l, 1))

                def gm_project(c):
                    project(ps[4 + c][:, 0:n], s, 512, c * P, c * P + P, n).then_inc(*now("gm_mm", l, c))
                    if c == 3:
                        mm(ps[2][0:1, 256:257], ones[:, 0:1], ones[:, 0:1], True, True).then_inc(s_used, 1)

                def u_turn(st):
                    if st == 0:
                        pe.wait_ge(*after("u_ready", l))
                    else:
                        pe.wait_ge(*after("uR_copied", l, st - 1))
                    for tc in range(2):
                        for c in range(2):
                            last = nc.tensor.transpose(ps[2][:, tc * 256 + c * P:tc * 256 + c * P + P],
                                                       z[:, 2 + c, st * 256 + tc * P:st * 256 + tc * P + P], ident[:])
                    last.then_inc(*now("u_turned", l, st))

                def u_spectrum(st):
                    pe.wait_ge(*after("uR_copied", l, st))
                    if st == 0:
                        pe.wait_ge(*after("pad_copied", l, 5))
                    else:
                        pe.wait_ge(*after("U_copied", l, st - 1))
                    for part, table in ((0, cos_s), (1, sin_s)):
                        for f in range(2):
                            for tc in range(2):
                                last = mm(ps[part][:, f * 256:f * 256 + 256], table[:, tc, f * P:f * P + P], uR[:, tc, :],
                                          tc == 0, tc == 1)
                    last.then_inc(*now("u_spec", l, st))

                def y_back(st):
                    pe.wait_ge(*after("Y_ready", l, st))
                    if st > 0:
                        pe.wait_ge(*after("b_done", l, st - 1))
                    for c in range(2):
                        q = 0
                        for part, table in ((0, cos_s), (1, sin_s)):
                            for f in range(2):
                                last = mm(ps[3][:, c * 256:c * 256 + 256], Y[:, part, f, c * P:c * P + P], table[:, f, :],
                                          q == 0, q == 3)
                                q += 1
                    last.then_inc(*now("y_back", l, st))

                def gv_sums():
                    for c in range(2):
                        pe.wait_ge(*after("gv_sq", l, c))
                        if c == 0:
                            pe.wait_ge(*after("U_copied", l, n // 256 - 1))
                        mm(ps[0][:, 0:n], ones[:], gsq[:, c, 0:n], c == 0, c == 1).then_inc(*now("gv_sum", l, c))

                gm_project(0)
                gm_project(1)
                u_turn(0)
                gm_project(2)
                u_spectrum(0)
                gm_project(3)
                for st in range(1, n // 256):
                    y_back(st - 1)
                    u_turn(st)
                    u_spectrum(st)
                gv_sums()
                y_back(n // 256 - 1)

                pe.wait_ge(*after("gv_normed", l))
                pe.wait_ge(*after("uR_copied", l, n // 256 - 1))
                for tc in range(n // P):
                    bk = (1, 2)[tc % 2]
                    if tc >= 2:
                        pe.wait_ge(*after("vR_copied", l, tc - 2))
                    for c in range(2):
                        last = nc.tensor.transpose(ps[bk][:, c * P:c * P + P], vn[:, c, tc * P:tc * P + P], ident[:])
                    last.then_inc(*now("gv_turned", l, tc))
                pe.wait_ge(*(after("const_loaded", 9) if l == 0 else after("spatial_loaded", l, 1)))
                pe.wait_ge(*after("gm_gelu", l, 3))
                pe.wait_ge(*after("vR_copied", l, n // P - 1))
                for g in range(GROUPS):
                    r = (g % 2) * 64
                    o = ps[4 + g // 2]
                    for tc in range(n // P):
                        oo = o[r:r + 64, tc * P:tc * P + P]
                        mm(oo, vR[:, tc, g * 64:g * 64 + 64], ws[:, g, :], True, False)
                        last = mm(oo, ones[0:1, 0:64], bs[0:1, g * P:g * P + P], False, True)
                    last.then_inc(*now("gm_spatial", l, g))

                def y_of(half):
                    return ylo4 if half == 0 else yhi4

                chunk = 0
                for half in range(2):
                    s = unit(8 + 4 * half)
                    if half == 0:
                        pe.wait_ge(*after("a_done", l, HEADS * (len(tiles) // 2) - 1))
                        pe.wait_ge(*after("b_done", l, n // 256 - 1))
                        pe.wait_ge(*after("m_done", l, 1))
                        pe.wait_ge(*after("vR_copied", l, n // P - 1))
                    for b, (act, nk, base) in enumerate(((aT, 4, 0), (bT, 2, 2048), (mT, 2, 3072))):
                        for j in range(4):
                            if chunk >= 4:
                                pe.wait_ge(*after("merge_evac", l, chunk - 4))
                            last = project(ps[chunk % 4][:, 0:n], s, 512, j * P, j * P + P, n, nk=nk, base=base, act=act)
                            last.then_inc(*now("branch_mm", l, half, b, j))
                            chunk += 1
                    mm(ps[4][0:1, 0:1], ones[:, 0:1], ones[:, 0:1], True, True).then_inc(s_used, 1)
                    for b in range(3):
                        s = unit(9 + 4 * half + b)
                        for j in range(4):
                            pe.wait_ge(*after("merge_evac", l, chunk - 4))
                            project(ps[chunk % 4][:, 0:n], s, 512, j * P, j * P + P, n).then_inc(*now("gate_mm", l, half, b, j))
                            chunk += 1
                        mm(ps[4][0:1, 0:1], ones[:, 0:1], ones[:, 0:1], True, True).then_inc(s_used, 1)
                for half in range(2):
                    s = unit(16 + half)
                    for j in range(4):
                        c = 4 * half + j
                        pe.wait_ge(*(after("merge_evac", l, chunk - 4) if c < 4 else after("x_mixed", l, c - 4)))
                        for k in range(8):
                            if c == 0:
                                pe.wait_ge(*after("y_ready", l, k))
                            y = y_of(k // 4)
                            last = mm3(ps[chunk % 4][:, 0:n], weights(s, k, 512, j * P, j * P + P),
                                       (y[:, k % 4, 0, 0:n], y[:, k % 4, 1, 0:n]), k == 0, k == 7)
                        last.then_inc(*now("out_mm", l, c))
                        chunk += 1
                    mm(ps[4][0:1, 0:1], ones[:, 0:1], ones[:, 0:1], True, True).then_inc(s_used, 1)

                norm_sum(1)
                pe.wait_ge(*after("x_mixed", l, 7))
                for k in range(KD):
                    pe.wait_ge(*after("hf_ready", l, 1, k))
                    mm(ps[0][0:NE, 0:n], rw[:, k, :], norm_h[1][:, k % 2, 0:n], k == 0, k == KD - 1).then_inc(*now("logits", l, k))
                nt = n // P
                pe.wait_ge(*after("logits_copied", l))
                for tc in range(nt):
                    last = nc.tensor.transpose(ps[2][:, tc * NE:tc * NE + NE], lgT[0:NE, tc * P:tc * P + P], ident[0:NE, 0:NE])
                last.then_inc(*now("logits_turned", l))
                for q in range(nt * 4):
                    tc, sd, half = q // 4, q // 2 % 2, q % 2
                    if q >= 4:
                        pe.wait_ge(*after("tokens_copied", l, q - 4))
                    if q == 0:
                        pe.wait_ge(*after("h_ready", l, 1, 7))
                    for k in range(4):
                        last = mm(ps[4 + q % 4][:, k * P:k * P + P], h[:, 4 * half + k, sd, tc * P:tc * P + P], ident_h, True, True)
                    last.then_inc(*now("tokens_turned", l, q))
                pe.wait_ge(*after("picked", l))
                for tc in range(nt):
                    for t2 in range(tc + 1):
                        mm(ps[3][:, tc * NE:tc * NE + NE], before_h if t2 == tc else ones_h, pickh[:, t2 * NE:t2 * NE + NE],
                           t2 == 0, t2 == tc)
                for tc in range(nt):
                    last = mm(ps[3][:, 4 * NE:5 * NE], ones_h, pickh[:, tc * NE:tc * NE + NE], tc == 0, tc == nt - 1)
                last.then_inc(*now("ranked", l))

                su0, _ = expert_unit(l, 0, 0)

                def gather_mm(k):
                    for tc in range(nt):
                        for sd in range(2):
                            last = mm(ps[k // 4][:, (k % 4) * P:(k % 4) * P + P], hR[:, tc, sd, k * P:k * P + P], sel[:, tc, :],
                                      tc == 0 and sd == 0, tc == nt - 1 and sd == 1)
                    return last

                def turn_mm(weight_at):
                    for tc in range(nt):
                        mm(ps[4][:, tc * P:tc * P + P], sel[:, tc, :], ident_h, True, True)
                    for tc in range(nt):
                        last = mm(ps[5][:, 0:3], sel[:, tc, :], comb3[:, weight_at(tc)], tc == 0, tc == nt - 1)
                    return last

                def expert_in(slot, bank):
                    for m in range(KF):
                        last = project(ps[bank][:, m * P:m * P + P], slot, FE, m * P, m * P + P, P, act=he)
                    return last

                def down_product(half):
                    for k in range(KF):
                        last = mm(ps[4 + half][:, :], hid[:, k * P:k * P + P],
                                  stage[:, 2, k * D + 512 * half:k * D + 512 * half + 512], k == 0, k == KF - 1)
                    return last

                def scatter_mm(bank, c):
                    mm(ps[bank][:, 0:n], yR[:, 0, c * P:c * P + P], selT[:, 0:n], True, False)
                    return mm(ps[bank][:, 0:n], yR[:, 1, c * P:c * P + P], selT[:, 0:n], False, True)

                def gather(e, off):
                    pe.wait_ge(X["tokens_chosen"], reached(l, e, 1, off))
                    for k in range(KD):
                        last = gather_mm(k)
                        if k % 4 == 3:
                            last.then_inc(X["gathered"], 1)

                def scatter(e, off, c):
                    if c == 0:
                        pe.wait_ge(X["result_lo"], reached(l, e, 2, 2 * off + 1))
                    if not (isinstance(e, int) and e + off == 0 and c < 2):
                        pe.wait_ge(X["added"], reached(l, e, 8, 8 * off + c - 2))
                    scatter_mm(6 + c % 2, c).then_inc(X["scattered"], 1)

                def expert(e, first=False, last_one=False):
                    pe.wait_ge(s_lo, e * 2 + (su0 + 1))
                    pe.wait_ge(X["input_lo"], reached(l, e, 2, 1))
                    for m in range(KF):
                        project(ps[2][:, m * P:m * P + P], 0, FE, m * P, m * P + P, P, act=he).then_inc(X["gate_mm"], 1)
                        if not first:
                            scatter(e, -1, 2 * m)
                            scatter(e, -1, 2 * m + 1)
                    turn_mm(lambda tc: bass.ds(e * 12 + tc * 3, 3) if not isinstance(e, int)
                            else slice(e * 12 + tc * 3, e * 12 + tc * 3 + 3)).then_inc(X["choice_turned"], 1)
                    pe.wait_ge(s_lo, e * 2 + (su0 + 2))
                    expert_in(1, 3).then_inc(X["up_mm"], 1)
                    if not last_one:
                        gather(e, 1)
                    pe.wait_ge(X["hidden"], reached(l, e))
                    pe.wait_ge(X["choice_copied"], reached(l, e))
                    pe.wait_ge(X["weight_ready"], reached(l, e))
                    pe.wait_ge(s_stage[2], e * 16 + down_base)
                    for half in range(2):
                        down_product(half).then_inc(X["down_mm"], 1)

                down_base = landed(l, NMOD + NMIX + 2)[1]
                pe.wait_ge(*after("tokens_copied", l, nt * 4 - 1))
                gather(0, 0)
                expert(0, True)
                expert(1)
                with pe.Fori(2, NE - 1) as e:
                    expert(e)
                expert(NE - 1, False, True)
                for i in range(2 * NE // 16):
                    mm(ps[0][0:1, 0:1], ones[:, 0:1], ones[:, 0:1], True, True).then_inc(s_used, 16)
                for c in range(KD):
                    scatter(NE - 1, 0, c)

                pe.wait_ge(*after("spare_listed", l))
                with pe.Fori(0, spare_blocks(l)) as j:
                    row = pe.value_load(spare_list[0:1, bass.ds(j, 1)], min_val=0, max_val=SPARE + NE - 1)
                    e = pe.value_load(spare_list[0:1, bass.ds(j + MORE, 1)], min_val=0, max_val=NE - 1)
                    with pe.If(row > 0):
                        pe.wait_ge(spare_dve(l), j * SPARE_DVE + 2)
                        for k in range(KD):
                            last = gather_mm(k)
                        last.then_inc(spare_pe(l), 1)
                        turn_mm(lambda tc: bass.ds(e * 12 + tc * 3, 3)).then_inc(spare_pe(l), 1)
                        pe.wait_ge(spare_dve(l), j * SPARE_DVE + 5)
                        expert_in(0, 2)
                        expert_in(1, 3).then_inc(spare_pe(l), 1)
                        pe.wait_ge(spare_act(l), j * SPARE_ACT + 4)
                        pe.wait_ge(spare_dve(l), j * SPARE_DVE + 7)
                        pe.wait_ge(spare_down_loaded(l), j * 16 + 16)
                        down_product(0)
                        down_product(1).then_inc(spare_pe(l), 1)
                        pe.wait_ge(spare_dve(l), j * SPARE_DVE + 8)
                        for c in range(KD):
                            last = scatter_mm(c, c)
                        last.then_inc(spare_pe(l), 1)

        @block.scalar
        def _(act):
            def f(o, i, func, **kw):
                return nc.scalar.activation(o, i, func, **kw)

            def split_hi(l, i, su, n_landed, width, slot):
                act.wait_ge(*n_landed)
                if i < 3:
                    act.wait_ge(s_mod, l * NMOD + 4)
                elif i == 4:
                    act.wait_ge(s_mod, (l + 1) * NMOD)
                if su >= RING:
                    act.wait_ge(s_used, su - RING + 1)
                f(whi[:, slot, 0:width], stage[:, where(i) % RING, 0:width], ACT.Copy).then_inc(s_hi, 1)

            def split(l, i):
                if i < NMIX:
                    su, _ = mix_unit(l, i)
                    split_hi(l, i, su, landed(l, where(i)), unit_width(l, MIX_UNITS[i]), i % RING)
                else:
                    su, _ = expert_unit(l, 0, i - NMIX)
                    split_hi(l, i, su, landed(l, NMOD + i), UNIT, i % RING)

            chain = sem_of("scalar_step")
            steps = [0]

            def rsqrt(pairs):
                for o, i, scale, rows, _ in pairs:
                    steps[0] += 1
                    f(o, i, ACT.Ln, bias=small[rows, 60:61], scale=scale).then_inc(chain, 1)
                for q, (o, _, _, _, done) in enumerate(pairs):
                    act.wait_ge(chain, steps[0] - len(pairs) + q + 1)
                    f(o, o, ACT.Exp, scale=-0.5).then_inc(*done)

            def mod_hi(l, g):
                act.wait_ge(*landed(l, SEQ.index(("mod", g))))
                if g == 4:
                    act.wait_ge(s_used, mix_unit(l, 1)[0] + 1)
                elif g > 4 or g == 3:
                    act.wait_ge(s_mod, l * NMOD + (g if g > 4 else 1))
                f(whi[:, mod_slot(g), :], stage[:, SEQ.index(("mod", g)) % RING, :], ACT.Copy).then_inc(s_mod_hi, 1)

            act.wait_ge(*after("small_loaded", 3))
            f(cT[:], cT[:], ACT.Silu).then_inc(*now("silu_c"))
            act.wait_ge(*after("silu_c"))
            f(chl[:, :, 0, :], cT[:], ACT.Copy).then_inc(*now("c_hi"))
            for l in range(DEPTH):
                n = T if l == 0 else LX
                if l > 0:
                    act.wait_ge(*after("moe_added", l - 1))
                for i in range(2):
                    act.wait_ge(*after("filt_arg", l, i))
                    f(fh[0:HID, i, :], fr_[0:HID, :], ACT.Sin).then_inc(*now("filt_sin", l, i))
                    mod_hi(l, i)
                for c in range(2):
                    act.wait_ge(*after("filt_mm", l, 2 + c))
                    f(decay[:, c, :], ps[4 + c][:, :], ACT.Exp).then_inc(*now("filt_decay", l, c))
                for c in range(2):
                    act.wait_ge(*after("filt_k", l, c))
                    f(ksq[:, c, :], kf[:, c, :], ACT.Square).then_inc(*now("filt_sq", l, c))
                mod_hi(l, 2)
                act.wait_ge(*after("filt_ssq", l))
                act.wait_ge(*after("eps_set"))
                rsqrt([(krs[:, :], ps[0][:, 0:256], 1.0, slice(None), now("filt_rsqrt", l))])
                mod_hi(l, 3)

                def squares(which):
                    m = T if which == 0 else n
                    for k in range(KD):
                        if which == 0 and k == 0:
                            if l == 0:
                                act.wait_ge(*after("x_loaded", 1))
                        elif which == 1:
                            act.wait_ge(*after("x_mixed", l, k))
                            if k == 0:
                                act.wait_ge(*after("y_ready", l, 7))
                        if k >= 2:
                            act.wait_ge(*after("x_summed", l, which, k - 2))
                        f(norm_sq[which][:, k % 2, 0:m], xT[:, k, 0:m], ACT.Square).then_inc(*now("x_squared", l, which, k))
                    act.wait_ge(*after("x_summed", l, which, 7))
                    act.wait_ge(*after("eps_set"))
                    rsqrt([(norm_rstd[which][:, 0:m], ps[norm_bank[which]][:, 0:m], 1.0 / D, slice(None), now("x_rsqrt", l, which))])

                def scaled(which):
                    m, hf = T if which == 0 else n, norm_h[which]
                    for k in range(KD):
                        act.wait_ge(*after("x_normed", l, which, k))
                        if k == 0:
                            act.wait_ge(*after("gs_ready", l, which))
                        for st in range(m // 256):
                            c = slice(st * 256, st * 256 + 256)
                            last = f(hf[:, k % 2, c], hf[:, k % 2, c], ACT.Identity, scale=gs[:, which, k, st:st + 1],
                                     bias=modc[:, 24 * which + k, st:st + 1])
                        last.then_inc(*now("hf_ready", l, which, k))
                        act.wait_ge(*after("hf_ready", l, which, k))
                        f(h[:, k, 0, 0:m], hf[:, k % 2, 0:m], ACT.Copy).then_inc(*now("h_hi", l, which, k))

                squares(0)
                split(l, 0)
                split(l, 1)
                scaled(0)
                for m in range(3):
                    act.wait_ge(*after("q_low", l, 2 if m == 2 else m))
                    if m == 0:
                        act.wait_ge(*after("h_ready", l, 0, 7))
                    if m == 2:
                        act.wait_ge(*after("q_low_sum", l, 0))
                    f(pq[:, m, 0:n], ps[2 + m][:, 0:n], ACT.Copy).then_inc(*now("q_low_copied", l, m))
                    act.wait_ge(*after("q_low_copied", l, m))
                    f(tmp[:, m % 2, 0:n], pq[:, m, 0:n], ACT.Square).then_inc(*now("q_low_sq", l, m))
                split(l, 2)
                split(l, 3)
                for m in range(2):
                    act.wait_ge(*after("kv_low", l, m))
                    act.wait_ge(*after("q_low_sum", l, 1 + m))
                    f(pkv[:, m, :], ps[5 + m][:, :], ACT.Copy).then_inc(*now("kv_low_copied", l, m))
                    act.wait_ge(*after("kv_low_copied", l, m))
                    f(tmp[:, (m + 1) % 2, :], pkv[:, m, :], ACT.Square).then_inc(*now("kv_low_sq", l, m))
                act.wait_ge(*after("kv_low", l, 2))
                f(kr[NOPE:QK, :], ps[7][NOPE:QK, :], ACT.Copy).then_inc(*now("kr_copied", l))
                act.wait_ge(*after("q_low_sum", l, 2))
                act.wait_ge(*after("kv_low_sum", l, 1))
                rsqrt([(rq[:, 0, 0:n], ps[0][:, 0:n], 1.0 / QR, slice(None), now("q_low_rsqrt", l)),
                       (rq[:, 1, :], ps[1][:, :], 1.0 / KVR, slice(None), now("kv_low_rsqrt", l))])
                mod_hi(l, 4)
                for tc in range(4):
                    act.wait_ge(*after("v_mm", l, tc))
                    f(V[:, tc, :], ps[2 + tc][:, :], ACT.Copy).then_inc(*now("v_copied", l, tc))

                ntile = 4 if l == 0 else 2

                act.wait_ge(*after("kr_copied", l))
                f(tmp[NOPE:QK, 1, :], kr[NOPE:QK, :], ACT.Square).then_inc(*now("kr_squared", l))

                def head_squares(i):
                    act.wait_ge(*after("q_mm", l, i))
                    f(tmp[0:QK, 0, 0:n], ps[0][0:QK, 0:n], ACT.Square).then_inc(*now("q_squared", l, i))
                    act.wait_ge(*after("k_mm", l, i))
                    f(tmp[0:NOPE, 1, :], ps[1][0:NOPE, :], ACT.Square).then_inc(*now("k_squared", l, i))

                def head_rsqrts(i):
                    if i > 0:
                        act.wait_ge(*after("k_roped", l, i - 1))
                    act.wait_ge(*after("q_sum", l, i))
                    act.wait_ge(*after("k_sum", l, i))
                    rsqrt([(rq[0:QK, 0, 0:n], ps[2][0:QK, 0:n], 1.0 / QK, slice(0, QK), now("q_rsqrt", l, i)),
                           (rq[0:QK, 1, :], ps[3][0:QK, :], 1.0 / QK, slice(0, QK), now("k_rsqrt", l, i))])

                def exps(i, t):
                    seq = i * ntile + t
                    nk = T if t < 2 else LC
                    act.wait_ge(*after("max_ready", l, seq))
                    if seq >= 2:
                        act.wait_ge(*after("prob_turn", l, seq - 2))
                    elif seq == 0:
                        act.wait_ge(*after("kvn_ready", l))
                    s2 = 4 * (seq % 2)
                    f(prob[:, seq % 2, 0:nk], ps[4 + seq % 2][:, 0:nk], ACT.Exp, bias=small[:, s2:s2 + 1],
                      scale=SCALE, accum_out=small[:, s2 + 1:s2 + 2]).then_inc(*now("exp_done", l, seq))

                def turned(i, t):
                    seq = i * ntile + t
                    nk = 4 if t < 2 else 2
                    act.wait_ge(*after("prob_turn", l, seq))
                    if t % 2 == 0:
                        if seq > 0:
                            act.wait_ge(*after("pv", l, seq // 2 - 1))
                    f(pT[:, 0:nk, (t % 2) * P:(t % 2) * P + P],
                      ps[6][:, 0:nk * P].rearrange("p (c q) -> p c q", c=nk), ACT.Copy).then_inc(*now("prob_turned", l, seq))

                for i in range(HEADS + 1):
                    if i < HEADS:
                        head_squares(i)
                    if i > 0:
                        exps(i - 1, 0)
                        exps(i - 1, 1)
                    if i < HEADS:
                        head_rsqrts(i)
                    if i > 0:
                        turned(i - 1, 0)
                        turned(i - 1, 1)
                        if l == 0:
                            exps(i - 1, 2)
                            exps(i - 1, 3)
                    if i < HEADS - 1:
                        mod_hi(l, 5 + i)
                    elif i == HEADS - 1:
                        split(l, 4)
                    if i > 0 and l == 0:
                        turned(i - 1, 2)
                        turned(i - 1, 3)

                split(l, 5)
                split(l, 6)
                for c in range(6):
                    act.wait_ge(*after("hy_mm", l, c))
                    if c >= 2:
                        act.wait_ge(*after("conv_done", l, c - 2))
                    else:
                        act.wait_ge(*after("pads_zero", l))
                    f(pad[:, c % 2, 0:n // 256, 1:257], ps[c % 2][:, 0:n].rearrange("p (s t) -> p s t", t=256),
                      ACT.Copy).then_inc(*now("pad_copied", l, c))
                    if c == 1:
                        split(l, 7)
                    if c == 3:
                        split(l, 8)
                    if c == 5:
                        split(l, 9)

                for st in range(n // 256):
                    act.wait_ge(*after("u_turned", l, st))
                    f(uR, ps[2][:, :].rearrange("p (c t) -> p c t", c=2), ACT.Copy).then_inc(*now("uR_copied", l, st))
                    act.wait_ge(*after("u_spec", l, st))
                    if st > 0:
                        act.wait_ge(*after("Y_ready", l, st - 1))
                    f(U[:, 0], ps[0][:, :].rearrange("p (f c) -> p f c", f=2), ACT.Copy)
                    f(U[:, 1], ps[1][:, :].rearrange("p (f c) -> p f c", f=2), ACT.Copy).then_inc(*now("U_copied", l, st))
                    if st == 0:
                        for c in range(4):
                            act.wait_ge(*after("gm_mm", l, c))
                            f(gl[:, c, 0:n], ps[4 + c][:, 0:n], ACT.Gelu_apprx_tanh).then_inc(*now("gm_gelu", l, c))
                        for c in range(2):
                            act.wait_ge(*after("gm_gelu", l, 2 + c))
                            f(gsq[:, c, 0:n], gl[:, 2 + c, 0:n], ACT.Square).then_inc(*now("gv_sq", l, c))
                act.wait_ge(*after("gv_sum", l, 1))
                rsqrt([(grs[:, 0:n], ps[0][:, 0:n], 1.0 / GM, slice(None), now("gv_rsqrt", l))])
                for tc in range(n // P):
                    act.wait_ge(*after("gv_turned", l, tc))
                    f(vR[:, tc, :], ps[(1, 2)[tc % 2]][:, 0:256], ACT.Copy).then_inc(*now("vR_copied", l, tc))

                chunk = 0
                for half in range(2):
                    for b in range(3):
                        for j in range(4):
                            act.wait_ge(*after("branch_mm", l, half, b, j))
                            if b == 0 and j == 0:
                                act.wait_ge(*(after("m_done", l, 1) if half == 0 else after("y_ready", l, 3)))
                            f(br[:, b, j, 0:n], ps[chunk % 4][:, 0:n], ACT.Copy).then_inc(*now("merge_evac", l, chunk))
                            chunk += 1
                    for b in range(3):
                        split(l, 10 + 4 * half + b)
                        for j in range(4):
                            act.wait_ge(*after("gate_mm", l, half, b, j))
                            g = half * 12 + b * 4 + j
                            if g >= 2:
                                act.wait_ge(*after("gated", l, g - 2))
                            f(sig[:, g % 2, 0:n], ps[chunk % 4][:, 0:n], ACT.Sigmoid).then_inc(*now("merge_evac", l, chunk))
                            chunk += 1
                    split(l, 13 + 4 * half)
                split(l, 18)
                squares(1)
                scaled(1)
                act.wait_ge(*after("logits_turned", l))
                m4 = n // P
                f(rt[:, 0:NE * m4], ps[2][:, 0:NE * m4], ACT.Sigmoid).then_inc(*now("aff", l))
                split(l, 19)
                for q in range(n // P * 4):
                    tc, sd, half = q // 4, q // 2 % 2, q % 2
                    act.wait_ge(*after("tokens_turned", l, q))
                    if q == 0:
                        act.wait_ge(*after("out_mm", l, 7))
                    f(hR[:, tc, sd, 512 * half:512 * half + 512], ps[4 + q % 4][:, :], ACT.Copy).then_inc(*now("tokens_copied", l, q))

                su0, _ = expert_unit(l, 0, 0)
                base = [landed(l, NMOD + NMIX + i)[1] for i in range(2)]

                def split_expert(e, i, off):
                    act.wait_ge(s_stage[i], e * 16 + (base[i] + 16 * off))
                    if isinstance(e, int) and e + off == 0:
                        act.wait_ge(s_used, su0 + i - RING + 1)
                    else:
                        per = (KF, 1)[i]
                        act.wait_ge(X[("gate_mm", "up_mm")[i]], reached(l, e, per, per * off - 1))
                    f(whi[:, i, :], stage[:, i, :], ACT.Copy).then_inc(s_hi, 1)

                def input_hi(half):
                    return f(he[:, 4 * half:4 * half + 4, 0, :], ps[half][:, :].rearrange("p (k t) -> p k t", k=4), ACT.Copy)

                def result_hi(half):
                    return f(yR[:, 0, 512 * half:512 * half + 512], ps[4 + half][:, :], ACT.Identity, scale=csum)

                def gathered(e, off):
                    for half in range(2):
                        act.wait_ge(X["gathered"], reached(l, e, 2, 2 * off + half))
                        input_hi(half).then_inc(X["input_hi"], 1)

                def expert(e, last_one=False):
                    act.wait_ge(X["gate_mm"], reached(l, e, KF, KF - 1))
                    f(sg, ps[2][:, :], ACT.Silu).then_inc(X["gate_silu"], 1)
                    if not last_one:
                        split_expert(e, 0, 1)
                    act.wait_ge(X["choice_turned"], reached(l, e))
                    f(selT[:, 0:n], ps[4][:, 0:n], ACT.Copy).then_inc(X["choice_copied"], 1)
                    if not last_one:
                        split_expert(e, 1, 1)
                        gathered(e, 1)
                    act.wait_ge(X["weight_ready"], reached(l, e))
                    for half in range(2):
                        act.wait_ge(X["down_mm"], reached(l, e, 2, half))
                        result_hi(half).then_inc(X["result_hi"], 1)

                gathered(0, 0)
                expert(0)
                with act.Fori(1, NE - 1) as e:
                    expert(e)
                expert(NE - 1, True)

                act.wait_ge(*after("spare_listed", l))
                with act.Fori(0, spare_blocks(l)) as j:
                    row = act.value_load(spare_list[0:1, bass.ds(j, 1)], min_val=0, max_val=SPARE + NE - 1)
                    with act.If(row > 0):
                        for i in range(2):
                            act.wait_ge(spare_loaded(l), j * 32 + 32)
                            f(whi[:, i, :], stage[:, i, :], ACT.Copy).then_inc(spare_act(l), 1)
                        act.wait_ge(spare_pe(l), j * SPARE_PE + 1)
                        input_hi(0)
                        input_hi(1).then_inc(spare_act(l), 1)
                        act.wait_ge(spare_pe(l), j * SPARE_PE + 2)
                        f(selT[:, 0:n], ps[4][:, 0:n], ACT.Copy).then_inc(spare_act(l), 1)
                        act.wait_ge(spare_pe(l), j * SPARE_PE + 3)
                        f(sg, ps[2][:, :], ACT.Silu).then_inc(spare_act(l), 1)
                        act.wait_ge(spare_pe(l), j * SPARE_PE + 4)
                        result_hi(0)
                        result_hi(1).then_inc(spare_act(l), 1)

        @block.vector
        def _(dve):
            chain = sem_of("vector_step")
            steps = [0]

            def link(ins_):
                steps[0] += 1
                ins_.then_inc(chain, 1)
                dve.wait_ge(chain, steps[0])

            def tt(o, a, b, op):
                return nc.vector.tensor_tensor(o, a, b, op)

            def ts(o, a, s1, s2, op0, op1=None):
                if op1 is None:
                    return nc.vector.tensor_scalar(o, a, s1, None, op0)
                return nc.vector.tensor_scalar(o, a, s1, s2, op0, op1)

            def stt(o, a, s, b, op0, op1):
                return nc.vector.scalar_tensor_tensor(out=o, in0=a, scalar=s, in1=b, op0=op0, op1=op1)

            def split(l, i):
                if i < NMIX:
                    su, _ = mix_unit(l, i)
                    width = unit_width(l, MIX_UNITS[i])
                else:
                    su, _ = expert_unit(l, 0, i - NMIX)
                    width = UNIT
                slot = i % RING
                dve.wait_ge(s_hi, su + 1)
                tt(wlo[:, slot, 0:width], stage[:, where(i) % RING, 0:width], whi[:, slot, 0:width], ALU.subtract).then_inc(s_lo, 1)

            def rsqrt_of(*done):
                dve.wait_ge(*after(*done))

            def mod_lo(l, g):
                dve.wait_ge(s_mod_hi, l * NMOD + g + 1)
                slot = mod_slot(g)
                tt(wlo[:, slot, :], stage[:, SEQ.index(("mod", g)) % RING, :], whi[:, slot, :], ALU.subtract).then_inc(s_mod_lo, 1)

            link(nc.vector.memset(small[:, 60:61], EPS))
            nc.vector.memset(small[:, 61:62], 0.0).then_inc(*now("eps_set"))
            dve.wait_ge(*after("c_hi"))
            tt(chl[:, :, 1, :], cT[:], chl[:, :, 0, :], ALU.subtract).then_inc(*now("c_split"))
            for l in range(DEPTH):
                n = T if l == 0 else LX
                for i in range(2):
                    dve.wait_ge(*after("filt_mm", l, i))
                    if i == 0:
                        dve.wait_ge(*after("filter_loaded", l, 5))
                    else:
                        dve.wait_ge(*after("filt_sin", l, 0))
                    w = slice(0, HID)
                    bcol = col(l, "b1" if i == 0 else "b2")[w]
                    link(ts(fa[w, :], ps[0][w, 256 * i:256 * i + 256], bcol, col(l, "freq")[w], ALU.add, ALU.mult))
                    link(ts(fk[w, :], fa[w, :], float(1 / (2 * np.pi)), ROUND, ALU.mult, ALU.add))
                    link(ts(fk[w, :], fk[w, :], ROUND, None, ALU.subtract))
                    link(stt(fa[w, :], fk[w, :], -TWO_PI_HI, fa[w, :], ALU.mult, ALU.add))
                    link(stt(fa[w, :], fk[w, :], -TWO_PI_LO, fa[w, :], ALU.mult, ALU.add))
                    ts(fr_[w, :], fa[w, :], 3.1415925, -3.1415925, ALU.min, ALU.max).then_inc(*now("filt_arg", l, i))
                    if i == 0:
                        mod_lo(l, 0)
                link(nc.vector.memset(fh[HID:HID + 1, 1, :], 1.0))
                stt(dec[0:1, :], dec[0:1, :], -1.0, dec[0:1, :], ALU.mult, ALU.max).then_inc(*now("decay_abs", l))
                mod_lo(l, 1)
                for c in range(2):
                    dve.wait_ge(*after("filt_decay", l, c))
                    tt(kf[:, c, :], ps[2 + c][:, :], decay[:, c, :], ALU.mult).then_inc(*now("filt_k", l, c))
                mod_lo(l, 2)
                dve.wait_ge(*after("filt_rsqrt", l))
                for c in range(2):
                    for d in range(2):
                        link(stt(kf[:, c, d * HY:d * HY + HY], kf[:, c, d * HY:d * HY + HY], 1.0 / 256, krs[:, :], ALU.mult, ALU.mult))
                link(ts(kf[0:1, 0, HY:2 * HY], kf[0:1, 0, HY:2 * HY], 0.0, None, ALU.mult))
                for c in range(2):
                    link(tt(kab[:, 0, c, :], kf[:, c, 0:HY], kf[:, c, HY:2 * HY], ALU.add))
                    last = tt(kab[:, 1, c, :], kf[:, c, HY:2 * HY], kf[:, c, 0:HY], ALU.subtract)
                    if c == 0:
                        link(last)
                last.then_inc(*now("filt_ab", l))
                mod_lo(l, 3)
                for fch in range(2):
                    dve.wait_ge(*after("filt_spec", l, fch))
                    nc.vector.tensor_copy(kfilt[:, l, :, fch, :], ps[6 + fch][:, :].rearrange("p (r c) -> p r c", r=2)
                                          ).then_inc(*now("filt_copied", l, fch))

                def modulated(part):
                    a, b = (0, 32) if part == 0 else (32, 96)
                    ab = COLS["bmod"][0]
                    dve.wait_ge(s_mod, l * NMOD + (4, NMOD)[part])
                    src = ps[1][:, a:b] if part == 0 else ps[7][:, 256 + a:256 + b]
                    tt(modc[:].rearrange("p a b -> p (a b)")[:, a:b], src, cols[:, l, ab + a:ab + b], ALU.add).then_inc(*now("mod_added", l, part))
                    dve.wait_ge(*after("mod_added", l, part))
                    at = (8, 32)[part]
                    stt(gs[:, part].rearrange("p a b -> p (a b)"), modc[:, at:at + 8, :].rearrange("p a b -> p (a b)"), 1.0,
                        col(l, ("g1", "g2")[part]), ALU.add, ALU.mult).then_inc(*now("gs_ready", l, part))

                modulated(0)

                def normed(which):
                    m, hf, rstd = T if which == 0 else n, norm_h[which], norm_rstd[which]
                    dve.wait_ge(*after("x_rsqrt", l, which))

                    def rest(k):
                        dve.wait_ge(*after("h_hi", l, which, k))
                        tt(h[:, k, 1, 0:m], hf[:, k % 2, 0:m], h[:, k, 0, 0:m], ALU.subtract).then_inc(*now("h_ready", l, which, k))

                    for k in range(KD):
                        if which == 1 and k >= 2:
                            dve.wait_ge(*after("logits", l, k - 2))
                        if k >= 2:
                            dve.wait_ge(*after("h_ready", l, which, k - 2))
                        tt(hf[:, k % 2, 0:m], xT[:, k, 0:m], rstd[:, 0:m], ALU.mult).then_inc(*now("x_normed", l, which, k))
                        if k > 0:
                            rest(k - 1)
                    rest(KD - 1)

                split(l, 0)
                split(l, 1)
                normed(0)
                split(l, 2)
                split(l, 3)

                def low_norm(src, r, gname, dst, nk, m, done):
                    for k in range(nk):
                        link(stt(src[:, k, 0:m], src[:, k, 0:m], col(l, gname)[:, k:k + 1], r, ALU.mult, ALU.mult))
                        link(nc.vector.tensor_copy(dst[:, k, 0, 0:m], src[:, k, 0:m]))
                        last = tt(dst[:, k, 1, 0:m], src[:, k, 0:m], dst[:, k, 0, 0:m], ALU.subtract)
                        if k < nk - 1:
                            link(last)
                    last.then_inc(*now(done, l))
                    dve.wait_ge(*after(done, l))

                dve.wait_ge(*after("kv_low_rsqrt", l))
                low_norm(pkv, rq[:, 1, :], "gkva", kvn, 2, T, "kvn_ready")
                dve.wait_ge(*after("q_low_copied", l, 2))
                low_norm(pq, rq[:, 0, 0:n], "gqa", qn, 3, n, "qn_ready")
                mod_lo(l, 4)

                ntile = 4 if l == 0 else 2

                def head_norms(i):
                    b = i % 2
                    if i >= 2:
                        dve.wait_ge(*after("scores", l, (i - 1) * ntile - 1))
                    rsqrt_of("q_rsqrt", l, i)
                    stt(qh[0:QK, b, 0:n], ps[0][0:QK, 0:n], col(l, "gqn")[0:QK], rq[0:QK, 0, 0:n],
                        ALU.mult, ALU.mult).then_inc(*now("q_normed", l, i))
                    rsqrt_of("k_rsqrt", l, i)
                    stt(kh[0:NOPE, b, :], ps[1][0:NOPE, :], col(l, "gkn")[0:NOPE], rq[0:NOPE, 1, :], ALU.mult, ALU.mult)
                    stt(kh[NOPE:QK, b, :], kr[NOPE:QK, :], col(l, "gkn")[NOPE:QK], rq[NOPE:QK, 1, :],
                        ALU.mult, ALU.mult).then_inc(*now("k_normed", l, i))

                def head_ropes(i):
                    b = i % 2
                    for which, (x, name) in enumerate(((qh, "q"), (kh, "k"))):
                        dve.wait_ge(*after(name + "_rot", l, i))
                        turn = rq[0:QK, which, 0:LX]
                        link(tt(x[0:QK, b, 0:LX], x[0:QK, b, 0:LX], rope[:, 0, :], ALU.mult))
                        link(tt(turn, ps[2 + which][0:QK, 0:LX], rope[:, 1, :], ALU.mult))
                        tt(x[0:QK, b, 0:LX], x[0:QK, b, 0:LX], turn, ALU.add).then_inc(*now(name + "_roped", l, i))

                def maxes(i, t):
                    seq = i * ntile + t
                    nk = T if t < 2 else LC
                    s2 = 4 * (seq % 2)
                    dve.wait_ge(*after("scores", l, seq))
                    if seq >= 2:
                        dve.wait_ge(*after("prob_ready", l, seq - 2))
                    nc.vector.tensor_reduce(small[:, s2 + 2:s2 + 3], ps[4 + seq % 2][:, 0:nk], AX.X, ALU.max).then_inc(*now("max_raw", l, seq))
                    dve.wait_ge(*after("max_raw", l, seq))
                    ts(small[:, s2:s2 + 1], small[:, s2 + 2:s2 + 3], -SCALE, None, ALU.mult).then_inc(*now("max_ready", l, seq))

                def normalised(i, t):
                    seq = i * ntile + t
                    nk = T if t < 2 else LC
                    s2 = 4 * (seq % 2)
                    dve.wait_ge(*after("exp_done", l, seq))
                    link(nc.vector.reciprocal(small[:, s2 + 3:s2 + 4], small[:, s2 + 1:s2 + 2]))
                    ts(prob[:, seq % 2, 0:nk], prob[:, seq % 2, 0:nk], small[:, s2 + 3:s2 + 4], None,
                       ALU.mult).then_inc(*now("prob_ready", l, seq))

                def head_out(i, g):
                    r = slice((i % 2) * VD, (i % 2) * VD + VD)
                    seq = i * (ntile // 2) + g
                    c = slice(g * 256, g * 256 + 256)
                    dve.wait_ge(*after("pv", l, seq))
                    link(nc.vector.tensor_copy(aT[r, i // 2, 0, c], ps[7][r, 0:256]))
                    tt(aT[r, i // 2, 1, c], ps[7][r, 0:256], aT[r, i // 2, 0, c], ALU.subtract).then_inc(*now("a_done", l, seq))

                dve.wait_ge(*after("const_loaded", 9))
                for i in range(HEADS + 1):
                    if i > 0:
                        maxes(i - 1, 0)
                        maxes(i - 1, 1)
                        normalised(i - 1, 0)
                        normalised(i - 1, 1)
                    if i < HEADS:
                        head_norms(i)
                    if i > 0 and l == 0:
                        maxes(i - 1, 2)
                        maxes(i - 1, 3)
                    if i > 0:
                        head_out(i - 1, 0)
                    if i < HEADS:
                        head_ropes(i)
                    if i > 0 and l == 0:
                        normalised(i - 1, 2)
                        normalised(i - 1, 3)
                        head_out(i - 1, 1)
                    if i < HEADS - 1:
                        mod_lo(l, 5 + i)
                    elif i == HEADS - 1:
                        split(l, 4)

                modulated(1)

                split(l, 5)
                split(l, 6)
                ns = n // 256
                dve.wait_ge(*after("v_copied", l, 3))
                dve.wait_ge(*after("pv", l, HEADS * (ntile // 2) - 1))
                for b in range(2):
                    for e in (0, 257):
                        last = nc.vector.memset(pad[:, b, :, e:e + 1], 0.0)
                        if (b, e) != (1, 257):
                            link(last)
                last.then_inc(*now("pads_zero", l))
                cw, cbias = col(l, "convw"), col(l, "convb")
                for c in range(6):
                    dve.wait_ge(*after("pad_copied", l, c))
                    zz = z[:, c, 0:n].rearrange("p (s t) -> p s t", t=256)
                    p = pad[:, c % 2, 0:ns]
                    link(ts(zz, p[:, :, 0:256], cw[:, c:c + 1], cbias[:, c:c + 1], ALU.mult, ALU.add))
                    link(stt(zz, p[:, :, 1:257], cw[:, 6 + c:7 + c], zz, ALU.mult, ALU.add))
                    stt(zz, p[:, :, 2:258], cw[:, 12 + c:13 + c], zz, ALU.mult, ALU.add).then_inc(*now("conv_done", l, c))
                    dve.wait_ge(*after("conv_done", l, c))
                    if c == 1:
                        split(l, 7)
                    if c == 3:
                        split(l, 8)
                    if c == 5:
                        split(l, 9)
                tt(z[:, 2:4, 0:n], z[:, 2:4, 0:n], z[:, 4:6, 0:n], ALU.mult).then_inc(*now("u_ready", l))
                def spectrum_product(st):
                    dve.wait_ge(*after("U_copied", l, st))
                    if st > 0:
                        dve.wait_ge(*after("y_back", l, st - 1))
                    K = kfilt[:, l]
                    link(tt(Y[:, 0], U[:, 0], K[:, 0], ALU.mult))
                    link(tt(hyt[:, 0], U[:, 1], K[:, 1], ALU.mult))
                    link(tt(Y[:, 0], Y[:, 0], hyt[:, 0], ALU.add))
                    link(tt(Y[:, 1], U[:, 1], K[:, 0], ALU.mult))
                    link(tt(hyt[:, 1], U[:, 0], K[:, 1], ALU.mult))
                    tt(Y[:, 1], Y[:, 1], hyt[:, 1], ALU.subtract).then_inc(*now("Y_ready", l, st))

                def hyena_out(st):
                    cs = slice(st * 256, st * 256 + 256)
                    dve.wait_ge(*after("y_back", l, st))
                    dve.wait_ge(*after("u_ready", l))
                    for c in range(2):
                        link(stt(hyb[:, c, :], z[:, 2 + c, cs], col(l, "hybias")[:, c:c + 1], ps[3][:, c * 256:c * 256 + 256],
                                 ALU.mult, ALU.add))
                        link(tt(hyb[:, c, :], hyb[:, c, :], z[:, c, cs], ALU.mult))
                        link(nc.vector.tensor_copy(bT[:, c, 0, cs], hyb[:, c, :]))
                        last = tt(bT[:, c, 1, cs], hyb[:, c, :], bT[:, c, 0, cs], ALU.subtract)
                        if c == 0:
                            link(last)
                    last.then_inc(*now("b_done", l, st))
                    dve.wait_ge(*after("b_done", l, st))

                for st in range(ns):
                    spectrum_product(st)
                    if st < ns - 1:
                        hyena_out(st)

                dve.wait_ge(*after("gv_rsqrt", l))
                for c in range(2):
                    last = stt(vn[:, c, 0:n], gl[:, 2 + c, 0:n], col(l, "gmg")[:, c:c + 1], grs[:, 0:n], ALU.mult, ALU.mult)
                    if c == 0:
                        link(last)
                last.then_inc(*now("gv_normed", l))
                hyena_out(ns - 1)
                for c in range(2):
                    dve.wait_ge(*after("gm_spatial", l, 2 * c + 1))
                    link(tt(gmt[:, c, 0:n], gl[:, c, 0:n], ps[4 + c][:, 0:n], ALU.mult))
                for c in range(2):
                    dve.wait_ge(*after("gm_spatial", l, 3))
                    link(nc.vector.tensor_copy(mT[:, c, 0, 0:n], gmt[:, c, 0:n]))
                    tt(mT[:, c, 1, 0:n], gmt[:, c, 0:n], mT[:, c, 0, 0:n], ALU.subtract).then_inc(*now("m_done", l, c))

                chunk = 0
                for half in range(2):
                    y = ylo4 if half == 0 else yhi4
                    chunk += 12
                    for b in range(3):
                        split(l, 10 + 4 * half + b)
                        for j in range(4):
                            dve.wait_ge(*after("merge_evac", l, chunk))
                            chunk += 1
                            g = half * 12 + b * 4 + j
                            tt(br[:, b, j, 0:n], br[:, b, j, 0:n], sig[:, g % 2, 0:n], ALU.mult).then_inc(*now("gated", l, g))
                            if b == 2:
                                dve.wait_ge(*after("gated", l, g))
                                link(tt(br[:, 0, j, 0:n], br[:, 0, j, 0:n], br[:, 1, j, 0:n], ALU.add))
                                link(tt(br[:, 0, j, 0:n], br[:, 0, j, 0:n], br[:, 2, j, 0:n], ALU.add))
                                link(nc.vector.tensor_copy(y[:, j, 0, 0:n], br[:, 0, j, 0:n]))
                                tt(y[:, j, 1, 0:n], br[:, 0, j, 0:n], y[:, j, 0, 0:n], ALU.subtract).then_inc(*now("y_ready", l, 4 * half + j))
                    split(l, 13 + 4 * half)
                split(l, 18)
                for c in range(8):
                    dve.wait_ge(*after("out_mm", l, c))
                    for st in range(ns):
                        cs = slice(st * 256, st * 256 + 256)
                        last = stt(xT[:, c, cs], ps[(48 + c) % 4][:, cs], modc[:, 16 + c, st:st + 1], xT[:, c, cs], ALU.mult, ALU.add)
                        if st < ns - 1:
                            link(last)
                    last.then_inc(*now("x_mixed", l, c))

                dve.wait_ge(*after("x_mixed", l, 7))
                normed(1)
                dve.wait_ge(*after("logits", l, 7))
                dve.wait_ge(*after("y_ready", l, 7))
                nc.vector.tensor_copy(lgT[0:NE, 0:n], ps[0][0:NE, 0:n]).then_inc(*now("logits_copied", l))
                m4 = n // P
                W = NE * m4

                def rv(a, w=16):
                    return rt[:, a:a + w * m4].rearrange("p (t e) -> p t e", t=m4)

                aff, score = rv(0), rv(64)
                hi1, lo1, hi2, lo2, gsc = rv(128, 4), rv(144, 4), rv(160, 4), rv(176, 4), rv(192, 4)
                gmax, comb = rv(208, 1), rv(256)
                msk, pick = rv(320), rv(384)
                pick2 = rv(448)
                dve.wait_ge(*after("aff", l))
                rbb = rb[:].unsqueeze(1).to_broadcast([P, m4, NE])
                link(tt(score, aff, rbb, ALU.add))
                s4 = score.rearrange("p t (g j) -> p t g j", g=4)
                link(tt(hi1, s4[:, :, :, 0], s4[:, :, :, 1], ALU.max))
                link(tt(lo1, s4[:, :, :, 0], s4[:, :, :, 1], ALU.min))
                link(tt(hi2, s4[:, :, :, 2], s4[:, :, :, 3], ALU.max))
                link(tt(lo2, s4[:, :, :, 2], s4[:, :, :, 3], ALU.min))
                link(tt(gsc, hi1, hi2, ALU.max))
                link(tt(hi1, hi1, hi2, ALU.min))
                link(tt(lo1, lo1, lo2, ALU.max))
                link(tt(hi1, hi1, lo1, ALU.max))
                link(tt(gsc, gsc, hi1, ALU.add))

                def first_max(dst, src, w, orders):
                    link(nc.vector.tensor_reduce(gmax, src, AX.X, ALU.max))
                    link(tt(dst, src, gmax.to_broadcast([P, m4, w]), ALU.is_equal))
                    link(tt(dst, dst, orders.unsqueeze(1).to_broadcast([P, m4, w]), ALU.mult))
                    link(nc.vector.tensor_reduce(gmax, dst, AX.X, ALU.max))
                    link(tt(dst, dst, gmax.to_broadcast([P, m4, w]), ALU.is_equal))

                first_max(hi2, gsc, 4, table("groups"))
                m4v = msk.rearrange("p t (g j) -> p t g j", g=4)
                g4 = hi2.unsqueeze(3).to_broadcast([P, m4, 4, 4])
                link(tt(m4v, s4, g4, ALU.mult))
                link(ts(hi2, hi2, BIG, -BIG, ALU.mult, ALU.add))
                link(tt(m4v, m4v, g4, ALU.add))
                first_max(pick, msk, NE, table("experts"))
                link(stt(msk, pick, -2 * BIG, msk, ALU.mult, ALU.add))
                first_max(pick2, msk, NE, table("experts"))
                link(tt(pick, pick, pick2, ALU.add))
                nt = n // P
                nc.vector.tensor_copy(pickh[:, 0:W].rearrange("p (t e) -> p t e", t=nt), pick).then_inc(*now("picked", l))
                link(tt(comb, pick, aff, ALU.mult))
                link(nc.vector.tensor_reduce(gmax, comb, AX.X, ALU.add))
                link(nc.vector.reciprocal(gmax, gmax))
                link(tt(comb, comb, gmax.to_broadcast([P, m4, NE]), ALU.mult))
                c3 = comb3.rearrange("p (e t q) -> p e t q", e=NE, t=4)[:, :, 0:nt, :]
                byexp, rest = comb.rearrange("p t e -> p e t"), msk.rearrange("p t e -> p (t e)").rearrange("p (e t) -> p e t", e=NE)
                link(nc.vector.tensor_copy(c3[:, :, :, 0], byexp))
                link(tt(rest, byexp, c3[:, :, :, 0], ALU.subtract))
                link(nc.vector.tensor_copy(c3[:, :, :, 1], rest))
                link(tt(rest, rest, c3[:, :, :, 1], ALU.subtract))
                link(nc.vector.tensor_copy(c3[:, :, :, 2], rest))
                dve.wait_ge(*after("ranked", l))
                rk = rank.rearrange("p (r e t) -> p r e t", r=4, e=NE)
                base_rank = rk[:, 0, :, 0:nt]
                link(stt(base_rank, ps[3][:, 0:W].rearrange("p (t e) -> p e t", t=nt), 1.0, pick.rearrange("p t e -> p e t"),
                         ALU.add, ALU.mult))
                link(ts(base_rank, base_rank, -1.0, None, ALU.add))
                for r in range(1, 4):
                    link(ts(rk[:, r, :, 0:nt], base_rank, -float(SLOTS * r), None, ALU.add))
                for w in (flagA, flagB):
                    link(nc.vector.memset(w, 0.0))
                cur, other = flagA, flagB
                link(tt(cur[:, 32:].rearrange("p (r e) -> p r e", r=3),
                        ps[3][:, 4 * NE:5 * NE].unsqueeze(1).to_broadcast([P, 3, NE]),
                        table("limit").rearrange("p (r e) -> p r e", r=3), ALU.is_gt))
                su0, _ = expert_unit(l, 0, 0)

                def split_expert(e, i, off):
                    dve.wait_ge(s_hi, e * 2 + (su0 + i + 2 * off + 1))
                    tt(wlo[:, i, :], stage[:, i, :], whi[:, i, :], ALU.subtract).then_inc(s_lo, 1)

                def choose(places):
                    return tt(sel[:, 0:nt, :], table("iota").unsqueeze(1).to_broadcast([P, nt, SLOTS]),
                              rank[:, places].unsqueeze(2).to_broadcast([P, nt, SLOTS]), ALU.is_equal)

                def input_lo(half):
                    c = slice(4 * half, 4 * half + 4)
                    return tt(he[:, c, 1, :], ps[half][:, :].rearrange("p (k t) -> p k t", k=4), he[:, c, 0, :], ALU.subtract)

                def result_lo(half):
                    c = slice(512 * half, 512 * half + 512)
                    return stt(yR[:, 1, c], ps[4 + half][:, :], csum, yR[:, 0, c], ALU.mult, ALU.subtract)

                def add(bank, c):
                    for st in range(ns):
                        cs = slice(st * 256, st * 256 + 256)
                        q = stt(xT[:, c, cs], ps[bank][:, cs], modc[:, 40 + c, st:st + 1], xT[:, c, cs], ALU.mult, ALU.add)
                    return q

                def chosen(e, off):
                    e4 = bass.ds(e * 4 + 4 * off, nt) if not isinstance(e, int) else slice(4 * (e + off), 4 * (e + off) + nt)
                    choose(e4).then_inc(X["tokens_chosen"], 1)

                def gathered(e, off):
                    for half in range(2):
                        dve.wait_ge(X["input_hi"], reached(l, e, 2, 2 * off + half))
                        input_lo(half).then_inc(X["input_lo"], 1)

                def adds(e, off):
                    for c in range(KD):
                        dve.wait_ge(X["scattered"], reached(l, e, 8, 8 * off + c))
                        if not (isinstance(e, int) and e + off == 0):
                            dve.wait_ge(X["added"], reached(l, e, 8, 8 * off - 8 + c))
                        add(6 + c % 2, c).then_inc(X["added"], 1)

                def expert(e, first=False, last_one=False):
                    if not first:
                        adds(e, -1)
                    dve.wait_ge(X["choice_turned"], reached(l, e))
                    nc.vector.tensor_reduce(csum, ps[5][:, 0:3], AX.X, ALU.add).then_inc(X["weight_ready"], 1)
                    if not last_one:
                        chosen(e, 1)
                        split_expert(e, 0, 1)
                    dve.wait_ge(X["gate_silu"], reached(l, e))
                    dve.wait_ge(X["up_mm"], reached(l, e))
                    tt(hid, sg, ps[3][:, :], ALU.mult).then_inc(X["hidden"], 1)
                    if not last_one:
                        split_expert(e, 1, 1)
                        gathered(e, 1)
                    dve.wait_ge(X["weight_ready"], reached(l, e))
                    for half in range(2):
                        dve.wait_ge(X["result_hi"], reached(l, e, 2, half))
                        result_lo(half).then_inc(X["result_lo"], 1)

                chosen(0, 0)
                split(l, 19)
                gathered(0, 0)
                flag = hits[:, 0:SPARE]
                link(nc.vector.tensor_copy(flag, cur[:, 32:]))
                for step in (1, 2, 4, 8, 16, 32):
                    link(tt(other[:, 32:], cur[:, 32:], cur[:, 32 - step:32 + SPARE - step], ALU.add))
                    cur, other = other, cur
                link(tt(cur[:, 32:], cur[:, 32:], flag, ALU.mult))
                hv = hits.rearrange("p (j i) -> p j i", j=MORE)
                places = cur[:, 32:].unsqueeze(1).to_broadcast([P, MORE, SPARE])
                js = table("count").unsqueeze(2).to_broadcast([P, MORE, SPARE])
                listed = other[:, 0:2 * MORE]
                for q, name in enumerate(("row", "expert_of")):
                    link(tt(hv, places, js, ALU.is_equal))
                    link(tt(hv, hv, table(name).unsqueeze(1).to_broadcast([P, MORE, SPARE]), ALU.mult))
                    link(nc.vector.tensor_reduce(listed[:, q * MORE:q * MORE + MORE], hv, AX.X, ALU.add))
                nc.vector.tensor_copy(spare_list[:, 0:2 * MORE], listed).then_inc(*now("spare_listed", l))

                expert(0, True)
                expert(1)
                with dve.Fori(2, NE - 1) as e:
                    expert(e)
                nc.vector.memset(small[:, 63:64], 0.0).then_inc(spare_dve(l), 1)
                expert(NE - 1, False, True)
                adds(NE - 1, 0)

                dve.wait_ge(*after("spare_listed", l))
                dve.wait_ge(X["added"], reached(l, NE - 1, 8, 7))
                with dve.Fori(0, spare_blocks(l)) as j:
                    row = dve.value_load(spare_list[0:1, bass.ds(j, 1)], min_val=0, max_val=SPARE + NE - 1)
                    with dve.If(row > 0):
                        choose(bass.ds(row * 4, nt)).then_inc(spare_dve(l), 1)
                        for i in range(2):
                            dve.wait_ge(spare_act(l), j * SPARE_ACT + (1 + i))
                            tt(wlo[:, i, :], stage[:, i, :], whi[:, i, :], ALU.subtract).then_inc(spare_dve(l), 1)
                        dve.wait_ge(spare_act(l), j * SPARE_ACT + 3)
                        input_lo(0)
                        input_lo(1).then_inc(spare_dve(l), 1)
                        dve.wait_ge(spare_pe(l), j * SPARE_PE + 2)
                        nc.vector.tensor_reduce(csum, ps[5][:, 0:3], AX.X, ALU.add).then_inc(spare_dve(l), 1)
                        dve.wait_ge(spare_act(l), j * SPARE_ACT + 5)
                        tt(hid, sg, ps[3][:, :], ALU.mult).then_inc(spare_dve(l), 1)
                        dve.wait_ge(spare_dve(l), j * SPARE_DVE + 7)
                        dve.wait_ge(spare_act(l), j * SPARE_ACT + 6)
                        result_lo(0)
                        result_lo(1).then_inc(spare_dve(l), 1)
                        dve.wait_ge(spare_pe(l), j * SPARE_PE + 5)
                        for c in range(KD):
                            last = add(c, c)
                        last.then_inc(spare_dve(l), 1)
                        dve.wait_ge(spare_dve(l), j * SPARE_DVE + (SPARE_DVE + 1))
                        nc.vector.memset(small[:, 63:64], 0.0)
                nc.vector.memset(small[:, 62:63], 0.0).then_inc(*now("moe_added", l))

    return found


def host_tables():
    f = np.float32
    t = np.arange(LX, dtype=np.float64)
    fr = np.arange(256, dtype=np.float64)
    k_ang = 2 * np.pi * np.outer(t, fr + 0.5) / 512
    s_ang = 2 * np.pi * np.outer(t + 0.5, fr + 0.5) / 512

    def two(a):
        return np.ascontiguousarray(a.astype(f).reshape(2, P, 256).transpose(1, 0, 2))

    rows = LX // GRID_W
    row = np.repeat(np.arange(rows, dtype=f), GRID_W)
    col = np.tile(np.arange(GRID_W, dtype=f), rows)
    nf = ROPE // 4
    inv = (f(10000.0) ** (-np.arange(nf, dtype=f) / f(nf))).astype(f)
    ang = np.concatenate([row[:, None] * inv, col[:, None] * inv], axis=-1)
    rope = np.zeros((QK, 2, LX), f)
    rope[:NOPE, 0] = 1
    rope[NOPE:, 0] = np.repeat(np.cos(ang).astype(f), 2, axis=1).T
    rope[NOPE:, 1] = np.repeat(np.sin(ang).astype(f), 2, axis=1).T
    rot = np.zeros((QK, QK), f)
    for j in range(NOPE, QK, 2):
        rot[j + 1, j] = -1
        rot[j, j + 1] = 1
    tu = (np.arange(LX, dtype=f) / f(LX - 1)).astype(f)
    bands = np.linspace(1e-4, BANDS - 1, BANDS, dtype=f)
    a = (f(2 * np.pi / LX) * np.arange(LX, dtype=f))[:, None] * bands[None]
    zt = np.concatenate([tu[:, None], np.cos(a), -np.sin(a)], axis=-1).astype(f).T
    r, e = np.divmod(np.arange(SPARE), NE)
    tables = np.tile(np.concatenate([np.arange(4, 0, -1), np.arange(NE, 0, -1), np.arange(SLOTS), SLOTS * (r + 1),
                                     NE * (r + 1) + e, e, np.arange(1, MORE + 1)]).astype(f), (P, 1))
    eye = np.eye(P, dtype=f)
    halves = np.stack([eye, np.triu(np.ones((P, P), f), 1), np.ones((P, P), f)], axis=1)
    return {"cosk": two(np.cos(k_ang)), "sink": two(np.sin(k_ang)), "cos_s": two(np.cos(s_ang)), "sin_s": two(np.sin(s_ang)),
            "rope": rope, "rot": rot, "zT": np.ascontiguousarray(zt), "tneg": -tu[None], "halves": halves,
            "tables": tables, "ident": np.eye(P, dtype=f), "ones": np.ones((P, P), f)}


def host_layout(a):
    f = np.float32

    def chunks(v):
        v = np.asarray(v)
        return np.moveaxis(v.reshape(*v.shape[:-1], -1, P), -1, 0)

    def short(v):
        o = np.zeros((P, 1), f)
        o[:v.shape[0], 0] = v
        return o

    cols = np.zeros((P, DEPTH, NCOLS), f)
    for l in range(DEPTH):
        def put(name, v):
            s, e = COLS[name]
            cols[:, l, s:e] = v.reshape(P, e - s)

        put("g1", np.repeat(chunks(a["norm1_g"][l]), 2, axis=1))
        put("g2", np.repeat(chunks(a["norm2_g"][l]), 2, axis=1))
        put("bmod", np.repeat(chunks(a["b_mod"][l]), 2, axis=1))
        put("gqa", chunks(a["g_qa"][l]))
        put("gkva", chunks(a["g_kva"][l]))
        put("gqn", short(a["g_qn"][l]))
        put("gkn", short(a["g_kn"][l]))
        put("convw", chunks(a["hy_conv_w"][l]))
        put("convb", chunks(a["hy_conv_b"][l]))
        put("hybias", chunks(a["hy_bias"][l]))
        put("gmg", chunks(a["gm_norm_g"][l]))
        put("b1", short(a["hy_b1"][l]))
        put("b2", short(a["hy_b2"][l]))
        put("freq", short(a["hy_freq"][l]))
    fw = np.zeros((DEPTH, P, FW), f)
    fw[:, :EMB, 0:HID] = a["hy_w1"]
    fw[:, :HID, HID:2 * HID] = a["hy_w2"]
    fw[:, :HID, 2 * HID:] = a["hy_w3"]
    fw[:, HID, 2 * HID:] = a["hy_b3"]
    c = np.ascontiguousarray
    return {
        "cT": c(np.stack([chunks(a["c"][0]), chunks(a["c_ctx"])], axis=-1)),
        "cols": cols, "fw": fw, "decay": c(a["hy_decay"].reshape(DEPTH, 2 * HY)),
        "xT": c(a["x"][0].T.reshape(KD, P, LX).transpose(1, 0, 2)),
        "ctxT": c(a["ctx"][0].T.reshape(KD, P, LC).transpose(1, 0, 2)),
        "rw": c(a["router_w"].reshape(KD, P, NE).transpose(1, 0, 2)),
        "rb": c(np.broadcast_to(a["router_b"], (P, NE))),
        "ws": c(a["gm_ws"].transpose(0, 3, 1, 2)), "bs": c(a["gm_bs"].reshape(DEPTH, GROUPS * P)),
        **{k: a[k] for k in ("w_mod", "w_in", "w_uq", "w_ukv", "w_pa", "w_pb", "w_pc", "w_out",
                             "moe_w_gate", "moe_w_up", "moe_w_down")},
    }


def kernel(**inputs):
    import concourse.bacc as bacc
    from concourse.bass_utils import run_bass_kernel_spmd

    a = {k: np.asarray(v) for k, v in inputs.items()}
    arrays = host_layout(a)
    arrays.update(host_tables())
    arrays["halves"] = arrays["halves"].astype(mybir.dt.np(BF16))

    def program(known):
        nc = bacc.Bacc("TRN2", target_bir_lowering=False, num_devices=1)
        ins = {k: nc.dram_tensor(f"in_{k}", v.shape, mybir.dt.from_np(v.dtype), kind="ExternalInput").ap()
               for k, v in arrays.items()}
        out = nc.dram_tensor("out_xT", (P, KD, LX), F32, kind="ExternalOutput").ap()
        return nc, build(nc, ins, out, known)

    _, known = program(None)
    nc, _ = program(known)
    r = run_bass_kernel_spmd(nc, [{f"in_{k}": v for k, v in arrays.items()}], core_ids=[0])
    o = r.results[0]["out_xT"]
    return np.ascontiguousarray(o.transpose(2, 1, 0).reshape(1, LX, D))
```
